# Optimizing a Trainium2 kernel written in Bass

```python
import math
import jax, jax.numpy as jnp
from jax import lax
import numpy as np

D_MODEL = 1024
BATCH = 1
SEQ = 256
DEPTH = 1

RET_HEADS = 4
RET_QK_DIM = 128
RET_V_DIM = 256
RET_CHUNK = 128
RET_QK_W = RET_HEADS * RET_QK_DIM
RET_V_W = RET_HEADS * RET_V_DIM
NA_HEADS = 8
NA_HEAD_DIM = 64
NA_W = NA_HEADS * NA_HEAD_DIM
GRID_W = 64
NA_WIN_ROWS = 8
NA_WIN_COLS = 16
NA_Q_BLOCK_COLS = 16
NA_K_BLOCK_COLS = 32
NA_REL_ROWS = 2 * NA_WIN_ROWS - 1
NA_REL_COLS = 2 * NA_WIN_COLS - 1
D_FF = 2816
RMS_EPS = 1e-6
ROPE_BASE = 10000.0
NEG_INF = -1e30
MIX_SPLITS = (RET_QK_W, RET_QK_W, RET_V_W, RET_V_W, NA_W, NA_W, NA_W, D_MODEL, D_MODEL)
MIX_IN_W = sum(MIX_SPLITS)


def _rms_norm(x, gain):
    xf = x.astype(jnp.float32)
    y = xf * lax.rsqrt(jnp.mean(xf * xf, axis=-1, keepdims=True) + RMS_EPS)
    return (y * gain.astype(jnp.float32)).astype(x.dtype)

def _swiglu(x, w_in, w_out):
    g, u = jnp.split(x @ w_in, 2, axis=-1)
    return (jax.nn.silu(g) * u) @ w_out

def _rotary(x, pos):
    half = x.shape[-1] // 2
    inv = 1.0 / (ROPE_BASE ** jnp.linspace(0.0, 1.0, half, dtype=jnp.float32))
    ang = pos[:, None] * inv[None, :]
    cos, sin = jnp.cos(ang), jnp.sin(ang)
    x1, x2 = x[..., :half], x[..., half:]
    return jnp.concatenate([x1 * cos - x2 * sin, x1 * sin + x2 * cos], axis=-1)

def _retention_one_dir(q, k, v, log_gamma, strict):
    B, H, S, DK = q.shape
    DV = v.shape[-1]
    C = RET_CHUNK
    N = S // C
    qc = q.reshape(B, H, N, C, DK)
    kc = k.reshape(B, H, N, C, DK)
    vc = v.reshape(B, H, N, C, DV)
    idx = jnp.arange(C, dtype=jnp.float32)
    diff = idx[:, None] - idx[None, :]
    lower = (diff > 0) if strict else (diff >= 0)
    intra = jnp.where(lower[None], jnp.exp(log_gamma[:, None, None] * jnp.where(lower, diff, 0.0)[None]), 0.0)
    scores = jnp.einsum('bhnqd,bhnkd->bhnqk', qc, kc) * intra[None, :, None]
    inner = jnp.einsum('bhnqk,bhnkv->bhnqv', scores, vc)
    k_dec = jnp.exp(log_gamma[:, None] * (C - 1 - idx)[None, :])
    upd = jnp.einsum('bhnkd,bhnkv->nbhdv', kc * k_dec[None, :, None, :, None], vc)
    chunk_dec = jnp.exp(log_gamma * C)[None, :, None, None]

    def step(state, u):
        return chunk_dec * state + u, state

    _, prev = lax.scan(step, jnp.zeros((B, H, DK, DV), jnp.float32), upd)
    q_dec = jnp.exp(log_gamma[:, None] * (idx + 1.0)[None, :])
    cross = jnp.einsum('bhnqd,nbhdv->bhnqv', qc * q_dec[None, :, None, :, None], prev)
    return (inner + cross).reshape(B, H, S, DV)

def _bidirectional_retention(q, k, v, decay_fwd_logit, decay_bwd_logit):
    lg_f = jax.nn.log_sigmoid(decay_fwd_logit.astype(jnp.float32))
    lg_b = jax.nn.log_sigmoid(decay_bwd_logit.astype(jnp.float32))
    y_f = _retention_one_dir(q, k, v, lg_f, strict=False)
    flip = lambda a: jnp.flip(a, axis=2)
    y_b = flip(_retention_one_dir(flip(q), flip(k), flip(v), lg_b, strict=True))
    return y_f + y_b

def _neighborhood_attention(q, k, v, rel_bias):
    B, S, NH, DH = q.shape
    rows = S // GRID_W
    kr = min(NA_WIN_ROWS, rows)
    ncb = GRID_W // NA_Q_BLOCK_COLS
    qg = (q * (DH ** -0.5)).reshape(B, rows, GRID_W, NH, DH)
    kg = k.reshape(B, rows, GRID_W, NH, DH)
    vg = v.reshape(B, rows, GRID_W, NH, DH)
    c0 = jnp.arange(ncb, dtype=jnp.int32) * NA_Q_BLOCK_COLS
    q_cols = c0[:, None] + jnp.arange(NA_Q_BLOCK_COLS, dtype=jnp.int32)[None, :]
    key_cols = (jnp.clip(c0 - NA_WIN_COLS // 2, 0, GRID_W - NA_K_BLOCK_COLS)[:, None]
                + jnp.arange(NA_K_BLOCK_COLS, dtype=jnp.int32)[None, :])
    win_start = jnp.clip(q_cols - NA_WIN_COLS // 2, 0, GRID_W - NA_WIN_COLS)
    kcb = key_cols[:, None, :]
    col_mask = (kcb >= win_start[:, :, None]) & (kcb < win_start[:, :, None] + NA_WIN_COLS)
    col_idx = jnp.clip(kcb - q_cols[:, :, None] + NA_WIN_COLS - 1, 0, NA_REL_COLS - 1)

    def row_block(r):
        rs = jnp.clip(r - kr // 2, 0, rows - kr)
        q_r = lax.dynamic_index_in_dim(qg, r, axis=1, keepdims=False).reshape(B, ncb, NA_Q_BLOCK_COLS, NH, DH)
        k_blk = lax.dynamic_slice_in_dim(kg, rs, kr, axis=1)[:, :, key_cols]
        v_blk = lax.dynamic_slice_in_dim(vg, rs, kr, axis=1)[:, :, key_cols]
        s = jnp.einsum('bnqhd,brnkhd->bhnqrk', q_r, k_blk).astype(jnp.float32)
        row_idx = rs + jnp.arange(kr, dtype=jnp.int32) - r + NA_WIN_ROWS - 1
        bias = rel_bias[:, row_idx[None, None, :, None], col_idx[:, :, None, :]].astype(jnp.float32)
        s = jnp.where(col_mask[:, :, None, :], s + bias, NEG_INF)
        p = jax.nn.softmax(s.reshape(B, NH, ncb, NA_Q_BLOCK_COLS, kr * NA_K_BLOCK_COLS), axis=-1)
        p = p.reshape(s.shape).astype(v.dtype)
        o = jnp.einsum('bhnqrk,brnkhd->bnqhd', p, v_blk)
        return o.reshape(B, GRID_W, NH, DH)

    out = lax.map(row_block, jnp.arange(rows, dtype=jnp.int32))
    return out.transpose(1, 0, 2, 3, 4).reshape(B, S, NH * DH)

def _token_mixing(u, w_in, decay_fwd, decay_bwd, rel_bias, w_ret_out, w_na_out, w_out, pos):
    B, S, _ = u.shape
    points = [sum(MIX_SPLITS[:i + 1]) for i in range(len(MIX_SPLITS) - 1)]
    rq, rk, rv, rg, nq, nk, nv, g_ret, g_na = jnp.split(u @ w_in, points, axis=-1)
    heads = lambda a, d: a.reshape(B, S, RET_HEADS, d).transpose(0, 2, 1, 3).astype(jnp.float32)
    q = _rotary(heads(rq, RET_QK_DIM), pos)
    k = _rotary(heads(rk, RET_QK_DIM), pos) * (RET_QK_DIM ** -0.5)
    y = _bidirectional_retention(q, k, heads(rv, RET_V_DIM), decay_fwd, decay_bwd)
    y = y * lax.rsqrt(jnp.mean(y * y, axis=-1, keepdims=True) + RMS_EPS)
    y = y.transpose(0, 2, 1, 3).reshape(B, S, RET_V_W).astype(u.dtype)
    y_ret = (jax.nn.silu(rg) * y) @ w_ret_out
    na_heads = lambda a: a.reshape(B, S, NA_HEADS, NA_HEAD_DIM)
    y_na = _neighborhood_attention(na_heads(nq), na_heads(nk), na_heads(nv), rel_bias) @ w_na_out
    merged = jax.nn.sigmoid(g_ret) * y_ret + jax.nn.sigmoid(g_na) * y_na
    return merged @ w_out

def first_inputs(seed: int = 0) -> dict:
    key = jax.random.key(seed)
    ks = jax.random.split(key, 20)
    f32 = jnp.float32

    def w(k, shape, fan_in):
        return jax.random.normal(k, (DEPTH,) + shape, f32) * (fan_in ** -0.5)

    def gain(k):
        return 1.0 + 0.05 * jax.random.normal(k, (DEPTH, D_MODEL), f32)

    gamma0 = 1.0 - 2.0 ** (-5.0 - np.arange(RET_HEADS, dtype=np.float32))
    logit0 = jnp.asarray(np.log(gamma0 / (1.0 - gamma0)), f32)
    return {
        "x": jax.random.normal(ks[0], (BATCH, SEQ, D_MODEL), f32),
        "ffn1_pre_norm": gain(ks[1]),
        "ffn1_w_in": w(ks[2], (D_MODEL, 2 * D_FF), D_MODEL),
        "ffn1_w_out": w(ks[3], (D_FF, D_MODEL), D_FF),
        "ffn1_post_norm": gain(ks[4]),
        "mix_pre_norm": gain(ks[5]),
        "w_mix_in": w(ks[6], (D_MODEL, MIX_IN_W), D_MODEL),
        "ret_decay_fwd": logit0[None] + 0.1 * jax.random.normal(ks[7], (DEPTH, RET_HEADS), f32),
        "ret_decay_bwd": logit0[None] + 0.1 * jax.random.normal(ks[8], (DEPTH, RET_HEADS), f32),
        "na_rel_bias": 0.02 * jax.random.normal(ks[9], (DEPTH, NA_HEADS, NA_REL_ROWS, NA_REL_COLS), f32),
        "w_ret_out": w(ks[10], (RET_V_W, D_MODEL), RET_V_W),
        "w_na_out": w(ks[11], (NA_W, D_MODEL), NA_W),
        "w_mix_out": w(ks[12], (D_MODEL, D_MODEL), D_MODEL),
        "mix_post_norm": gain(ks[13]),
        "ffn2_pre_norm": gain(ks[14]),
        "ffn2_w_in": w(ks[15], (D_MODEL, 2 * D_FF), D_MODEL),
        "ffn2_w_out": w(ks[16], (D_FF, D_MODEL), D_FF),
        "ffn2_post_norm": gain(ks[17]),
    }

def first_block(x, ffn1_pre_norm, ffn1_w_in, ffn1_w_out, ffn1_post_norm, mix_pre_norm, w_mix_in,
              ret_decay_fwd, ret_decay_bwd, na_rel_bias, w_ret_out, w_na_out, w_mix_out, mix_post_norm,
              ffn2_pre_norm, ffn2_w_in, ffn2_w_out, ffn2_post_norm):
    S = x.shape[1]
    pos = jnp.arange(S, dtype=jnp.float32)
    for l in range(DEPTH):
        h = _swiglu(_rms_norm(x, ffn1_pre_norm[l]), ffn1_w_in[l], ffn1_w_out[l])
        x = x + 0.5 * _rms_norm(h, ffn1_post_norm[l])
        m = _token_mixing(_rms_norm(x, mix_pre_norm[l]), w_mix_in[l], ret_decay_fwd[l], ret_decay_bwd[l],
                          na_rel_bias[l], w_ret_out[l], w_na_out[l], w_mix_out[l], pos)
        x = x + _rms_norm(m, mix_post_norm[l])
        h = _swiglu(_rms_norm(x, ffn2_pre_norm[l]), ffn2_w_in[l], ffn2_w_out[l])
        x = x + 0.5 * _rms_norm(h, ffn2_post_norm[l])
    return x


DEPTH_2 = 2

N_MIXERS = 2
N_A = (DEPTH_2 + 1) // 2
N_B = DEPTH_2 // 2
WIDTH = 3 * D_MODEL // 2
LRU_HEADS = 12
LRU_BLOCK = WIDTH // LRU_HEADS
CONV_A = 4
CONV_B = 3
LRU_C = 8.0
NORM_EPS = 1e-6


def rmsnorm(x, g):
    xf = x.astype(jnp.float32)
    inv = lax.rsqrt(jnp.mean(xf * xf, axis=-1, keepdims=True) + NORM_EPS)
    return (xf * inv * g.astype(jnp.float32)).astype(x.dtype)

def causal_depthwise_conv(u, w, b=None):
    k_width = w.shape[0]
    s = u.shape[1]
    up = jnp.pad(u, ((0, 0), (k_width - 1, 0), (0, 0)))
    out = up[:, 0:s] * w[0]
    for k in range(1, k_width):
        out = out + up[:, k:k + s] * w[k]
    if b is not None:
        out = out + b
    return out

def rg_lru(u, gate_w, gate_b, lam):
    bsz, s, w = u.shape
    uh = u.reshape(bsz, s, LRU_HEADS, LRU_BLOCK)
    g = jnp.einsum('bshi,hio->bsho', uh, gate_w) + gate_b
    g = jax.nn.sigmoid(g.astype(jnp.float32))
    r = g[..., :LRU_BLOCK].reshape(bsz, s, w)
    i = g[..., LRU_BLOCK:].reshape(bsz, s, w)
    log_a = -LRU_C * r * jax.nn.softplus(-lam.astype(jnp.float32))
    a = jnp.exp(log_a)
    mult = jnp.sqrt(-jnp.expm1(2.0 * log_a))
    bterm = mult * (i * u.astype(jnp.float32))

    def combine(left, right):
        a_l, b_l = left
        a_r, b_r = right
        return a_l * a_r, a_r * b_l + b_r

    _, h = lax.associative_scan(combine, (a, bterm), axis=1)
    return h.astype(u.dtype)

def recurrent_mixer(h, w_in, conv_w, conv_b, gate_w, gate_b, lam, w_out):
    u = jnp.einsum('bsd,dc->bsc', h, w_in)
    gate, xb = u[..., :WIDTH], u[..., WIDTH:]
    xb = causal_depthwise_conv(xb, conv_w, conv_b)
    y = rg_lru(xb, gate_w, gate_b, lam)
    return jnp.einsum('bsc,cd->bsd', y * jax.nn.silu(gate), w_out)

def shortconv_mixer(h, w_in, conv_w, w_out):
    u = jnp.einsum('bsd,dc->bsc', h, w_in)
    bg = u[..., :WIDTH]
    cg = u[..., WIDTH:2 * WIDTH]
    xv = u[..., 2 * WIDTH:3 * WIDTH]
    gate = u[..., 3 * WIDTH:]
    y = bg * causal_depthwise_conv(cg * xv, conv_w)
    return jnp.einsum('bsc,cd->bsd', y * jax.nn.silu(gate), w_out)

def second_inputs(seed: int = 0) -> dict:
    key = jax.random.key(seed)
    ks = jax.random.split(key, 16)
    f32 = jnp.float32
    x = jax.random.normal(ks[0], (BATCH, SEQ, D_MODEL), f32)
    norm_g = 1.0 + 0.02 * jax.random.normal(ks[1], (DEPTH_2, D_MODEL), f32)
    a_w_in = jax.random.normal(ks[2], (N_A, D_MODEL, 2 * WIDTH), f32) * D_MODEL ** -0.5
    a_conv_w = jax.random.normal(ks[3], (N_A, CONV_A, WIDTH), f32) * CONV_A ** -0.5
    a_conv_b = 0.02 * jax.random.normal(ks[4], (N_A, WIDTH), f32)
    a_gate_w = jax.random.normal(ks[5], (N_A, LRU_HEADS, LRU_BLOCK, 2 * LRU_BLOCK), f32) * LRU_BLOCK ** -0.5
    a_gate_b = 0.02 * jax.random.normal(ks[6], (N_A, LRU_HEADS, 2 * LRU_BLOCK), f32)
    a0 = jax.random.uniform(ks[7], (N_A, WIDTH), f32, minval=0.9, maxval=0.999)
    a_lambda = jnp.log(a0) - jnp.log1p(-a0)
    a_w_out = jax.random.normal(ks[8], (N_A, WIDTH, D_MODEL), f32) * WIDTH ** -0.5
    b_w_in = jax.random.normal(ks[9], (N_B, D_MODEL, 4 * WIDTH), f32) * D_MODEL ** -0.5
    b_conv_w = jax.random.normal(ks[10], (N_B, CONV_B, WIDTH), f32) * CONV_B ** -0.5
    b_w_out = jax.random.normal(ks[11], (N_B, WIDTH, D_MODEL), f32) * WIDTH ** -0.5
    final_g = 1.0 + 0.02 * jax.random.normal(ks[12], (D_MODEL,), f32)
    return {"x": x, "norm_g": norm_g, "a_w_in": a_w_in, "a_conv_w": a_conv_w,
            "a_conv_b": a_conv_b, "a_gate_w": a_gate_w, "a_gate_b": a_gate_b,
            "a_lambda": a_lambda, "a_w_out": a_w_out, "b_w_in": b_w_in,
            "b_conv_w": b_conv_w, "b_w_out": b_w_out, "final_g": final_g}

def second_block(x, norm_g, a_w_in, a_conv_w, a_conv_b, a_gate_w, a_gate_b, a_lambda,
              a_w_out, b_w_in, b_conv_w, b_w_out, final_g):
    for i in range(DEPTH_2):
        h = rmsnorm(x, norm_g[i])
        j = i // N_MIXERS
        if i % N_MIXERS == 0:
            x = x + recurrent_mixer(h, a_w_in[j], a_conv_w[j], a_conv_b[j], a_gate_w[j],
                                    a_gate_b[j], a_lambda[j], a_w_out[j])
        else:
            x = x + shortconv_mixer(h, b_w_in[j], b_conv_w[j], b_w_out[j])
    return rmsnorm(x, final_g)


def setup_inputs(seed=0):
    out = dict(first_inputs(seed))
    for name, value in second_inputs(seed + 1).items():
        if name != "x":
            out[name + "_2"] = value
    return out


def reference(
    x, ffn1_pre_norm, ffn1_w_in, ffn1_w_out, ffn1_post_norm, mix_pre_norm, w_mix_in,
    ret_decay_fwd, ret_decay_bwd, na_rel_bias, w_ret_out, w_na_out, w_mix_out, mix_post_norm,
    ffn2_pre_norm, ffn2_w_in, ffn2_w_out, ffn2_post_norm, norm_g_2, a_w_in_2, a_conv_w_2,
    a_conv_b_2, a_gate_w_2, a_gate_b_2, a_lambda_2, a_w_out_2, b_w_in_2, b_conv_w_2, b_w_out_2,
    final_g_2,
):
    x = first_block(
        x, ffn1_pre_norm, ffn1_w_in, ffn1_w_out, ffn1_post_norm, mix_pre_norm, w_mix_in,
        ret_decay_fwd, ret_decay_bwd, na_rel_bias, w_ret_out, w_na_out, w_mix_out,
        mix_post_norm, ffn2_pre_norm, ffn2_w_in, ffn2_w_out, ffn2_post_norm,
    )
    return second_block(
        x, norm_g_2, a_w_in_2, a_conv_w_2, a_conv_b_2, a_gate_w_2, a_gate_b_2, a_lambda_2,
        a_w_out_2, b_w_in_2, b_conv_w_2, b_w_out_2, final_g_2,
    )


_drawn_inputs = setup_inputs


def setup_inputs(seed=0):
    import zlib

    import numpy as np

    out = dict(_drawn_inputs(seed))
    spreads = {}
    factors = {'na_rel_bias': 8.0,
     'ffn2_post_norm': 3.031,
     'norm_g_2': 3.491,
     'a_conv_b_2': 3.123,
     'a_gate_b_2': 8.0,
     'final_g_2': 2.836}
    for name, (base, spread) in spreads.items():
        noise = np.random.default_rng([zlib.crc32(name.encode()), seed]).standard_normal(out[name].shape)
        drawn = base * np.exp(spread * noise) if base else spread * noise
        out[name] = __import__('jax').numpy.asarray(drawn.astype(out[name].dtype))
    for name, factor in factors.items():
        out[name] = (out[name] * factor).astype(out[name].dtype)
    return out
```

```python
from contextlib import ExitStack

import numpy as np

import concourse.bass as bass
from concourse import mybir

F32 = mybir.dt.float32
F32R = mybir.dt.float32r
ALU = mybir.AluOpType
ACT = mybir.ActivationFunctionType

P = 128
S = 256
T = S // P
DM = 1024
KD = DM // P
FF = 2816
W2 = 1536
CH = W2 // P
RH, RQ, RV = 4, 128, 256
NH, ND = 8, 64
GW, GR = 64, S // 64
WIN = 16
REL_R, REL_C = 15, 31
EPS = 1e-6
BIG = 1e30
UNIT = 512
GROUP = 4 * UNIT
RING = 4

STAGES = [("f1_in", 22), ("f1_out", 11), ("mix_in", 26), ("na_out", 2), ("ret_out", 4), ("mix_out", 4),
          ("f2_in", 22), ("f2_out", 11), ("a_in", 12), ("a_out", 6), ("b_in", 24), ("b_out", 6)]
NG = sum(n for _, n in STAGES)
FIRST_GROUP = {name: sum(n for _, n in STAGES[:i]) for i, (name, _) in enumerate(STAGES)}
GROUPS = dict(STAGES)

ACC_READERS = {"f1_in": "V" * 11, "f1_out": "V", "mix_in": "AAAVVAAVVAAAA", "na_out": "V", "mix_out": "V",
               "f2_in": "V" * 11, "f2_out": "V", "a_in": "AAAVVV", "a_out": "V", "b_in": "V" * 12, "b_out": "V"}
ACC_ORDER = "".join(ACC_READERS.values())
FIRST_ACC = {}
for _name in ACC_READERS:
    FIRST_ACC[_name] = sum(len(v) for k, v in ACC_READERS.items() if k in FIRST_ACC)

FILL_COUNTS = [("t0", 4), ("f1_in", 11), ("t1", 4), ("nq", 2), ("nk", 2), ("rq", 2), ("rk", 2), ("rs", 4), ("rp", 4),
               ("yna", 2), ("yret", 4), ("merged", 4), ("t2", 4), ("f2_in", 11), ("t3", 4),
               ("a_in", 12), ("t4", 4), ("b_in", 12)]
FIRST_FILL = {name: sum(n for _, n in FILL_COUNTS[:i]) for i, (name, _) in enumerate(FILL_COUNTS)}
SPLIT_COUNTS = [("t0", 4), ("f1_in", 11), ("t1", 4), ("yna", 2), ("yret", 4), ("merged", 4), ("t2", 4),
                ("f2_in", 11), ("t3", 4), ("gate", 6), ("t4", 4), ("b_in", 12)]
FIRST_SPLIT = {name: sum(n for _, n in SPLIT_COUNTS[:i]) for i, (name, _) in enumerate(SPLIT_COUNTS)}

RELEASE = []
for _name, _n in STAGES:
    for _g in range(_n):
        if _name.endswith("_in") and _g % 2 or _name.endswith("_out") and _g == _n - 1:
            if _name == "ret_out":
                RELEASE.append(("ret", T))
            else:
                RELEASE.append(("acc", FIRST_ACC[_name] + (_g // 2 if _name.endswith("_in") else 0) + 1))
        else:
            RELEASE.append(("used", 1 + sum(kind == "used" for kind, _ in RELEASE)))

NORMS = [(0, False, 0.0, None), (1, True, 0.5, "f1_out"), (2, True, 1.0, "mix_out"), (3, True, 0.5, "f2_out"),
         (4, False, 1.0, "a_out"), (5, False, 1.0, "b_out")]


class Chain:

    def __init__(self, engine, semaphore):
        self.engine, self.semaphore, self.base, self.n = engine, semaphore, 0, 0

    def __call__(self, instruction):
        instruction.then_inc(self.semaphore, 1)
        self.n += 1
        self.engine.wait_ge(self.semaphore, self.base + self.n)


def build(nc, weights, x_in, gains, ident_in, rot_in, colmask_in, dist_in, decay_in, lam_in, bias_in, gate_w_in,
          gate_b_in, conv_a_in, conv_ab_in, conv_b_in, out):
    with ExitStack() as ctx:
        base = nc.sbuf_base + (-nc.sbuf_base) % 32
        cursor = [base]

        def at(name, shape, dt, offset):
            return nc.alloc_sbuf_tensor_at(name, shape, dt, offset=offset)

        def sb(name, shape, dt=F32):
            size = 4 * int(np.prod(shape[1:]))
            size += -size % 32
            tensor = at(name, shape, dt, cursor[0])
            cursor[0] += size
            return tensor

        def sem(name):
            return ctx.enter_context(nc.semaphore(name))

        raw = sb("raw", [P, RING, GROUP])
        w_hi = sb("w_hi", [P, RING, GROUP], F32R)
        w_lo = sb("w_lo", [P, RING, GROUP], F32R)
        xT_hi = sb("xT_hi", [P, KD, S], F32R)
        xT_lo = sb("xT_lo", [P, KD, S], F32R)
        x = sb("x", [P, T, DM])
        gain_post = sb("gain_post", [P, DM])
        gain_pre = sb("gain_pre", [P, DM])
        ident = sb("ident", [P, P])
        rot = sb("rot", [P, T, 3, 64])
        colmask = sb("colmask", [P, GW])
        conv_a = sb("conv_a", [P, CH, 4])
        conv_ab = sb("conv_ab", [P, CH])
        conv_b = sb("conv_b", [P, CH, 3])
        gate_b = sb("gate_b", [P, CH, 2])
        logit = sb("logit", [P, 2 * RH + CH])
        ls = [sb(f"ls{i}", [P, 2 * RH + CH]) for i in range(5)]
        lrate = sb("lrate", [P, 2, CH])
        eps1 = sb("eps1", [P, 1])
        eps4 = sb("eps4", [P, 1])
        zero = sb("zero", [P, 1])
        sumsq = sb("sumsq", [P, 4])
        std = sb("std", [P, 4])
        rstd = sb("rstd", [P, 4])
        ret_sumsq = sb("ret_sumsq", [P, T, RH])
        ret_std = sb("ret_std", [P, T, RH])
        ret_rstd = sb("ret_rstd", [P, T, RH])
        neg_max = sb("neg_max", [P, T * NH])
        prob_sum = sb("prob_sum", [P, T * NH])
        prob_rec = sb("prob_rec", [P, T * NH])

        area = cursor[0]
        temp_at = nc.sbuf_usable_end - 4 * T * DM - 64
        temp_at = temp_at() if callable(temp_at) else temp_at
        temp_at -= temp_at % 32
        assert temp_at - area >= 67584, temp_at - area
        tmp = at("tmp", [P, T, DM], F32, temp_at)
        hT_hi = at("hT_hi", [P, FF // P, S], F32R, area)
        hT_lo = at("hT_lo", [P, FF // P, S], F32R, area + 22528)
        silu_g = at("silu_g", [P, T, 256], F32, area + 45056)
        prod = at("prod", [P, 2, T, 256], F32, area + 47104)
        nqT = [at(f"nqT{i}", [P, NH // 2, S], F32, area + 4096 * i) for i in range(2)]
        nkT = at("nkT", [P, NH // 2, S], F32, area + 8192)
        nv = at("nv", [P, T, NH * ND], F32, area + 12288)
        yretT_hi = at("yretT_hi", [P, KD, S], F32R, area)
        yretT_lo = at("yretT_lo", [P, KD, S], F32R, area + 8192)
        rqT = at("rqT", [P, RH, S], F32, area + 16384)
        rkT = at("rkT", [P, RH, S], F32, area + 20480)
        m_ret = at("m_ret", [P, T, DM], F32, area + 16384)
        rv = at("rv", [P, T, RH * RV], F32, area + 24576)
        ynaT_hi = at("ynaT_hi", [P, NH // 2, S], F32R, area + 24576)
        ynaT_lo = at("ynaT_lo", [P, NH // 2, S], F32R, area + 28672)
        decay = at("decay", [P, RH, T, S], F32, area + 32768)
        m_na = at("m_na", [P, T, DM], F32, area + 32768)
        y_ret = at("y_ret", [P, T, RH * RV], F32, area + 40960)
        y_na = at("y_na", [P, T, NH * ND], F32, area + 49152)
        stage = at("stage", [P, T, 512], F32, area + 53248)
        rot_b = at("rot_b", [P, T, 512], F32, area + 57344)
        dist = at("dist", [P, 2, T, S], F32, area + 57344)
        bias_raw = at("bias_raw", [P, 2, GR, GW], F32, area + 61440)
        bias_m = at("bias_m", [P, 2, GR, GW], F32, area + 63488)
        neg_s = at("neg_s", [P, 2, S], F32, area + 65536)
        prob = at("prob", [P, 2, S], F32, temp_at)
        probT = at("probT", [P, 2, T, P], F32, temp_at + 2048)
        u = at("u", [P, CH, S], F32, area)
        ri = at("ri", [P, CH, 2, S], F32, area + 12288)
        av = at("av", [P, CH, S], F32, area + 36864)
        gate_w = at("gate_w", [P, CH, 2, P], F32, area + 51200)
        a_stage = at("a_stage", [P, T, 512], F32, area + 63488)
        yg = at("yg", [P, 2, 512], F32, temp_at)
        yT_hi = at("yT_hi", [P, CH, S], F32R, area + 12288)
        yT_lo = at("yT_lo", [P, CH, S], F32R, area + 24576)
        b_gate = at("b_gate", [P, T, 256], F32, area)
        b_prod = at("b_prod", [P, 2, T, 256], F32, area + 2048)
        b_conv = at("b_conv", [P, S], F32, area + 6144)
        b_y = at("b_y", [P, 2, S], F32, area + 7168)

        acc = ctx.enter_context(nc.psum_tensor("acc", [P, T, 2, UNIT], F32))
        aux = ctx.enter_context(nc.psum_tensor("aux", [P, 4, UNIT], F32))

        landed = [sem(f"landed{i}") for i in range(RING)]
        hi_done = sem("hi_done")
        lo_done = sem("lo_done")
        group_used = sem("group_used")
        acc_full = [sem(f"acc_full{t}") for t in range(T)]
        acc_free_act = [sem(f"acc_free_act{t}") for t in range(T)]
        acc_free_dve = [sem(f"acc_free_dve{t}") for t in range(T)]
        gate_ready = [sem(f"gate_ready{t}") for t in range(T)]
        bank_full = sem("bank_full")
        bank_hi = sem("bank_hi")
        bank_free = sem("bank_free")
        consts_in = sem("consts_in")
        x_landed = sem("x_landed")
        gains_in = sem("gains_in")
        post_std = sem("post_std")
        pre_std = sem("pre_std")
        x_ready = sem("x_ready")
        xn_ready = sem("xn_ready")
        act_step = sem("act_step")
        dve_step = sem("dve_step")
        pool_step = sem("pool_step")
        eps_set = sem("eps_set")
        ls_neg = sem("ls_neg")
        ls_exp = sem("ls_exp")
        decay_arg = sem("decay_arg")
        decay_done = sem("decay_done")
        dist_in_s = sem("dist_in_s")
        bias_in_s = [sem(f"bias_in{i}") for i in range(2)]
        bias_ready = sem("bias_ready")
        pad_set = sem("pad_set")
        rot_done = sem("rot_done")
        s_full = sem("s_full")
        s_reduced = sem("s_reduced")
        p_ready = sem("p_ready")
        pT_full = sem("pT_full")
        pT_copied = sem("pT_copied")
        o_full = sem("o_full")
        o_taken = sem("o_taken")
        ret_sq = sem("ret_sq")
        ret_std_s = sem("ret_std_s")
        y_ret_ready = sem("y_ret_ready")
        ret_acc_full = sem("ret_acc_full")
        merged_ready = sem("merged_ready")
        gate_w_in_s = sem("gate_w_in_s")
        conv_head = sem("conv_head")
        g_full = sem("g_full")
        g_taken = sem("g_taken")
        iu_ready = sem("iu_ready")
        et_ready = sem("et_ready")
        v_ready = sem("v_ready")
        mult_ready = sem("mult_ready")
        yg_ready = sem("yg_ready")
        b_y_ready = sem("b_y_ready")
        stored = sem("stored")

        def wait_acc_free(pe, t, n):
            a = ACC_ORDER[:n].count("A")
            v = n - a
            if a:
                pe.wait_ge(acc_free_act[t], a)
            if v:
                pe.wait_ge(acc_free_dve[t], v)

        def act_frees(t, instruction):
            instruction.then_inc(acc_free_act[t], 1)

        block = ctx.enter_context(nc.Block())

        @block.sync
        def _(sp):
            for t in range(T):
                sp.dma_start(x[:, t, :], x_in[t * P:(t + 1) * P, :]).then_inc(x_landed, 16)
            for g in range(RING):
                sp.dma_start(raw[:, g, :], weights[g]).then_inc(landed[g], 16)
            with sp.Fori(1, NG // RING) as lap:
                for s in range(RING):
                    sp.wait_ge(lo_done, lap * RING + (s + 1 - RING))
                    sp.dma_start(raw[:, s, :], weights[bass.ds(lap * RING + s, 1)].rearrange("a p n -> p (a n)"))\
                        .then_inc(landed[s], 16)
            for g in range(NG // RING * RING, NG):
                sp.wait_ge(lo_done, g + 1 - RING)
                sp.dma_start(raw[:, g % RING, :], weights[g]).then_inc(landed[g % RING], 16)
            for t in range(T):
                sp.wait_ge(xn_ready, 2 * 2 * 5 + 2 * (t + 1))
                sp.dma_start(out[t * P:(t + 1) * P, :], tmp[:, t, :]).then_inc(stored, 16)
            sp.wait_ge(stored, 16 * T)

        @block.gpsimd
        def _(pool):
            g = nc.gpsimd
            step = Chain(pool, pool_step)
            g.memset(eps1[:], EPS).then_inc(eps_set, 1)
            g.memset(eps4[:], 4 * EPS).then_inc(eps_set, 1)
            g.memset(zero[:], 0.0).then_inc(eps_set, 1)

            def load_gains(n, post, pre):
                if post is not None:
                    pool.dma_start(gain_post[:], gains[post:post + 1, :].partition_broadcast(P)).then_inc(gains_in, 16)
                else:
                    pool.dma_start(gain_post[0:1, 0:16], gains[0:1, 0:16]).then_inc(gains_in, 16)
                pool.dma_start(gain_pre[:], gains[pre:pre + 1, :].partition_broadcast(P)).then_inc(gains_in, 16)

            load_gains(0, None, 0)
            for dst, src in ((ident, ident_in), (colmask, colmask_in), (conv_a, conv_a_in), (conv_ab, conv_ab_in),
                             (conv_b, conv_b_in), (gate_b, gate_b_in), (rot, rot_in)):
                pool.dma_start(dst[:], src).then_inc(consts_in, 16)
            pool.dma_start(logit[:, 0:2 * RH], decay_in.partition_broadcast(P)).then_inc(consts_in, 16)
            pool.dma_start(logit[:, 2 * RH:], lam_in).then_inc(consts_in, 16)
            pool.wait_ge(xn_ready, 4)
            load_gains(1, 1, 2)
            pool.dma_start(dist[:], dist_in).then_inc(dist_in_s, 16)

            def load_bias(s):
                t, h = s // NH, s % NH
                if s >= 2:
                    pool.wait_ge(bias_ready, s - 1)
                for r in range(2):
                    first = GR - 1 - 2 * t - r
                    pool.dma_start(bias_raw[r * GW:(r + 1) * GW, s % 2], bias_in[:, h, first:first + GR, :])\
                        .then_inc(bias_in_s[s % 2], 16)

            load_bias(0)
            load_bias(1)
            pool.wait_ge(xn_ready, 8)
            load_gains(2, 3, 4)
            g.memset(nqT[0][64:128], 0.0).then_inc(pad_set, 1)
            pool.wait_ge(pad_set, 1)
            g.memset(nqT[1][0:64], 0.0).then_inc(pad_set, 1)
            pool.wait_ge(pad_set, 2)

            def mask_bias(s):
                pool.wait_ge(bias_in_s[s % 2], 32 * (s // 2 + 1))
                if s == 0:
                    pool.wait_ge(consts_in, 16 * 9)
                if s >= 2:
                    pool.wait_ge(s_reduced, s - 1)
                g.tensor_tensor(bias_m[:, s % 2], bias_raw[:, s % 2],
                                colmask[:].unsqueeze(1).to_broadcast([P, GR, GW]), ALU.add).then_inc(bias_ready, 1)
                if s + 2 < T * NH:
                    load_bias(s + 2)

            mask_bias(0)
            mask_bias(1)
            for n in range(2 * T):
                t = n % T
                pool.wait_ge(acc_free_dve[t], ACC_ORDER[:FIRST_ACC["mix_in"] + 4 + n // T].count("V"))
                g.tensor_tensor(stage[:, t], stage[:, t], rot_b[:, t], ALU.add).then_inc(rot_done, 1)
                mask_bias(n + 2)
            for s in range(2 * T + 2, T * NH):
                mask_bias(s)
            pool.wait_ge(xn_ready, 12)
            load_gains(3, 5, 6)
            pool.wait_ge(x_ready, 2 * 2 + 1)
            pool.dma_start(gate_w[:], gate_w_in).then_inc(gate_w_in_s, 16)
            pool.wait_ge(xn_ready, 16)
            load_gains(4, None, 7)
            for ch in range(CH):
                pool.wait_ge(g_taken, ch + 1)
                g.tensor_tensor(ri[:, ch, 1], ri[:, ch, 1], u[:, ch], ALU.mult).then_inc(iu_ready, 1)
            pool.wait_ge(xn_ready, 20)
            load_gains(5, None, 8)

        @block.scalar
        def _(act):
            a = nc.scalar
            step = Chain(act, act_step)
            split = [0]

            def round_group(g, slot=None, wait_used=True):
                slot = g % RING if slot is None else slot
                lap = g // RING if isinstance(g, int) else None
                act.wait_ge(landed[slot], 16 * (lap + 1))
                if g >= RING:
                    kind, n = RELEASE[g - RING]
                    act.wait_ge({"used": group_used, "acc": acc_full[1], "ret": ret_acc_full}[kind], n)
                a.activation(w_hi[:, slot], raw[:, slot], ACT.Copy).then_inc(hi_done, 1)

            def round_to(n):
                while split[0] < min(n, NG):
                    round_group(split[0])
                    split[0] += 1

            def round_in_loop(base_group, i, i0, b, per=4):
                slot = (base_group + b) % RING
                lap0 = (base_group + b) // RING
                act.wait_ge(landed[slot], (i * (16 * per // RING)) + (16 * (lap0 + 1) - i0 * (16 * per // RING)))
                kind, n = RELEASE[base_group + b - RING]
                act.wait_ge({"used": group_used, "acc": acc_full[1]}[kind], i * (per // 2) + (n - i0 * (per // 2)))
                a.activation(w_hi[:, slot], raw[:, slot], ACT.Copy).then_inc(hi_done, 1)

            def take_hi(stage_name, n, dst, bank, source=None, scale=1.0, per_fill=None):
                act.wait_ge(bank_full, FIRST_FILL[stage_name] + n + 1)
                a.activation(dst, source if source is not None else aux[:, bank], ACT.Copy, scale=scale)\
                    .then_inc(bank_hi, 1)

            def norm(n, post, factor, stage_name):
                def root(t, which):
                    c = which * 2 + t
                    step(a.activation(tmp[:, t], acc[:, t] if which == 0 else x[:, t], ACT.Square,
                                      accum_out=sumsq[:, c:c + 1]))
                    a.activation(std[:, c:c + 1], sumsq[:, c:c + 1], ACT.Sqrt, bias=eps1[:], scale=1.0 / DM)\
                        .then_inc(post_std if which == 0 else pre_std, 1)

                def first(t):
                    if post:
                        act.wait_ge(acc_full[t], FIRST_ACC[stage_name] + 1)
                        root(t, 0)

                def second(t):
                    if post:
                        act.wait_ge(x_ready, 2 * (n - 1) + t + 1)
                    elif n:
                        act.wait_ge(acc_free_dve[t], ACC_ORDER[:FIRST_ACC[stage_name] + 1].count("V"))
                    else:
                        act.wait_ge(x_landed, 16 * T)
                        act.wait_ge(eps_set, 3)
                    root(t, 1)

                def parts(t):
                    if n == 5:
                        return
                    for h in range(2):
                        take_hi(f"t{n}", 2 * t + h, xT_hi[:, 4 * h:4 * h + 4, t * P:(t + 1) * P], 2 * t + h,
                                source=aux[:, 2 * t + h].rearrange("p (c q) -> p c q", c=4))

                first(0)
                second(0)
                if n == 0:
                    round_to(2)
                first(1)
                parts(0)
                second(1)
                parts(1)

            act.wait_ge(ls_neg, 1)
            a.activation(ls[1][:], ls[0][:], ACT.Exp).then_inc(ls_exp, 1)
            norm(*NORMS[0])

            def swiglu(which, normed):
                st = f"{which}_in"
                g0, c0, f0 = FIRST_GROUP[st], FIRST_ACC[st], FIRST_FILL[st]
                prods0 = ACC_ORDER[:c0].count("V")

                def silu(j, par, t):
                    act.wait_ge(acc_full[t], c0 + 1 + j)
                    if not (isinstance(j, int) and j == 0 and prods0 == 0):
                        act.wait_ge(acc_free_dve[t], prods0 + j)
                    a.activation(silu_g[:, t], acc[:, t, par, 0:256], ACT.Silu).then_inc(gate_ready[t], 1)

                def hidden_hi(j, par):
                    act.wait_ge(bank_full, f0 + 1 + j)
                    dst = hT_hi[:, bass.ds(2 * j, 2), :] if not isinstance(j, int) else hT_hi[:, 2 * j:2 * j + 2, :]
                    a.activation(dst, aux[:, par].rearrange("p (c q) -> p c q", c=2), ACT.Copy).then_inc(bank_hi, 1)

                def column(j, par, rounds):
                    rounds()
                    silu(j, par, 0)
                    if not (isinstance(j, int) and j == 0):
                        hidden_hi(j - 1, 1 - par)
                    silu(j, par, 1)

                for j in range(2):
                    column(j, j, lambda: round_to(g0 + 2 * j + 4))
                with act.Fori(1, 5) as i:
                    for b in range(2):
                        column(i * 2 + b, b, lambda: [round_in_loop(g0 + 6, i, 1, 2 * b + h) for h in range(2)])
                split[0] += 16
                column(10, 0, lambda: round_to(g0 + 24))
                hidden_hi(10, 0)
                g1, n1 = FIRST_GROUP[f"{which}_out"], GROUPS[f"{which}_out"]
                round_to(g1 + n1 + 2)

            swiglu("f1", 0)
            norm(*NORMS[1])

            g0, c0 = FIRST_GROUP["mix_in"], FIRST_ACC["mix_in"]
            gates = [11, 11]

            def exp_step(s):
                act.wait_ge(s_reduced, s + 1)
                if s >= 2:
                    act.wait_ge(pT_full, s - 1)
                a.activation(prob[:, s % 2], neg_s[:, s % 2], ACT.Exp, bias=neg_max[:, s:s + 1], scale=-1.0,
                             accum_out=prob_sum[:, s:s + 1]).then_inc(p_ready, 1)

            def ret_squares(h):
                act.wait_ge(bank_full, FIRST_FILL["rp"] + h + 1)
                for t in range(T):
                    i = a.activation(rot_b[:, t, 0:RV], aux[:, 0, t * RV:(t + 1) * RV], ACT.Square,
                                     accum_out=ret_sumsq[:, t, h:h + 1])
                    if t == 0:
                        step(i)
                    else:
                        i.then_inc(ret_sq, 1)
                act.wait_ge(ret_sq, h + 1)

            for c in range(13):
                for t in range(T):
                    par = c % 2
                    slot = 2 * c + t
                    round_to(g0 + 2 * c + 3 + t)
                    if c == 0 and t == 0:
                        for h in range(RH):
                            act.wait_ge(decay_arg, h + 1)
                            a.activation(decay[:, h], decay[:, h], ACT.Exp).then_inc(decay_done, 1)
                    source = acc[:, t, par]
                    act.wait_ge(acc_full[t], c0 + c + 1)
                    if c < 2:
                        if c:
                            act.wait_ge(bank_full, FIRST_FILL["nq"] + t + 1)
                        i = a.activation(stage[:, t], source, ACT.Copy, scale=ND ** -0.5 if c == 0 else 1.0)
                        act_frees(t, i)
                    elif c == 2:
                        act_frees(t, a.activation(nv[:, t], source, ACT.Copy))
                    elif c in (5, 6):
                        act_frees(t, a.activation(rv[:, t, (c - 5) * 512:(c - 4) * 512], source, ACT.Copy))
                    elif c in (7, 8):
                        i = a.activation(y_ret[:, t, (c - 7) * 512:(c - 6) * 512], source, ACT.Tanh, scale=0.5)
                        i.then_inc(gate_ready[t], 1)
                    elif c >= 9:
                        dst, col = (m_ret, c - 9) if c < 11 else (m_na, c - 11)
                        act_frees(t, a.activation(dst[:, t, col * 512:(col + 1) * 512], source, ACT.Tanh, scale=0.5))
                    if 6 <= slot < 6 + 16:
                        exp_step(slot - 6)
                    if 18 <= slot < 22:
                        ret_squares(slot - 18)
                    if slot == 22:
                        a.activation(ret_std[:], ret_sumsq[:], ACT.Sqrt, bias=eps4[:], scale=4.0 / RV)\
                            .then_inc(ret_std_s, 1)
                    if slot == 24:
                        for tt in range(T):
                            take_hi("yna", tt, ynaT_hi[:, :, tt * P:(tt + 1) * P], 1 + tt,
                                    source=aux[:, 1 + tt].rearrange("p (c q) -> p c q", c=4))
                    if slot in (24, 25):
                        tt = slot - 24
                        for h in range(2):
                            bank = 0 if h == 0 else 3
                            take_hi("yret", 2 * tt + h, yretT_hi[:, 4 * h:4 * h + 4, tt * P:(tt + 1) * P], bank,
                                    source=aux[:, bank].rearrange("p (c q) -> p c q", c=4))
            round_to(FIRST_GROUP["ret_out"] + 4)
            for t in range(T):
                for h in range(2):
                    take_hi("merged", 2 * t + h, xT_hi[:, 4 * h:4 * h + 4, t * P:(t + 1) * P], 2 * t + h,
                            source=aux[:, 2 * t + h].rearrange("p (c q) -> p c q", c=4), scale=0.5)
                if t == 0:
                    round_to(FIRST_GROUP["mix_out"] + 2)
            round_to(FIRST_GROUP["f2_in"] + 2)
            norm(*NORMS[2])

            swiglu("f2", 0)
            norm(*NORMS[3])

            g0, c0, f0 = FIRST_GROUP["a_in"], FIRST_ACC["a_in"], FIRST_FILL["a_in"]

            def conv_start(f):
                act.wait_ge(bank_full, f0 + f + 1)
                for k in range(2):
                    ch = 2 * f + k
                    a.activation(u[:, ch], aux[:, f % 2, k * S:(k + 1) * S], ACT.Identity,
                                 bias=conv_ab[:, ch:ch + 1], scale=conv_a[:, ch, 3:4]).then_inc(conv_head, 1)

            def gate_sigmoids(ch):
                act.wait_ge(g_full, ch + 1)
                for k in range(2):
                    i = a.activation(ri[:, ch, k], aux[:, 2 + ch % 2, k * S:(k + 1) * S], ACT.Sigmoid,
                                     bias=gate_b[:, ch, k:k + 1])
                    if k == 1:
                        i.then_inc(g_taken, 1)

            def exp_tanh(ch):
                act.wait_ge(iu_ready, ch + 1)
                a.activation(av[:, ch], ri[:, ch, 0], ACT.Exp, scale=lrate[:, 0, ch:ch + 1]).then_inc(et_ready, 1)
                a.activation(ri[:, ch, 0], ri[:, ch, 0], ACT.Tanh, scale=lrate[:, 1, ch:ch + 1]).then_inc(et_ready, 1)

            def gated_hi(n):
                act.wait_ge(yg_ready, n + 1)
                a.activation(yT_hi[:, 2 * n:2 * n + 2, :], yg[:, n % 2].rearrange("p (c q) -> p c q", c=2), ACT.Copy)\
                    .then_inc(bank_hi, 1)

            for c in range(6):
                for t in range(T):
                    round_to(g0 + 2 * c + 3 + t)
                    act.wait_ge(acc_full[t], c0 + c + 1)
                    if c:
                        act.wait_ge(bank_full, f0 + 2 * c)
                    if c < 3:
                        act_frees(t, a.activation(a_stage[:, t], acc[:, t, c % 2], ACT.Copy))
                    else:
                        a.activation(a_stage[:, t], acc[:, t, c % 2], ACT.Tanh, scale=0.5).then_inc(gate_ready[t], 1)
                    if t == 0 and 1 <= c <= 3:
                        conv_start(2 * c - 2)
                        conv_start(2 * c - 1)
                    if t == 1 and 1 <= c <= 3:
                        gate_sigmoids(4 * c - 4)
                        gate_sigmoids(4 * c - 3)
                    if t == 0 and 2 <= c <= 4:
                        gate_sigmoids(4 * c - 6)
                        gate_sigmoids(4 * c - 5)
                    if c == 4:
                        for ch in range(6 * t, 6 * t + 6):
                            exp_tanh(ch)
                    if c == 5 and t == 0:
                        for m in range(3):
                            act.wait_ge(v_ready, m + 1)
                            a.activation(ri[:, 4 * m:4 * m + 4, 0], ri[:, 4 * m:4 * m + 4, 0], ACT.Sqrt,
                                         bias=zero[:], scale=-1.0).then_inc(mult_ready, 1)
            for n in range(6):
                gated_hi(n)
                if n == 1:
                    round_to(FIRST_GROUP["a_out"] + 4)
            round_to(FIRST_GROUP["b_in"] + 2)
            norm(*NORMS[4])

            g0, c0, f0 = FIRST_GROUP["b_in"], FIRST_ACC["b_in"], FIRST_FILL["b_in"]
            prods0 = ACC_ORDER[:c0].count("V")

            def b_gates(j, par, t):
                act.wait_ge(acc_full[t], c0 + 1 + j)
                act.wait_ge(acc_free_dve[t], prods0 + j)
                a.activation(b_gate[:, t, 0:P], acc[:, t, par, 2 * P:3 * P], ACT.Silu).then_inc(gate_ready[t], 1)
                a.activation(b_gate[:, t, P:2 * P], acc[:, t, par, 3 * P:4 * P], ACT.Copy).then_inc(gate_ready[t], 1)

            def b_hi(j, par):
                act.wait_ge(b_y_ready, 1 + j)
                dst = yT_hi[:, j, :] if isinstance(j, int) else yT_hi[:, bass.ds(j, 1), :].rearrange("p a q -> p (a q)")
                a.activation(dst, b_y[:, par], ACT.Copy).then_inc(bank_hi, 1)

            def b_column(j, par, rounds):
                rounds()
                b_gates(j, par, 0)
                if not (isinstance(j, int) and j == 0):
                    b_hi(j - 1, 1 - par)
                b_gates(j, par, 1)

            for j in range(2):
                b_column(j, j, lambda: round_to(g0 + 2 * j + 4))
            with act.Fori(1, 6) as i:
                for b in range(2):
                    b_column(i * 2 + b, b, lambda: [round_in_loop(g0 + 6, i, 1, 2 * b + h) for h in range(2)])

            split[0] += 20
            b_hi(11, 1)
            round_to(NG)
            norm(*NORMS[5])

        @block.vector
        def _(dve):
            v = nc.vector
            step = Chain(dve, dve_step)
            split = [0]

            def low_group(g, slot):
                dve.wait_ge(hi_done, g + 1)
                v.tensor_tensor(w_lo[:, slot], raw[:, slot], w_hi[:, slot].bitcast(F32), ALU.subtract)\
                    .then_inc(lo_done, 1)

            def low_to(n):
                while split[0] < min(n, NG):
                    low_group(split[0], split[0] % RING)
                    split[0] += 1

            def low_in_loop(base_group, i, i0, b, per=4):
                low_group(i * per + (base_group + b - i0 * per), (base_group + b) % RING)

            def take_lo(stage_name, q, dst, hi, source, scale=None):
                dve.wait_ge(bank_hi, FIRST_SPLIT[stage_name] + q + 1)
                if scale is None:
                    i = v.tensor_tensor(dst, source, hi.bitcast(F32), ALU.subtract)
                else:
                    i = v.scalar_tensor_tensor(dst, source, scale, hi.bitcast(F32), ALU.mult, ALU.subtract)
                i.then_inc(bank_free, 1)

            def norm(n, post, factor, stage_name):
                posts = {1: 0, 2: 1, 3: 2}
                for t in range(T):
                    if n:
                        if t == 0:
                            dve.wait_ge(gains_in, 32 * (n + 1))
                        if post:
                            dve.wait_ge(post_std, 2 * posts[n] + t + 1)
                            step(v.reciprocal(rstd[:, t:t + 1], std[:, t:t + 1]))
                            i = v.scalar_tensor_tensor(tmp[:, t], acc[:, t].rearrange("p h n -> p (h n)"),
                                                       rstd[:, t:t + 1], gain_post[:], ALU.mult, ALU.mult)
                            i.then_inc(acc_free_dve[t], 1)
                            dve.wait_ge(acc_free_dve[t], ACC_ORDER[:FIRST_ACC[stage_name] + 1].count("V"))
                            v.scalar_tensor_tensor(x[:, t], tmp[:, t], factor, x[:, t], ALU.mult, ALU.add)\
                                .then_inc(x_ready, 1)
                        else:
                            dve.wait_ge(acc_full[t], FIRST_ACC[stage_name] + 1)
                            v.tensor_tensor(x[:, t], acc[:, t].rearrange("p h n -> p (h n)"), x[:, t], ALU.add)\
                                .then_inc(acc_free_dve[t], 1)
                    elif t == 0:
                        dve.wait_ge(gains_in, 32)
                        dve.wait_ge(x_landed, 16 * T)
                    dve.wait_ge(pre_std, 2 * n + t + 1)
                    step(v.reciprocal(rstd[:, 2 + t:3 + t], std[:, 2 + t:3 + t]))
                    for h in range(2):
                        part = slice(h * 512, (h + 1) * 512)
                        v.scalar_tensor_tensor(tmp[:, t, part], x[:, t, part], rstd[:, 2 + t:3 + t],
                                               gain_pre[:, part], ALU.mult, ALU.mult).then_inc(xn_ready, 1)
                    if n < 5:
                        for h in range(2):
                            cols = slice(t * P, (t + 1) * P)
                            take_lo(f"t{n}", 2 * t + h, xT_lo[:, 4 * h:4 * h + 4, cols],
                                    xT_hi[:, 4 * h:4 * h + 4, cols],
                                    aux[:, 2 * t + h].rearrange("p (c q) -> p c q", c=4))
                    if n == 0 and t == 0:
                        low_to(2)

            dve.wait_ge(consts_in, 16 * 9)
            step(v.tensor_scalar(ls[2][:], logit[:], -1.0, None, ALU.mult))
            v.tensor_tensor(ls[0][:], logit[:], ls[2][:], ALU.min).then_inc(ls_neg, 1)
            norm(*NORMS[0])
            dve.wait_ge(ls_exp, 1)
            step(v.tensor_scalar(ls[2][:], ls[1][:], 2.0, None, ALU.add))
            step(v.reciprocal(ls[3][:], ls[2][:]))
            step(v.tensor_tensor(ls[2][:], ls[1][:], ls[3][:], ALU.mult))
            step(v.tensor_tensor(ls[3][:], ls[2][:], ls[2][:], ALU.mult))
            step(v.tensor_scalar(ls[4][:], ls[3][:], 1.0 / 17, None, ALU.mult))
            for k in (15, 13, 11, 9, 7, 5, 3):
                step(v.scalar_tensor_tensor(ls[4][:], ls[4][:], 1.0 / k, ls[3][:], ALU.add, ALU.mult))
            step(v.scalar_tensor_tensor(ls[4][:], ls[4][:], 1.0, ls[2][:], ALU.add, ALU.mult))
            step(v.tensor_scalar(ls[0][:], logit[:], 0.0, None, ALU.min))
            step(v.scalar_tensor_tensor(ls[1][:], ls[4][:], -2.0, ls[0][:], ALU.mult, ALU.add))
            log_gamma = ls[1]
            step(v.tensor_scalar(lrate[:, 0], log_gamma[:, 2 * RH:], 8.0, None, ALU.mult))
            step(v.tensor_scalar(lrate[:, 1], log_gamma[:, 2 * RH:], 4.0, None, ALU.mult))

            def swiglu(which):
                st = f"{which}_in"
                g0, f0, q0 = FIRST_GROUP[st], FIRST_FILL[st], FIRST_SPLIT[st]
                gate0 = {"f1": 0, "f2": GATES_F2}[which]

                def up(j, par, t):
                    dve.wait_ge(gate_ready[t], gate0 + 1 + j)
                    if not (isinstance(j, int) and j < 2):
                        dve.wait_ge(bank_full, f0 - 1 + j)
                    v.tensor_tensor(prod[:, par, t], acc[:, t, par, 256:512], silu_g[:, t], ALU.mult)\
                        .then_inc(acc_free_dve[t], 1)

                def hidden_lo(j, par):
                    chunks = slice(2 * j, 2 * j + 2) if isinstance(j, int) else bass.ds(2 * j, 2)
                    dve.wait_ge(bank_hi, q0 + 1 + j)
                    v.tensor_tensor(hT_lo[:, chunks, :], aux[:, par].rearrange("p (c q) -> p c q", c=2),
                                    hT_hi[:, chunks, :].bitcast(F32), ALU.subtract).then_inc(bank_free, 1)

                def column(j, par, lows):
                    lows()
                    up(j, par, 0)
                    if not (isinstance(j, int) and j == 0):
                        hidden_lo(j - 1, 1 - par)
                    up(j, par, 1)

                for j in range(2):
                    column(j, j, lambda: low_to(g0 + 2 * j + 4))
                with dve.Fori(1, 5) as i:
                    for b in range(2):
                        column(i * 2 + b, b, lambda: [low_in_loop(g0 + 6, i, 1, 2 * b + h) for h in range(2)])
                split[0] += 16
                column(10, 0, lambda: low_to(g0 + 24))
                hidden_lo(10, 0)
                low_to(FIRST_GROUP[f"{which}_out"] + GROUPS[f"{which}_out"] + 2)

            GATES_F2 = 11 + 2
            swiglu("f1")
            norm(*NORMS[1])

            g0, c0 = FIRST_GROUP["mix_in"], FIRST_ACC["mix_in"]

            def copy_fill(name, n, copies):
                dve.wait_ge(bank_full, FIRST_FILL[name] + n + 1)
                for k, (dst, src) in enumerate(copies):
                    i = v.tensor_copy(dst, src)
                i.then_inc(bank_free, 1)

            def heads_of(bank):
                return aux[:, bank].rearrange("p (c q) -> p c q", c=4)

            def rotate(t, par, n):
                source = acc[:, t, par].rearrange("p (h s i) -> p h s i", h=RH, s=2)
                turned = rot_b[:, t].rearrange("p (h s i) -> p h s i", h=RH, s=2)
                v.tensor_tensor(stage[:, t].rearrange("p (a i) -> p a i", a=2 * RH),
                                acc[:, t, par].rearrange("p (a i) -> p a i", a=2 * RH),
                                rot[:, t, 0:1].to_broadcast([P, 2 * RH, 64]), ALU.mult)
                v.tensor_tensor(turned[:, :, 0], source[:, :, 1], rot[:, t, 2:3].to_broadcast([P, RH, 64]), ALU.mult)
                i = v.tensor_tensor(turned[:, :, 1], source[:, :, 0], rot[:, t, 1:2].to_broadcast([P, RH, 64]),
                                    ALU.mult)
                i.then_inc(acc_free_dve[t], 1)

            for c in range(13):
                for t in range(T):
                    par, slot = c % 2, 2 * c + t
                    low_to(g0 + 2 * c + 3 + t)
                    if slot == 0:
                        dve.wait_ge(dist_in_s, 16)
                        for h in range(RH):
                            step(v.tensor_scalar(decay[:, h], dist[:, 0], log_gamma[:, h:h + 1], None, ALU.mult))
                            v.scalar_tensor_tensor(decay[:, h].rearrange("p a q -> p (a q)"),
                                                   dist[:, 1].rearrange("p a q -> p (a q)"),
                                                   log_gamma[:, RH + h:RH + h + 1],
                                                   decay[:, h].rearrange("p a q -> p (a q)"), ALU.mult, ALU.add)\
                                .then_inc(decay_arg, 1)
                    if c in (3, 4):
                        dve.wait_ge(acc_full[t], c0 + c + 1)
                        if c == 3:
                            dve.wait_ge(bank_full, FIRST_FILL["nk"] + t + 1)
                            if t == 0:
                                dve.wait_ge(decay_arg, RH)
                        else:
                            dve.wait_ge(bank_full, FIRST_FILL["rq"] + t + 1)
                        rotate(t, par, T * (c - 3) + t)
                    if c in (7, 8):
                        dve.wait_ge(gate_ready[t], 11 + c - 6)
                        part = y_ret[:, t, (c - 7) * 512:(c - 6) * 512]
                        v.scalar_tensor_tensor(part, part, 1.0, acc[:, t, par], ALU.add, ALU.mult)\
                            .then_inc(acc_free_dve[t], 1)
                        if c == 8 and t == 1:
                            for tt in range(T):
                                dve.wait_ge(acc_free_dve[tt], ACC_ORDER[:c0 + c + 1].count("V"))
                    if slot == 2:
                        for tt in range(T):
                            cols = slice(tt * P, (tt + 1) * P)
                            if tt == 0:
                                dve.wait_ge(pad_set, 2)
                            copy_fill("nq", tt, [(nqT[e][64 * e:64 * e + 64, :, cols],
                                                  heads_of(tt)[64 * e:64 * e + 64]) for e in range(2)])
                    if slot == 4:
                        for tt in range(T):
                            copy_fill("nk", tt, [(nkT[:, :, tt * P:(tt + 1) * P], heads_of(tt))])
                    if 8 <= slot < 12:
                        name, dst = ("rq", rqT) if slot < 10 else ("rk", rkT)
                        copy_fill(name, t, [(dst[:, :, t * P:(t + 1) * P], heads_of(0))])
                    if 12 <= slot < 16:
                        h = slot - 12
                        dve.wait_ge(bank_full, FIRST_FILL["rs"] + h + 1)
                        if h == 0:
                            dve.wait_ge(decay_done, RH)
                        flat = decay[:, h].rearrange("p a q -> p (a q)")
                        v.scalar_tensor_tensor(flat, aux[:, 0], RQ ** -0.5, flat, ALU.mult, ALU.mult)\
                            .then_inc(bank_free, 1)
                    s = slot - 6
                    if 0 <= s - 1 < 16:
                        dve.wait_ge(pT_full, s)
                        if s - 1 >= 2:
                            dve.wait_ge(o_full, s - 2)
                        v.tensor_copy(probT[:, (s - 1) % 2].rearrange("p a q -> p (a q)"), aux[:, 2, 0:S])\
                            .then_inc(pT_copied, 1)
                    if 0 <= s - 2 < 16:
                        n = s - 2
                        dve.wait_ge(o_full, n + 1)
                        dve.wait_ge(p_ready, n + 1)
                        step(v.reciprocal(prob_rec[:, n:n + 1], prob_sum[:, n:n + 1]))
                        h = n % NH
                        v.tensor_scalar(y_na[:, n // NH, h * ND:(h + 1) * ND], aux[:, 3, 0:ND],
                                        prob_rec[:, n:n + 1], None, ALU.mult).then_inc(o_taken, 1)
                    if 0 <= s < 16:
                        dve.wait_ge(s_full, s + 1)
                        dve.wait_ge(bias_ready, s + 1)
                        if s >= 2:
                            dve.wait_ge(p_ready, s - 1)
                        v.tensor_tensor_reduce(out=neg_s[:, s % 2], in0=aux[:, 1, 0:S],
                                               in1=bias_m[:, s % 2].rearrange("p a q -> p (a q)"), scale=-1.0,
                                               scalar=3e38, op0=ALU.add, op1=ALU.min,
                                               accum_out=neg_max[:, s:s + 1]).then_inc(s_reduced, 1)
                    if 18 <= slot < 22:
                        h = slot - 18
                        dve.wait_ge(ret_sq, h + 1)
                        for tt in range(T):
                            part = y_ret[:, tt, h * RV:(h + 1) * RV]
                            i = v.tensor_tensor(part, part, aux[:, 0, tt * RV:(tt + 1) * RV], ALU.mult)
                        i.then_inc(bank_free, 1)
                        if h == RH - 1:
                            dve.wait_ge(bank_free, FIRST_FILL["rp"] + RH)
                    if slot == 22:
                        dve.wait_ge(ret_std_s, 1)
                        step(v.reciprocal(ret_rstd[:], ret_std[:]))
                        for tt in range(T):
                            for h in range(RH):
                                part = y_ret[:, tt, h * RV:(h + 1) * RV]
                                i = v.tensor_scalar(part, part, ret_rstd[:, tt, h:h + 1], None, ALU.mult)
                            i.then_inc(y_ret_ready, 1)
                    if slot == 24:
                        for tt in range(T):
                            cols = slice(tt * P, (tt + 1) * P)
                            take_lo("yna", tt, ynaT_lo[:, :, cols], ynaT_hi[:, :, cols], heads_of(1 + tt))
                    if slot in (24, 25):
                        tt = slot - 24
                        cols = slice(tt * P, (tt + 1) * P)
                        for h in range(2):
                            chunks = slice(4 * h, 4 * h + 4)
                            take_lo("yret", 2 * tt + h, yretT_lo[:, chunks, cols], yretT_hi[:, chunks, cols],
                                    heads_of(0 if h == 0 else 3))
            low_to(FIRST_GROUP["ret_out"] + 4)
            for t in range(T):
                dve.wait_ge(acc_full[t], FIRST_ACC["na_out"] + 1)
                dve.wait_ge(acc_free_act[t], ACC_ORDER[:FIRST_ACC["na_out"]].count("A"))
                v.scalar_tensor_tensor(m_na[:, t], m_na[:, t], 1.0, acc[:, t].rearrange("p h n -> p (h n)"),
                                       ALU.add, ALU.mult).then_inc(acc_free_dve[t], 1)
            for t in range(T):
                dve.wait_ge(acc_free_dve[t], ACC_ORDER[:FIRST_ACC["na_out"] + 1].count("V"))
                dve.wait_ge(ret_acc_full, t + 1)
                for h in range(2):
                    part = slice(h * 512, (h + 1) * 512)
                    step(v.scalar_tensor_tensor(m_ret[:, t, part], m_ret[:, t, part], 1.0, aux[:, 2 * t + h],
                                                ALU.add, ALU.mult))
                    v.tensor_tensor(m_ret[:, t, part], m_ret[:, t, part], m_na[:, t, part], ALU.add)\
                        .then_inc(merged_ready, 1)
                for h in range(2):
                    cols, chunks = slice(t * P, (t + 1) * P), slice(4 * h, 4 * h + 4)
                    take_lo("merged", 2 * t + h, xT_lo[:, chunks, cols], xT_hi[:, chunks, cols], heads_of(2 * t + h),
                            scale=0.5)
                if t == 0:
                    low_to(FIRST_GROUP["mix_out"] + 2)
            low_to(FIRST_GROUP["f2_in"] + 2)
            norm(*NORMS[2])

            swiglu("f2")
            norm(*NORMS[3])

            g0, c0, f0 = FIRST_GROUP["a_in"], FIRST_ACC["a_in"], FIRST_FILL["a_in"]
            gate0 = GATES_F2 + 11

            def conv_rest(f):
                dve.wait_ge(conv_head, 2 * f + 2)
                for lag in (1, 2, 3):
                    for k in range(2):
                        ch = 2 * f + k
                        i = v.scalar_tensor_tensor(u[:, ch, lag:], aux[:, f % 2, k * S:(k + 1) * S - lag],
                                                   conv_a[:, ch, 3 - lag:4 - lag], u[:, ch, lag:], ALU.mult, ALU.add)
                        if k == 1 and lag < 3:
                            step(i)
                i.then_inc(bank_free, 1)

            def rates(m):
                four = slice(4 * m, 4 * m + 4)
                dve.wait_ge(et_ready, 8 * (m + 1))
                step(v.scalar_tensor_tensor(ri[:, four, 0], av[:, four], 1.0, ri[:, four, 0], ALU.add, ALU.mult))
                step(v.tensor_scalar(av[:, four], ri[:, four, 0], 1.0, None, ALU.add))
                v.scalar_tensor_tensor(ri[:, four, 0], ri[:, four, 0], 2.0, ri[:, four, 0], ALU.add, ALU.mult)\
                    .then_inc(v_ready, 1)

            def scans(m):
                four = slice(4 * m, 4 * m + 4)
                dve.wait_ge(mult_ready, m + 1)
                step(v.tensor_tensor(ri[:, four, 1], ri[:, four, 1], ri[:, four, 0], ALU.mult))
                for ch in range(4 * m, 4 * m + 4):
                    i = v.tensor_tensor_scan(u[:, ch], av[:, ch], ri[:, ch, 1], 0.0, ALU.mult, ALU.add)
                step(i)

            def gate_fill_bank(n):
                return (0, 1, 2, 3, 0, 1)[n]

            def gated(n):
                dve.wait_ge(bank_full, f0 + 6 + n + 1)
                if n >= 2:
                    dve.wait_ge(bank_free, f0 + 6 + n - 1)
                v.scalar_tensor_tensor(yg[:, n % 2], aux[:, gate_fill_bank(n)], 0.5,
                                       u[:, 2 * n:2 * n + 2].rearrange("p c q -> p (c q)"), ALU.mult, ALU.mult)\
                    .then_inc(yg_ready, 1)

            def gated_lo(n):
                take_lo("gate", n, yT_lo[:, 2 * n:2 * n + 2].rearrange("p c q -> p (c q)"),
                        yT_hi[:, 2 * n:2 * n + 2].rearrange("p c q -> p (c q)"), yg[:, n % 2])

            for c in range(6):
                for t in range(T):
                    low_to(g0 + 2 * c + 3 + t)
                    if c >= 3:
                        dve.wait_ge(gate_ready[t], gate0 + c - 2)
                        v.scalar_tensor_tensor(a_stage[:, t], a_stage[:, t], 1.0, acc[:, t, c % 2], ALU.add, ALU.mult)\
                            .then_inc(acc_free_dve[t], 1)
                    if t == 0 and 1 <= c <= 3:
                        conv_rest(2 * c - 2)
                        conv_rest(2 * c - 1)
                    if c == 4 and t == 1:
                        rates(0)
                    if c == 5 and t == 0:
                        rates(1)
                        rates(2)
                    if c == 5 and t == 1:
                        for m in range(3):
                            scans(m)
            for n in range(6):
                gated(n)
                if n:
                    gated_lo(n - 1)
                if n == 2:
                    low_to(FIRST_GROUP["a_out"] + 4)
            gated_lo(5)
            low_to(FIRST_GROUP["b_in"] + 2)
            norm(*NORMS[4])

            g0, c0, f0, q0 = FIRST_GROUP["b_in"], FIRST_ACC["b_in"], FIRST_FILL["b_in"], FIRST_SPLIT["b_in"]
            gate0 = GATES_F2 + 11 + 3

            def b_products(j, par, t):
                dve.wait_ge(gate_ready[t], j * 2 + (gate0 + 2))
                if not (isinstance(j, int) and j < 2):
                    dve.wait_ge(bank_full, f0 - 1 + j)
                v.tensor_tensor(b_prod[:, par, t], acc[:, t, par, 0:2 * P], b_gate[:, t], ALU.mult)\
                    .then_inc(acc_free_dve[t], 1)

            def tap(j, k):
                if isinstance(j, int):
                    return conv_b[:, j, k:k + 1]
                return conv_b[:, bass.ds(j, 1), k:k + 1].rearrange("p a b -> p (a b)")

            def b_short_conv(j, par):
                dve.wait_ge(bank_full, f0 + 1 + j)
                if not (isinstance(j, int) and j == 0):
                    dve.wait_ge(b_y_ready, j)
                p = aux[:, par, S:2 * S]
                step(v.tensor_scalar(b_conv[:], p, tap(j, 2), None, ALU.mult))
                step(v.scalar_tensor_tensor(b_conv[:, 1:], p[:, 0:S - 1], tap(j, 1), b_conv[:, 1:], ALU.mult, ALU.add))
                step(v.scalar_tensor_tensor(b_conv[:, 2:], p[:, 0:S - 2], tap(j, 0), b_conv[:, 2:], ALU.mult, ALU.add))
                v.tensor_tensor(b_y[:, par], aux[:, par, 0:S], b_conv[:], ALU.mult).then_inc(b_y_ready, 1)

            def b_lo(j, par):
                dve.wait_ge(bank_hi, q0 + 1 + j)
                one = (slice(j, j + 1) if isinstance(j, int) else bass.ds(j, 1))
                v.tensor_tensor(yT_lo[:, one, :].rearrange("p a q -> p (a q)"), b_y[:, par],
                                yT_hi[:, one, :].rearrange("p a q -> p (a q)").bitcast(F32), ALU.subtract)\
                    .then_inc(bank_free, 1)

            def b_column(j, par, lows):
                lows()
                b_products(j, par, 0)
                if not (isinstance(j, int) and j == 0):
                    b_short_conv(j - 1, 1 - par)
                b_products(j, par, 1)
                if not (isinstance(j, int) and j == 0):
                    b_lo(j - 1, 1 - par)

            for j in range(2):
                b_column(j, j, lambda: low_to(g0 + 2 * j + 4))
            before, per_lap = step.n, 2 * 3
            with dve.Fori(1, 6) as i:
                step.base = (i - 1) * per_lap
                for b in range(2):
                    b_column(i * 2 + b, b, lambda: [low_in_loop(g0 + 6, i, 1, 2 * b + h) for h in range(2)])
                assert step.n == before + per_lap
            step.base = 0
            step.n = before + 5 * per_lap
            split[0] += 20
            b_short_conv(11, 1)
            b_lo(11, 1)
            low_to(NG)
            norm(*NORMS[5])

        @block.tensor
        def _(pe):
            m = nc.tensor

            def product(dst, hi, lo, k, t, slot, unit, first, last):
                cols = slice(t * P, (t + 1) * P)
                w = slice(unit * UNIT, (unit + 1) * UNIT)
                m.matmul(dst, hi[:, k, cols], w_hi[:, slot, w], start=first, stop=False)
                m.matmul(dst, hi[:, k, cols], w_lo[:, slot, w], start=False, stop=False)
                return m.matmul(dst, lo[:, k, cols], w_hi[:, slot, w], start=False, stop=last)

            def column_tile(g, slot0, par, t):
                for half in range(2):
                    if t == 0:
                        pe.wait_ge(lo_done, g + (half + 1))
                    for unit in range(4):
                        i = product(acc[:, t, par], xT_hi, xT_lo, 4 * half + unit, t, (slot0 + half) % RING, unit,
                                    half == 0 and unit == 0, half == 1 and unit == 3)
                    if t == 1 and half == 0:
                        i.then_inc(group_used, 1)
                i.then_inc(acc_full[t], 1)

            def wait_operand(fills):
                pe.wait_ge(bank_free, fills)

            def out_tile(st, n, t, hi, lo, chunks, target, done):
                g = FIRST_GROUP[st] + n
                if t == 0:
                    pe.wait_ge(lo_done, g + 1)
                for kk in range(2):
                    k = 2 * n + kk
                    for half in range(2):
                        i = product(target(t, half), hi, lo, k, t, g % RING, 2 * kk + half, k == 0, k == chunks - 1)
                if n == chunks // 2 - 1:
                    i.then_inc(*done(t))
                elif t == 1:
                    i.then_inc(group_used, 1)

            def acc_target(t, half):
                return acc[:, t, half]

            def out_stage(st, hi, lo, chunks, wait_chunk=lambda n: None):
                n_acc = FIRST_ACC[st]
                groups = chunks // 2
                for t in range(T):
                    wait_acc_free(pe, t, n_acc)
                for n in range(groups - 2):
                    wait_chunk(n)
                    for t in range(T):
                        out_tile(st, n, t, hi, lo, chunks, acc_target, lambda t: (acc_full[t], 1))
                for n in range(groups - 2, groups):
                    wait_chunk(n)
                for t in range(T):
                    for n in range(groups - 2, groups):
                        out_tile(st, n, t, hi, lo, chunks, acc_target, lambda t: (acc_full[t], 1))

            def norm_transposes(n):
                def run(t):
                    for h in range(2):
                        pe.wait_ge(xn_ready, 4 * n + 2 * t + h + 1)
                        if FIRST_FILL[f"t{n}"]:
                            pe.wait_ge(bank_free, FIRST_FILL[f"t{n}"])
                        for c in range(4):
                            i = m.transpose(aux[:, 2 * t + h, c * P:(c + 1) * P],
                                            tmp[:, t, (4 * h + c) * P:(4 * h + c + 1) * P], ident[:])
                        i.then_inc(bank_full, 1)
                return run

            def first_column(n, st):
                run = norm_transposes(n)
                for t in range(T):
                    run(t)
                    wait_operand(FIRST_FILL[f"t{n}"] + 2 * (t + 1))
                    wait_acc_free(pe, t, FIRST_ACC[st])
                    column_tile(FIRST_GROUP[st], FIRST_GROUP[st] % RING, 0, t)

            def swiglu(which, n):
                st = f"{which}_in"
                g0, c0, f0 = FIRST_GROUP[st], FIRST_ACC[st], FIRST_FILL[st]
                prods0 = ACC_ORDER[:c0].count("V")
                n_act = ACC_ORDER[:c0].count("A")
                n_dve = c0 - n_act

                def hidden_transposes(j, par):
                    for t in range(T):
                        pe.wait_ge(acc_free_dve[t], prods0 + 1 + j)
                    pe.wait_ge(bank_free, f0 if isinstance(j, int) and j < 2 else f0 - 1 + j)
                    for c in range(2):
                        for t in range(T):
                            i = m.transpose(aux[:, par, c * S + t * P:c * S + (t + 1) * P],
                                            prod[:, par, t, c * P:(c + 1) * P], ident[:])
                    i.then_inc(bank_full, 1)

                def column(j, par):
                    for t in range(T):
                        pe.wait_ge(acc_free_dve[t], n_dve - 1 + j)
                        column_tile(g0 + 2 * j, (g0 + 2 * par) % RING, par, t)
                        if t == 0:
                            hidden_transposes(j - 1, 1 - par)

                first_column(n, st)
                column(1, 1)
                with pe.Fori(1, 5) as i:
                    for b in range(2):
                        column(i * 2 + b, b)
                column(10, 0)
                hidden_transposes(10, 0)

                def wait_chunk(g):
                    pe.wait_ge(bank_free, f0 + g + 1)

                out_stage(f"{which}_out", hT_hi, hT_lo, FF // P, wait_chunk)

            pe.wait_ge(consts_in, 16 * 9)
            swiglu("f1", 0)

            g0, c0 = FIRST_GROUP["mix_in"], FIRST_ACC["mix_in"]
            fill = [FIRST_FILL["nq"]]

            def transposes(bank, source, n_free):
                pe.wait_ge(bank_free, n_free)
                for c in range(4):
                    i = m.transpose(aux[:, bank, c * P:(c + 1) * P], source[:, c * P:(c + 1) * P], ident[:])
                i.then_inc(bank_full, 1)

            def scores(s):
                t, h = s // NH, s % NH
                if s:
                    pe.wait_ge(s_reduced, s)
                else:
                    pe.wait_ge(bank_free, FIRST_FILL["nk"] + 2)
                m.matmul(aux[:, 1, 0:S], nqT[h % 2][:, h // 2, t * P:(t + 1) * P], nkT[:, h // 2, :],
                         start=True, stop=True).then_inc(s_full, 1)

            def prob_transposes(s):
                pe.wait_ge(p_ready, s + 1)
                if s:
                    pe.wait_ge(pT_copied, s)
                for k in range(T):
                    i = m.transpose(aux[:, 2, k * P:(k + 1) * P], prob[:, s % 2, k * P:(k + 1) * P], ident[:])
                i.then_inc(pT_full, 1)

            def attend(s):
                pe.wait_ge(pT_copied, s + 1)
                if s:
                    pe.wait_ge(o_taken, s)
                h = s % NH
                for k in range(T):
                    i = m.matmul(aux[:, 3, 0:ND], probT[:, s % 2, k, :], nv[:, k, h * ND:(h + 1) * ND],
                                 start=k == 0, stop=k == T - 1)
                i.then_inc(o_full, 1)

            def extras(slot):
                if slot == 2:
                    for t in range(T):
                        pe.wait_ge(acc_free_act[t], 1)
                        transposes(t, stage[:, t], FIRST_FILL["nq"])
                if slot == 4:
                    for t in range(T):
                        pe.wait_ge(acc_free_act[t], 2)
                        transposes(t, stage[:, t], FIRST_FILL["nk"])
                if 8 <= slot < 12:
                    t = slot % 2
                    n = slot - 8
                    pe.wait_ge(rot_done, n + 1)
                    transposes(0, stage[:, t], FIRST_FILL["rq"] + n)
                if 12 <= slot < 16:
                    h = slot - 12
                    pe.wait_ge(bank_free, FIRST_FILL["rs"] + h)
                    for k in range(T):
                        i = m.matmul(aux[:, 0, k * S:(k + 1) * S], rkT[:, h, k * P:(k + 1) * P], rqT[:, h, :],
                                     start=True, stop=True)
                    i.then_inc(bank_full, 1)
                if 18 <= slot < 22:
                    h = slot - 18
                    pe.wait_ge(bank_free, FIRST_FILL["rp"] + h)
                    if h == 0:
                        for t in range(T):
                            pe.wait_ge(acc_free_act[t], ACC_ORDER[:c0 + 7].count("A"))
                    for t in range(T):
                        for k in range(T):
                            i = m.matmul(aux[:, 0, t * RV:(t + 1) * RV], decay[:, h, k, t * P:(t + 1) * P],
                                         rv[:, k, h * RV:(h + 1) * RV], start=k == 0, stop=k == T - 1)
                    i.then_inc(bank_full, 1)
                s = slot - 6
                if 0 <= s < 16:
                    scores(s)
                if 0 <= s - 1 < 16:
                    prob_transposes(s - 1)
                if 0 <= s - 2 < 16:
                    attend(s - 2)
                if slot == 24:
                    pe.wait_ge(o_taken, 16)
                    for t in range(T):
                        transposes(1 + t, y_na[:, t], FIRST_FILL["yna"])
                if slot in (24, 25):
                    t = slot - 24
                    pe.wait_ge(y_ret_ready, t + 1)
                    for h in range(2):
                        transposes(0 if h == 0 else 3, y_ret[:, t, h * 512:(h + 1) * 512],
                                   FIRST_FILL["yret"] + 2 * t if t else FIRST_FILL["yna"])

            for c in range(13):
                if c == 0:
                    first_column(1, "mix_in")
                    continue
                for t in range(T):
                    wait_acc_free(pe, t, c0 + c - 1)
                    column_tile(g0 + 2 * c, (g0 + 2 * c) % RING, c % 2, t)
                    extras(2 * c + t)

            for t in range(T):
                wait_acc_free(pe, t, FIRST_ACC["na_out"])
                if t == 0:
                    pe.wait_ge(bank_free, FIRST_FILL["yret"] + 4)
                for n in range(2):
                    out_tile("na_out", n, t, ynaT_hi, ynaT_lo, NH // 2, acc_target, lambda t: (acc_full[t], 1))

            def aux_target(t, half):
                return aux[:, 2 * t + half]

            for n, t in ((0, 0), (0, 1), (1, 0), (1, 1), (2, 0), (3, 0), (2, 1), (3, 1)):
                out_tile("ret_out", n, t, yretT_hi, yretT_lo, KD, aux_target, lambda t: (ret_acc_full, 1))

            def merged_transposes(t):
                for h in range(2):
                    pe.wait_ge(merged_ready, 2 * t + h + 1)
                    bank = 2 * t + h
                    for c in range(4):
                        i = m.transpose(aux[:, bank, c * P:(c + 1) * P],
                                        m_ret[:, t, (4 * h + c) * P:(4 * h + c + 1) * P], ident[:])
                    i.then_inc(bank_full, 1)
                pe.wait_ge(bank_free, FIRST_FILL["merged"] + 2 * (t + 1))

            for t in range(T):
                merged_transposes(t)
                wait_acc_free(pe, t, FIRST_ACC["mix_out"])
                for n in range(2):
                    out_tile("mix_out", n, t, xT_hi, xT_lo, KD, acc_target, lambda t: (acc_full[t], 1))
            for t in range(T):
                for n in range(2, 4):
                    out_tile("mix_out", n, t, xT_hi, xT_lo, KD, acc_target, lambda t: (acc_full[t], 1))

            swiglu("f2", 2)

            g0, c0, f0 = FIRST_GROUP["a_in"], FIRST_ACC["a_in"], FIRST_FILL["a_in"]

            def pair_transposes(c, banks):
                for k in range(2):
                    f = 2 * c + k
                    pe.wait_ge(bank_free, f0 + max(0, f - 1) if f < 8 else f0 + 6 if f < 10 else f0 + f - 3)
                    for j in range(2):
                        for t in range(T):
                            col = (2 * k + j) * P
                            i = m.transpose(aux[:, banks[k], j * S + t * P:j * S + (t + 1) * P],
                                            a_stage[:, t, col:col + P], ident[:])
                    i.then_inc(bank_full, 1)

            def lru_gates(ch):
                pe.wait_ge(bank_free, f0 + ch // 2 + 1)
                if ch >= 2:
                    pe.wait_ge(g_taken, ch - 1)
                if ch == 0:
                    pe.wait_ge(gate_w_in_s, 16)
                for k in range(2):
                    i = m.matmul(aux[:, 2 + ch % 2, k * S:(k + 1) * S], gate_w[:, ch, k], u[:, ch], start=True, stop=True)
                i.then_inc(g_full, 1)

            def a_extras(c, t):
                if t == 0 and 2 <= c <= 4:
                    lru_gates(4 * c - 6)
                    lru_gates(4 * c - 5)
                if t == 0 and c >= 1:
                    for tt in range(T):
                        wait_acc_free(pe, tt, c0 + c)
                    if c == 5:
                        pe.wait_ge(g_taken, CH)
                    pair_transposes(c - 1, (2, 3) if c == 5 else (0, 1))
                if t == 1 and 1 <= c <= 3:
                    lru_gates(4 * c - 4)
                    lru_gates(4 * c - 3)

            first_column(3, "a_in")
            for c in range(1, 6):
                for t in range(T):
                    wait_acc_free(pe, t, c0 + c - 1)
                    column_tile(g0 + 2 * c, (g0 + 2 * c) % RING, c % 2, t)
                    a_extras(c, t)
            for t in range(T):
                wait_acc_free(pe, t, c0 + 6)
            pair_transposes(5, (0, 1))
            out_stage("a_out", yT_hi, yT_lo, CH, lambda n: pe.wait_ge(bank_free, f0 + 6 + n + 1))

            g0, c0, f0 = FIRST_GROUP["b_in"], FIRST_ACC["b_in"], FIRST_FILL["b_in"]
            n_dve = ACC_ORDER[:c0].count("V")

            def b_transposes(j, par):
                for t in range(T):
                    pe.wait_ge(acc_free_dve[t], n_dve + 1 + j)
                if isinstance(j, int) and j < 2:
                    pe.wait_ge(bank_free, f0)
                else:
                    pe.wait_ge(b_y_ready, j - 1)
                for k in range(2):
                    for t in range(T):
                        i = m.transpose(aux[:, par, k * S + t * P:k * S + (t + 1) * P],
                                        b_prod[:, par, t, k * P:(k + 1) * P], ident[:])
                i.then_inc(bank_full, 1)

            def b_column(j, par):
                for t in range(T):
                    pe.wait_ge(acc_free_dve[t], n_dve - 1 + j)
                    column_tile(g0 + 2 * j, (g0 + 2 * par) % RING, par, t)
                    if t == 0:
                        b_transposes(j - 1, 1 - par)

            first_column(4, "b_in")
            b_column(1, 1)
            with pe.Fori(1, 6) as i:
                for b in range(2):
                    b_column(i * 2 + b, b)
            b_transposes(11, 1)
            out_stage("b_out", yT_hi, yT_lo, CH, lambda n: pe.wait_ge(bank_free, f0 + 2 * n + 2))


def _stream(inputs):
    def columns(w, order):
        w = w.reshape(KD, P, -1)[:, :, order]
        w = w.reshape(2, 4, P, order.shape[0], UNIT).transpose(3, 0, 2, 1, 4)
        return w.reshape(-1, P, GROUP)

    def rows(w):
        return w.reshape(-1, 2, P, DM).transpose(0, 2, 1, 3).reshape(-1, P, GROUP)

    def blocks(parts, width, at):
        each = at[1] // width
        return np.array([[p * at[1] + b * width + i for p in parts for i in range(width)] for b in range(each)])

    ff = blocks((0, 1), 256, (0, FF))
    mix_starts = {"rq": 0, "rk": 512, "rv": 1024, "rg": 2048, "nq": 3072, "nk": 3584, "nv": 4096,
                  "gr": 4608, "gn": 5632}
    mix = np.array([np.arange(mix_starts[n] + 512 * c, mix_starts[n] + 512 * (c + 1))
                    for n, c in (("nq", 0), ("nk", 0), ("nv", 0), ("rq", 0), ("rk", 0), ("rv", 0), ("rv", 1),
                                 ("rg", 0), ("rg", 1), ("gr", 0), ("gr", 1), ("gn", 0), ("gn", 1))])
    a_cols = np.array([np.arange(W2 + 512 * c, W2 + 512 * (c + 1)) for c in range(3)]
                      + [np.arange(512 * c, 512 * (c + 1)) for c in range(3)])
    b_cols = blocks((0, 1, 3, 2), P, (0, W2))
    a = {k: np.asarray(v) for k, v in inputs.items()}
    return np.concatenate([
        columns(a["ffn1_w_in"][0], ff), rows(a["ffn1_w_out"][0]), columns(a["w_mix_in"][0], mix),
        rows(a["w_na_out"][0]), rows(a["w_ret_out"][0]), rows(a["w_mix_out"][0]),
        columns(a["ffn2_w_in"][0], ff), rows(a["ffn2_w_out"][0]), columns(a["a_w_in_2"][0], a_cols),
        rows(a["a_w_out_2"][0]), columns(a["b_w_in_2"][0], b_cols), rows(a["b_w_out_2"][0])])


def _bias_windows(rel):
    rows = rel[:, REL_R // 2 - (GR - 1):REL_R // 2 + GR]
    padded = np.pad(rows, ((0, 0), (0, 0), (GW - 1 - REL_C // 2, GW - 1 - REL_C // 2)))
    return np.stack([padded[:, :, GW - 1 - c:2 * GW - 1 - c] for c in range(GW)])


def _by_chunk(v):
    v = np.asarray(v)
    return np.moveaxis(v.reshape(v.shape[:-1] + (CH, P)), (-1, -2), (0, 1))


def kernel(**inputs):
    import concourse.bacc as bacc
    from concourse.bass_utils import run_bass_kernel_spmd

    f = np.float32
    inv = (f(1.0) / (f(10000.0) ** np.linspace(0.0, 1.0, 64, dtype=f))).astype(f)
    angle = np.arange(S, dtype=f)[:, None] * inv[None, :]
    rot = np.stack([np.cos(angle), np.sin(angle), -np.sin(angle)], axis=1).astype(f)
    rot = rot.reshape(T, P, 3, 64).transpose(1, 0, 2, 3)
    col = np.arange(P) % GW
    start = np.clip(col - WIN // 2, 0, GW - WIN)[:, None]
    key = np.arange(GW)[None, :]
    colmask = np.where((key >= start) & (key < start + WIN), f(0), f(-BIG)).astype(f)
    diff = (np.arange(S)[None, :] - np.arange(S)[:, None]).astype(f)
    dist = np.stack([np.maximum(diff, 0), np.maximum(-diff, 0)]).reshape(2, T, P, S).transpose(2, 0, 1, 3)

    a = {k: np.asarray(v) for k, v in inputs.items()}
    arrays = {
        "weights": _stream(inputs),
        "x_in": a["x"][0],
        "gains": np.concatenate([a["ffn1_pre_norm"], a["ffn1_post_norm"], a["mix_pre_norm"], a["mix_post_norm"],
                                 a["ffn2_pre_norm"], a["ffn2_post_norm"], a["norm_g_2"], a["final_g_2"][None]]),
        "ident_in": np.eye(P, dtype=f),
        "rot_in": rot,
        "colmask_in": colmask,
        "dist_in": dist,
        "decay_in": np.concatenate([a["ret_decay_fwd"], a["ret_decay_bwd"]], axis=1),
        "lam_in": _by_chunk(a["a_lambda_2"][0]),
        "bias_in": _bias_windows(a["na_rel_bias"][0]),
        "gate_w_in": a["a_gate_w_2"][0].reshape(CH, P, 2, P).transpose(1, 0, 2, 3),
        "gate_b_in": a["a_gate_b_2"][0].reshape(CH, 2, P).transpose(2, 0, 1),
        "conv_a_in": _by_chunk(a["a_conv_w_2"][0]),
        "conv_ab_in": _by_chunk(a["a_conv_b_2"][0]),
        "conv_b_in": _by_chunk(a["b_conv_w_2"][0]),
    }
    nc = bacc.Bacc("TRN2", target_bir_lowering=False, num_devices=1)
    args = {}
    for name, value in arrays.items():
        arrays[name] = np.ascontiguousarray(value)
        args[name] = nc.dram_tensor(name, arrays[name].shape, F32, kind="ExternalInput").ap()
    args["out"] = nc.dram_tensor("out", (S, DM), F32, kind="ExternalOutput").ap()
    build(nc, **args)
    result = run_bass_kernel_spmd(nc, [arrays], core_ids=[0])
    return np.asarray(result.results[0]["out"]).reshape(1, S, DM)
```

```python
from contextlib import ExitStack

import numpy as np

import concourse.bass as bass
from concourse import mybir

F32 = mybir.dt.float32
F32R = mybir.dt.float32r
ALU = mybir.AluOpType
ACT = mybir.ActivationFunctionType

P = 128
S = 256
T = S // P
DM = 1024
KD = DM // P
FF = 2816
W2 = 1536
CH = W2 // P
RH, RQ, RV = 4, 128, 256
NH, ND = 8, 64
GW, GR = 64, S // 64
WIN = 16
REL_R, REL_C = 15, 31
EPS = 1e-6
BIG = 1e30
UNIT = 512
GROUP = 4 * UNIT
RING = 4

STAGES = [("f1_in", 22), ("f1_out", 11), ("mix_in", 26), ("na_out", 2), ("ret_out", 4), ("mix_out", 4),
          ("f2_in", 22), ("f2_out", 11), ("a_in", 12), ("a_out", 6), ("b_in", 24), ("b_out", 6)]
NG = sum(n for _, n in STAGES)
FIRST_GROUP = {name: sum(n for _, n in STAGES[:i]) for i, (name, _) in enumerate(STAGES)}
GROUPS = dict(STAGES)

ACC_READERS = {"f1_in": "V" * 11, "f1_out": "V", "mix_in": "AAAVVAAVVAAAA", "na_out": "V", "mix_out": "V",
               "f2_in": "V" * 11, "f2_out": "V", "a_in": "AAAVVV", "a_out": "V", "b_in": "V" * 12, "b_out": "V"}
ACC_ORDER = "".join(ACC_READERS.values())
FIRST_ACC = {}
for _name in ACC_READERS:
    FIRST_ACC[_name] = sum(len(v) for k, v in ACC_READERS.items() if k in FIRST_ACC)

FILL_COUNTS = [("t0", 4), ("f1_in", 11), ("t1", 4), ("nq", 2), ("nk", 2), ("rq", 2), ("rk", 2), ("rs", 4), ("rp", 4),
               ("yna", 2), ("yret", 4), ("merged", 4), ("t2", 4), ("f2_in", 11), ("t3", 4),
               ("a_in", 12), ("t4", 4), ("b_in", 12)]
FIRST_FILL = {name: sum(n for _, n in FILL_COUNTS[:i]) for i, (name, _) in enumerate(FILL_COUNTS)}
SPLIT_COUNTS = [("t0", 4), ("f1_in", 11), ("t1", 4), ("yna", 2), ("yret", 4), ("merged", 4), ("t2", 4),
                ("f2_in", 11), ("t3", 4), ("gate", 6), ("t4", 4), ("b_in", 12)]
FIRST_SPLIT = {name: sum(n for _, n in SPLIT_COUNTS[:i]) for i, (name, _) in enumerate(SPLIT_COUNTS)}

RELEASE = []
for _name, _n in STAGES:
    for _g in range(_n):
        if _name.endswith("_in") and _g % 2 or _name.endswith("_out") and _g == _n - 1:
            if _name == "ret_out":
                RELEASE.append(("ret", T))
            else:
                RELEASE.append(("acc", FIRST_ACC[_name] + (_g // 2 if _name.endswith("_in") else 0) + 1))
        else:
            RELEASE.append(("used", 1 + sum(kind == "used" for kind, _ in RELEASE)))

NORMS = [(0, False, 0.0, None), (1, True, 0.5, "f1_out"), (2, True, 1.0, "mix_out"), (3, True, 0.5, "f2_out"),
         (4, False, 1.0, "a_out"), (5, False, 1.0, "b_out")]


NEXT_GROUP = [FIRST_GROUP[name] for name in ("f1_in", "mix_in", "f2_in", "a_in", "b_in")] + [NG]


class Chain:

    def __init__(self, engine, semaphore):
        self.engine, self.semaphore, self.base, self.n = engine, semaphore, 0, 0

    def __call__(self, instruction):
        instruction.then_inc(self.semaphore, 1)
        self.n += 1
        self.engine.wait_ge(self.semaphore, self.base + self.n)


def build(nc, weights, x_in, gains, ident_in, rot_in, colmask_in, dist_in, decay_in, lam_in, bias_in, gate_w_in,
          gate_b_in, conv_a_in, conv_ab_in, conv_b_in, out):
    with ExitStack() as ctx:
        base = nc.sbuf_base + (-nc.sbuf_base) % 32
        cursor = [base]

        def at(name, shape, dt, offset):
            return nc.alloc_sbuf_tensor_at(name, shape, dt, offset=offset)

        def sb(name, shape, dt=F32):
            size = 4 * int(np.prod(shape[1:]))
            size += -size % 32
            tensor = at(name, shape, dt, cursor[0])
            cursor[0] += size
            return tensor

        def sem(name):
            return ctx.enter_context(nc.semaphore(name))

        raw = sb("raw", [P, RING, GROUP])
        w_hi = sb("w_hi", [P, RING, GROUP], F32R)
        w_lo = sb("w_lo", [P, RING, GROUP], F32R)
        xT_hi = sb("xT_hi", [P, KD, S], F32R)
        xT_lo = sb("xT_lo", [P, KD, S], F32R)
        x = sb("x", [P, T, DM])
        gain_post = sb("gain_post", [P, DM])
        gain_pre = sb("gain_pre", [P, DM])
        ident = sb("ident", [P, P])
        rot = sb("rot", [P, T, 3, 64])
        colmask = sb("colmask", [P, GW])
        conv_a = sb("conv_a", [P, CH, 4])
        conv_ab = sb("conv_ab", [P, CH])
        conv_b = sb("conv_b", [P, CH, 3])
        gate_b = sb("gate_b", [P, CH, 2])
        logit = sb("logit", [P, 2 * RH + CH])
        ls = [sb(f"ls{i}", [P, 2 * RH + CH]) for i in range(5)]
        lrate = sb("lrate", [P, 2, CH])
        eps1 = sb("eps1", [P, 1])
        eps4 = sb("eps4", [P, 1])
        zero = sb("zero", [P, 1])
        sumsq = sb("sumsq", [P, 4])
        std = sb("std", [P, 4])
        rstd = sb("rstd", [P, 4])
        ret_sumsq = sb("ret_sumsq", [P, T, RH])
        ret_std = sb("ret_std", [P, T, RH])
        ret_rstd = sb("ret_rstd", [P, T, RH])
        neg_max = sb("neg_max", [P, T * NH])
        prob_sum = sb("prob_sum", [P, T * NH])
        prob_rec = sb("prob_rec", [P, T * NH])

        area = cursor[0]
        temp_at = nc.sbuf_usable_end - 4 * T * DM - 64
        temp_at = temp_at() if callable(temp_at) else temp_at
        temp_at -= temp_at % 32
        assert temp_at - area >= 67584, temp_at - area
        tmp = at("tmp", [P, T, DM], F32, temp_at)
        hT_hi = at("hT_hi", [P, FF // P, S], F32R, area)
        hT_lo = at("hT_lo", [P, FF // P, S], F32R, area + 22528)
        silu_g = at("silu_g", [P, T, 256], F32, area + 45056)
        prod = at("prod", [P, 2, T, 256], F32, area + 47104)
        nqT = [at(f"nqT{i}", [P, NH // 2, S], F32, area + 4096 * i) for i in range(2)]
        nkT = at("nkT", [P, NH // 2, S], F32, area + 8192)
        nv = at("nv", [P, T, NH * ND], F32, area + 12288)
        yretT_hi = at("yretT_hi", [P, KD, S], F32R, area)
        yretT_lo = at("yretT_lo", [P, KD, S], F32R, area + 8192)
        rqT = at("rqT", [P, RH, S], F32, area + 16384)
        rkT = at("rkT", [P, RH, S], F32, area + 20480)
        m_ret = at("m_ret", [P, T, DM], F32, area + 16384)
        rv = at("rv", [P, T, RH * RV], F32, area + 24576)
        ynaT_hi = at("ynaT_hi", [P, NH // 2, S], F32R, area + 24576)
        ynaT_lo = at("ynaT_lo", [P, NH // 2, S], F32R, area + 28672)
        decay = at("decay", [P, RH, T, S], F32, area + 32768)
        m_na = at("m_na", [P, T, DM], F32, area + 32768)
        y_ret = at("y_ret", [P, T, RH * RV], F32, area + 40960)
        y_na = at("y_na", [P, T, NH * ND], F32, area + 49152)
        stage = at("stage", [P, T, 512], F32, area + 53248)
        rot_b = at("rot_b", [P, T, 512], F32, area + 57344)
        dist = at("dist", [P, 2, T, S], F32, temp_at + 4096)
        bias_raw = at("bias_raw", [P, 2, GR, GW], F32, area + 61440)
        bias_m = at("bias_m", [P, 2, GR, GW], F32, area + 63488)
        neg_s = at("neg_s", [P, 2, S], F32, area + 65536)
        prob = at("prob", [P, 2, S], F32, temp_at)
        probT = at("probT", [P, 2, T, P], F32, temp_at + 2048)
        u = at("u", [P, CH, S], F32, area)
        ri = at("ri", [P, CH, 2, S], F32, area + 12288)
        av = at("av", [P, CH, S], F32, area + 36864)
        gate_w = at("gate_w", [P, CH, 2, P], F32, area + 51200)
        a_stage = at("a_stage", [P, T, 512], F32, area + 63488)
        yg = at("yg", [P, 2, 512], F32, temp_at)
        yT_hi = at("yT_hi", [P, CH, S], F32R, area + 51200)
        yT_lo = at("yT_lo", [P, CH, S], F32R, area + 12288)
        b_gate = at("b_gate", [P, T, 256], F32, area)
        b_prod = at("b_prod", [P, 2, T, 256], F32, area + 2048)
        b_conv = at("b_conv", [P, S], F32, area + 6144)
        b_y = at("b_y", [P, 2, S], F32, area + 7168)

        acc = ctx.enter_context(nc.psum_tensor("acc", [P, T, 2, UNIT], F32))
        aux = ctx.enter_context(nc.psum_tensor("aux", [P, 4, UNIT], F32))

        landed = [sem(f"landed{i}") for i in range(RING)]
        hi_done = sem("hi_done")
        lo_done = sem("lo_done")
        group_used = sem("group_used")
        acc_full = [sem(f"acc_full{t}") for t in range(T)]
        acc_free_act = [sem(f"acc_free_act{t}") for t in range(T)]
        acc_free_dve = [sem(f"acc_free_dve{t}") for t in range(T)]
        gate_ready = [sem(f"gate_ready{t}") for t in range(T)]
        bank_full = sem("bank_full")
        bank_hi = sem("bank_hi")
        bank_free = sem("bank_free")
        consts_in = sem("consts_in")
        x_landed = [sem(f"x_landed{t}") for t in range(T)]
        ident_landed = sem("ident_landed")
        gain0_landed = sem("gain0_landed")
        gains_in = sem("gains_in")
        post_std = sem("post_std")
        pre_std = sem("pre_std")
        x_ready = sem("x_ready")
        xn_ready = sem("xn_ready")
        act_step = sem("act_step")
        dve_step = sem("dve_step")
        pool_step = sem("pool_step")
        eps_set = sem("eps_set")
        ls_neg = sem("ls_neg")
        ls_exp = sem("ls_exp")
        decay_arg = sem("decay_arg")
        decay_done = sem("decay_done")
        dist_in_s = sem("dist_in_s")
        bias_in_s = [sem(f"bias_in{i}") for i in range(2)]
        bias_ready = sem("bias_ready")
        pad_set = sem("pad_set")
        rot_done = sem("rot_done")
        s_full = sem("s_full")
        s_reduced = sem("s_reduced")
        p_ready = sem("p_ready")
        pT_full = sem("pT_full")
        pT_copied = sem("pT_copied")
        o_full = sem("o_full")
        o_taken = sem("o_taken")
        ret_sq = sem("ret_sq")
        ret_std_s = sem("ret_std_s")
        y_ret_ready = sem("y_ret_ready")
        ret_acc_full = sem("ret_acc_full")
        merged_ready = sem("merged_ready")
        gate_w_in_s = sem("gate_w_in_s")
        conv_head = sem("conv_head")
        g_full = sem("g_full")
        g_taken = sem("g_taken")
        iu_ready = sem("iu_ready")
        et_ready = sem("et_ready")
        v_ready = sem("v_ready")
        mult_ready = sem("mult_ready")
        yg_ready = sem("yg_ready")
        b_y_ready = sem("b_y_ready")
        stored = sem("stored")

        def wait_acc_free(pe, t, n):
            a = ACC_ORDER[:n].count("A")
            v = n - a
            if a:
                pe.wait_ge(acc_free_act[t], a)
            if v:
                pe.wait_ge(acc_free_dve[t], v)

        def act_frees(t, instruction):
            instruction.then_inc(acc_free_act[t], 1)

        block = ctx.enter_context(nc.Block())

        @block.sync
        def _(sp):
            sp.dma_start(x[:, 0, :], x_in[0:P, :]).then_inc(x_landed[0], 16)
            for g in range(RING):
                sp.dma_start(raw[:, g, :], weights[g]).then_inc(landed[g], 16)
                if g == 1:
                    sp.dma_start(x[:, 1, :], x_in[P:2 * P, :]).then_inc(x_landed[1], 16)
            with sp.Fori(1, NG // RING) as lap:
                for s in range(RING):
                    sp.wait_ge(lo_done, lap * RING + (s + 1 - RING))
                    sp.dma_start(raw[:, s, :], weights[bass.ds(lap * RING + s, 1)].rearrange("a p n -> p (a n)"))\
                        .then_inc(landed[s], 16)
            for g in range(NG // RING * RING, NG):
                sp.wait_ge(lo_done, g + 1 - RING)
                sp.dma_start(raw[:, g % RING, :], weights[g]).then_inc(landed[g % RING], 16)
            for t in range(T):
                sp.wait_ge(xn_ready, 2 * 2 * 5 + 2 * (t + 1))
                sp.dma_start(out[t * P:(t + 1) * P, :], tmp[:, t, :]).then_inc(stored, 16)
            sp.wait_ge(stored, 16 * T)

        @block.gpsimd
        def _(pool):
            g = nc.gpsimd
            step = Chain(pool, pool_step)
            g.memset(eps1[:], EPS).then_inc(eps_set, 1)
            g.memset(eps4[:], 4 * EPS).then_inc(eps_set, 1)
            g.memset(zero[:], 0.0).then_inc(eps_set, 1)

            def load_gains(n, post, pre):
                if post is not None:
                    pool.dma_start(gain_post[:], gains[post:post + 1, :].partition_broadcast(P)).then_inc(gains_in, 16)
                pool.dma_start(gain_pre[:], gains[pre:pre + 1, :].partition_broadcast(P)).then_inc(gains_in, 16)

            for dst, src in ((colmask, colmask_in), (conv_a, conv_a_in), (conv_ab, conv_ab_in),
                             (conv_b, conv_b_in), (gate_b, gate_b_in), (rot, rot_in)):
                pool.dma_start(dst[:], src).then_inc(consts_in, 16)
            pool.dma_start(logit[:, 0:2 * RH], decay_in.partition_broadcast(P)).then_inc(consts_in, 16)
            pool.dma_start(logit[:, 2 * RH:], lam_in).then_inc(consts_in, 16)
            pool.wait_ge(xn_ready, 4)
            load_gains(1, 1, 2)

            def load_bias(s):
                t, h = s // NH, s % NH
                if s >= 2:
                    pool.wait_ge(bias_ready, s - 1)
                for r in range(2):
                    first = GR - 1 - 2 * t - r
                    pool.dma_start(bias_raw[r * GW:(r + 1) * GW, s % 2], bias_in[:, h, first:first + GR, :])\
                        .then_inc(bias_in_s[s % 2], 16)

            load_bias(0)
            load_bias(1)
            pool.wait_ge(xn_ready, 8)
            load_gains(2, 3, 4)
            pool.wait_ge(bank_full, FIRST_FILL["t1"] + 4)
            pool.dma_start(dist[:], dist_in).then_inc(dist_in_s, 16)
            g.memset(nqT[0][64:128], 0.0).then_inc(pad_set, 1)
            pool.wait_ge(pad_set, 1)
            g.memset(nqT[1][0:64], 0.0).then_inc(pad_set, 1)
            pool.wait_ge(pad_set, 2)

            def mask_bias(s):
                pool.wait_ge(bias_in_s[s % 2], 32 * (s // 2 + 1))
                if s == 0:
                    pool.wait_ge(consts_in, 16 * 8)
                if s >= 2:
                    pool.wait_ge(s_reduced, s - 1)
                g.tensor_tensor(bias_m[:, s % 2], bias_raw[:, s % 2],
                                colmask[:].unsqueeze(1).to_broadcast([P, GR, GW]), ALU.add).then_inc(bias_ready, 1)
                if s + 2 < T * NH:
                    load_bias(s + 2)

            mask_bias(0)
            mask_bias(1)
            for n in range(2 * T):
                t = n % T
                pool.wait_ge(acc_free_dve[t], ACC_ORDER[:FIRST_ACC["mix_in"] + 4 + n // T].count("V"))
                g.tensor_tensor(stage[:, t], stage[:, t], rot_b[:, t], ALU.add).then_inc(rot_done, 1)
                mask_bias(n + 2)
            for s in range(2 * T + 2, T * NH):
                mask_bias(s)
            pool.wait_ge(xn_ready, 12)
            load_gains(3, 5, 6)
            pool.wait_ge(x_ready, 2 * 2 + 1)
            pool.dma_start(gate_w[:], gate_w_in).then_inc(gate_w_in_s, 16)
            pool.wait_ge(xn_ready, 16)
            load_gains(4, None, 7)
            def input_gates(chunks):
                for ch in chunks:
                    pool.wait_ge(g_taken, ch + 1)
                    g.tensor_tensor(ri[:, ch, 1], ri[:, ch, 1], u[:, ch], ALU.mult).then_inc(iu_ready, 1)

            input_gates(range(CH))
            pool.wait_ge(xn_ready, 20)
            load_gains(5, None, 8)

        @block.scalar
        def _(act):
            a = nc.scalar
            step = Chain(act, act_step)
            split = [0]

            def round_group(g, slot=None, wait_used=True):
                slot = g % RING if slot is None else slot
                lap = g // RING if isinstance(g, int) else None
                act.wait_ge(landed[slot], 16 * (lap + 1))
                if g >= RING:
                    kind, n = RELEASE[g - RING]
                    act.wait_ge({"used": group_used, "acc": acc_full[1], "ret": ret_acc_full}[kind], n)
                a.activation(w_hi[:, slot], raw[:, slot], ACT.Copy).then_inc(hi_done, 1)

            def round_to(n):
                while split[0] < min(n, NG):
                    round_group(split[0])
                    split[0] += 1

            def round_in_loop(base_group, i, i0, b, per=4):
                slot = (base_group + b) % RING
                lap0 = (base_group + b) // RING
                act.wait_ge(landed[slot], (i * (16 * per // RING)) + (16 * (lap0 + 1) - i0 * (16 * per // RING)))
                kind, n = RELEASE[base_group + b - RING]
                act.wait_ge({"used": group_used, "acc": acc_full[1]}[kind], i * (per // 2) + (n - i0 * (per // 2)))
                a.activation(w_hi[:, slot], raw[:, slot], ACT.Copy).then_inc(hi_done, 1)

            def take_hi(stage_name, n, dst, bank, source=None, scale=1.0, per_fill=None):
                act.wait_ge(bank_full, FIRST_FILL[stage_name] + n + 1)
                a.activation(dst, source if source is not None else aux[:, bank], ACT.Copy, scale=scale)\
                    .then_inc(bank_hi, 1)

            def norm(n, post, factor, stage_name):
                def root(t, which):
                    c = which * 2 + t
                    step(a.activation(tmp[:, t], acc[:, t] if which == 0 else x[:, t], ACT.Square,
                                      accum_out=sumsq[:, c:c + 1]))
                    a.activation(std[:, c:c + 1], sumsq[:, c:c + 1], ACT.Sqrt, bias=eps1[:], scale=1.0 / DM)\
                        .then_inc(post_std if which == 0 else pre_std, 1)

                def first(t):
                    if post:
                        act.wait_ge(acc_full[t], FIRST_ACC[stage_name] + 1)
                        root(t, 0)

                def second(t):
                    if post:
                        act.wait_ge(x_ready, 2 * (n - 1) + t + 1)
                    elif n:
                        act.wait_ge(acc_free_dve[t], ACC_ORDER[:FIRST_ACC[stage_name] + 1].count("V"))
                    else:
                        act.wait_ge(x_landed[t], 16)
                        act.wait_ge(eps_set, 3)
                    root(t, 1)

                def parts(t):
                    if n == 5:
                        return
                    for h in range(2):
                        take_hi(f"t{n}", 2 * t + h, xT_hi[:, 4 * h:4 * h + 4, t * P:(t + 1) * P], 2 * t + h,
                                source=aux[:, 2 * t + h].rearrange("p (c q) -> p c q", c=4))

                after = NEXT_GROUP[n]
                first(0)
                round_to(after + 1)
                second(0)
                if n:
                    round_to(after + 2)
                parts(0)
                round_to(after + 3)
                first(1)
                if n:
                    round_to(after + 4)
                second(1)
                if not n:
                    round_to(after + 4)
                parts(1)

            act.dma_start(gain_pre[:], gains[0:1, :].partition_broadcast(P)).then_inc(gain0_landed, 16)
            act.dma_start(ident[:], ident_in).then_inc(ident_landed, 16)
            norm(*NORMS[0])
            act.wait_ge(ls_neg, 1)
            a.activation(ls[1][:], ls[0][:], ACT.Exp).then_inc(ls_exp, 1)

            def swiglu(which, normed):
                st = f"{which}_in"
                g0, c0, f0 = FIRST_GROUP[st], FIRST_ACC[st], FIRST_FILL[st]
                prods0 = ACC_ORDER[:c0].count("V")

                def silu(j, par, t):
                    act.wait_ge(acc_full[t], c0 + 1 + j)
                    if not (isinstance(j, int) and j == 0 and prods0 == 0):
                        act.wait_ge(acc_free_dve[t], prods0 + j)
                    a.activation(silu_g[:, t], acc[:, t, par, 0:256], ACT.Silu).then_inc(gate_ready[t], 1)

                def hidden_hi(j, par):
                    act.wait_ge(bank_full, f0 + 1 + j)
                    dst = hT_hi[:, bass.ds(2 * j, 2), :] if not isinstance(j, int) else hT_hi[:, 2 * j:2 * j + 2, :]
                    a.activation(dst, aux[:, par].rearrange("p (c q) -> p c q", c=2), ACT.Copy).then_inc(bank_hi, 1)

                def column(j, par, rounds):
                    rounds()
                    silu(j, par, 0)
                    if not (isinstance(j, int) and j == 0):
                        hidden_hi(j - 1, 1 - par)
                    silu(j, par, 1)

                silu(0, 0, 0)
                silu(1, 1, 0)
                round_to(g0 + 5)
                silu(0, 0, 1)
                round_to(g0 + 6)
                silu(1, 1, 1)
                hidden_hi(0, 0)
                with act.Fori(1, 5) as i:
                    for b in range(2):
                        column(i * 2 + b, b, lambda: [round_in_loop(g0 + 6, i, 1, 2 * b + h) for h in range(2)])
                split[0] += 16
                column(10, 0, lambda: round_to(g0 + 24))
                round_to(g0 + 25)
                hidden_hi(10, 0)
                g1, n1 = FIRST_GROUP[f"{which}_out"], GROUPS[f"{which}_out"]
                round_to(g1 + n1 + 1)

            swiglu("f1", 0)
            norm(*NORMS[1])

            g0, c0 = FIRST_GROUP["mix_in"], FIRST_ACC["mix_in"]
            gates = [11, 11]

            def exp_step(s):
                act.wait_ge(s_reduced, s + 1)
                if s >= 2:
                    act.wait_ge(pT_full, s - 1)
                a.activation(prob[:, s % 2], neg_s[:, s % 2], ACT.Exp, bias=neg_max[:, s:s + 1], scale=-1.0,
                             accum_out=prob_sum[:, s:s + 1]).then_inc(p_ready, 1)

            def ret_squares(h):
                act.wait_ge(bank_full, FIRST_FILL["rp"] + h + 1)
                for t in range(T):
                    i = a.activation(rot_b[:, t, 0:RV], aux[:, 0, t * RV:(t + 1) * RV], ACT.Square,
                                     accum_out=ret_sumsq[:, t, h:h + 1])
                    if t == 0:
                        step(i)
                    else:
                        i.then_inc(ret_sq, 1)
                act.wait_ge(ret_sq, h + 1)

            for c in range(13):
                for t in range(T):
                    par = c % 2
                    slot = 2 * c + t
                    round_to(g0 + 2 * c + 4 + t)
                    if 2 <= slot < 2 + RH:
                        h = slot - 2
                        act.wait_ge(decay_arg, h + 1)
                        a.activation(decay[:, h], decay[:, h], ACT.Exp).then_inc(decay_done, 1)
                    source = acc[:, t, par]
                    act.wait_ge(acc_full[t], c0 + c + 1)
                    if c < 2:
                        if c:
                            act.wait_ge(bank_full, FIRST_FILL["nq"] + t + 1)
                        i = a.activation(stage[:, t], source, ACT.Copy, scale=ND ** -0.5 if c == 0 else 1.0)
                        act_frees(t, i)
                    elif c == 2:
                        act_frees(t, a.activation(nv[:, t], source, ACT.Copy))
                    elif c in (5, 6):
                        act_frees(t, a.activation(rv[:, t, (c - 5) * 512:(c - 4) * 512], source, ACT.Copy))
                    elif c in (7, 8):
                        i = a.activation(y_ret[:, t, (c - 7) * 512:(c - 6) * 512], source, ACT.Tanh, scale=0.5)
                        i.then_inc(gate_ready[t], 1)
                    elif c >= 9:
                        dst, col = (m_ret, c - 9) if c < 11 else (m_na, c - 11)
                        act_frees(t, a.activation(dst[:, t, col * 512:(col + 1) * 512], source, ACT.Tanh, scale=0.5))
                    if 6 <= slot < 6 + 16:
                        exp_step(slot - 6)
                    if 18 <= slot < 22:
                        ret_squares(slot - 18)
                    if slot == 22:
                        a.activation(ret_std[:], ret_sumsq[:], ACT.Sqrt, bias=eps4[:], scale=4.0 / RV)\
                            .then_inc(ret_std_s, 1)
                    if slot == 24:
                        for tt in range(T):
                            take_hi("yna", tt, ynaT_hi[:, :, tt * P:(tt + 1) * P], 1 + tt,
                                    source=aux[:, 1 + tt].rearrange("p (c q) -> p c q", c=4))
                    if slot in (24, 25):
                        tt = slot - 24
                        for h in range(2):
                            bank = 0 if h == 0 else 3
                            take_hi("yret", 2 * tt + h, yretT_hi[:, 4 * h:4 * h + 4, tt * P:(tt + 1) * P], bank,
                                    source=aux[:, bank].rearrange("p (c q) -> p c q", c=4))
            round_to(FIRST_GROUP["ret_out"] + 4)
            for t in range(T):
                for h in range(2):
                    take_hi("merged", 2 * t + h, xT_hi[:, 4 * h:4 * h + 4, t * P:(t + 1) * P], 2 * t + h,
                            source=aux[:, 2 * t + h].rearrange("p (c q) -> p c q", c=4), scale=0.5)
                if t == 0:
                    round_to(FIRST_GROUP["mix_out"] + 4)
            norm(*NORMS[2])

            swiglu("f2", 0)
            norm(*NORMS[3])

            g0, c0, f0 = FIRST_GROUP["a_in"], FIRST_ACC["a_in"], FIRST_FILL["a_in"]

            def conv_start(f):
                act.wait_ge(bank_full, f0 + f + 1)
                for k in range(2):
                    ch = 2 * f + k
                    a.activation(u[:, ch], aux[:, f % 2, k * S:(k + 1) * S], ACT.Identity,
                                 bias=conv_ab[:, ch:ch + 1], scale=conv_a[:, ch, 3:4]).then_inc(conv_head, 1)

            def gate_sigmoids(ch):
                act.wait_ge(g_full, ch + 1)
                for k in range(2):
                    i = a.activation(ri[:, ch, k], aux[:, 2 + ch % 2, k * S:(k + 1) * S], ACT.Sigmoid,
                                     bias=gate_b[:, ch, k:k + 1])
                    if k == 1:
                        i.then_inc(g_taken, 1)

            def exp_tanh(ch):
                act.wait_ge(g_taken, ch + 1)
                a.activation(av[:, ch], ri[:, ch, 0], ACT.Exp, scale=lrate[:, 0, ch:ch + 1]).then_inc(et_ready, 1)
                a.activation(ri[:, ch, 0], ri[:, ch, 0], ACT.Tanh, scale=lrate[:, 1, ch:ch + 1]).then_inc(et_ready, 1)

            def gated_hi(n):
                act.wait_ge(yg_ready, n + 1)
                a.activation(yT_hi[:, 2 * n:2 * n + 2, :], yg[:, n % 2].rearrange("p (c q) -> p c q", c=2), ACT.Copy)\
                    .then_inc(bank_hi, 1)

            def root(m):
                act.wait_ge(v_ready, m + 1)
                a.activation(av[:, 4 * m:4 * m + 4], av[:, 4 * m:4 * m + 4], ACT.Sqrt,
                             bias=zero[:], scale=-1.0).then_inc(mult_ready, 1)

            def stage_columns(c, t):
                act.wait_ge(acc_full[t], c0 + c + 1)
                if c:
                    act.wait_ge(bank_full, f0 + 2 * c)
                if c < 3:
                    act_frees(t, a.activation(a_stage[:, t], acc[:, t, c % 2], ACT.Copy))
                else:
                    a.activation(a_stage[:, t], acc[:, t, c % 2], ACT.Tanh, scale=0.5).then_inc(gate_ready[t], 1)

            plan = {(1, 0): (None, "stage", conv_start, 0, 1),
                    (1, 1): ("stage", None),
                    (2, 0): (None, "stage", conv_start, 2, 3),
                    (2, 1): (None, gate_sigmoids, 0, 1, "stage"),
                    (3, 0): (None, gate_sigmoids, 2, 3, conv_start, 4, 5, gate_sigmoids, 4, 5, "stage"),
                    (3, 1): (gate_sigmoids, 6, 7, exp_tanh, 0, 1, 2, 3, "stage", None),
                    (4, 0): (None, gate_sigmoids, 8, 9, 10, 11, "stage", exp_tanh, 4, 5, 6, 7),
                    (4, 1): (None, "stage", exp_tanh, 8, 9, 10, 11),
                    (5, 0): ("stage", root, 0, None, root, 1, gated_hi, 0, 1),
                    (5, 1): ("stage", None, gated_hi, 2, 3)}
            for c in range(6):
                for t in range(T):
                    todo = None
                    for item in plan.get((c, t), (None, "stage")):
                        if item is None:
                            round_to(g0 + 2 * c + 4 + t)
                        elif item == "stage":
                            stage_columns(c, t)
                        elif isinstance(item, int):
                            todo(item)
                        else:
                            todo = item
            round_to(FIRST_GROUP["a_out"] + 4)
            root(2)
            for n in (4, 5):
                round_to(FIRST_GROUP["a_out"] + n + 1)
                gated_hi(n)
            round_to(FIRST_GROUP["b_in"] + 1)
            norm(*NORMS[4])

            g0, c0, f0 = FIRST_GROUP["b_in"], FIRST_ACC["b_in"], FIRST_FILL["b_in"]
            prods0 = ACC_ORDER[:c0].count("V")

            def b_gates(j, par, t):
                act.wait_ge(acc_full[t], c0 + 1 + j)
                act.wait_ge(acc_free_dve[t], prods0 + j)
                a.activation(b_gate[:, t, 0:P], acc[:, t, par, 2 * P:3 * P], ACT.Silu).then_inc(gate_ready[t], 1)
                a.activation(b_gate[:, t, P:2 * P], acc[:, t, par, 3 * P:4 * P], ACT.Copy).then_inc(gate_ready[t], 1)

            def b_hi(j, par):
                act.wait_ge(b_y_ready, 1 + j)
                dst = yT_hi[:, j, :] if isinstance(j, int) else yT_hi[:, bass.ds(j, 1), :].rearrange("p a q -> p (a q)")
                a.activation(dst, b_y[:, par], ACT.Copy).then_inc(bank_hi, 1)

            def b_column(j, par, rounds):
                rounds()
                b_gates(j, par, 0)
                if not (isinstance(j, int) and j == 0):
                    b_hi(j - 1, 1 - par)
                b_gates(j, par, 1)

            b_gates(0, 0, 0)
            b_gates(1, 1, 0)
            round_to(g0 + 5)
            b_gates(0, 0, 1)
            round_to(g0 + 6)
            b_gates(1, 1, 1)
            b_hi(0, 0)
            with act.Fori(1, 6) as i:
                for b in range(2):
                    b_column(i * 2 + b, b, lambda: [round_in_loop(g0 + 6, i, 1, 2 * b + h) for h in range(2)])

            split[0] += 20
            round_to(FIRST_GROUP["b_out"] + 3)
            b_hi(11, 1)
            round_to(NG)
            norm(*NORMS[5])

        @block.vector
        def _(dve):
            v = nc.vector
            step = Chain(dve, dve_step)
            split = [0]

            def low_group(g, slot):
                dve.wait_ge(hi_done, g + 1)
                v.tensor_tensor(w_lo[:, slot], raw[:, slot], w_hi[:, slot].bitcast(F32), ALU.subtract)\
                    .then_inc(lo_done, 1)

            def low_to(n):
                while split[0] < min(n, NG):
                    low_group(split[0], split[0] % RING)
                    split[0] += 1

            def low_in_loop(base_group, i, i0, b, per=4):
                low_group(i * per + (base_group + b - i0 * per), (base_group + b) % RING)

            def take_lo(stage_name, q, dst, hi, source, scale=None):
                dve.wait_ge(bank_hi, FIRST_SPLIT[stage_name] + q + 1)
                if scale is None:
                    i = v.tensor_tensor(dst, source, hi.bitcast(F32), ALU.subtract)
                else:
                    i = v.scalar_tensor_tensor(dst, source, scale, hi.bitcast(F32), ALU.mult, ALU.subtract)
                i.then_inc(bank_free, 1)

            def norm(n, post, factor, stage_name):
                posts = {1: 0, 2: 1, 3: 2}
                after = NEXT_GROUP[n]
                for t in range(T):
                    if n:
                        if t == 0:
                            dve.wait_ge(gains_in, (32, 64, 96, 112, 128)[n - 1])
                        if post:
                            dve.wait_ge(post_std, 2 * posts[n] + t + 1)
                            step(v.reciprocal(rstd[:, t:t + 1], std[:, t:t + 1]))
                            i = v.scalar_tensor_tensor(tmp[:, t], acc[:, t].rearrange("p h n -> p (h n)"),
                                                       rstd[:, t:t + 1], gain_post[:], ALU.mult, ALU.mult)
                            i.then_inc(acc_free_dve[t], 1)
                            dve.wait_ge(acc_free_dve[t], ACC_ORDER[:FIRST_ACC[stage_name] + 1].count("V"))
                            v.scalar_tensor_tensor(x[:, t], tmp[:, t], factor, x[:, t], ALU.mult, ALU.add)\
                                .then_inc(x_ready, 1)
                            if t == 0:
                                low_to(after + 1)
                            else:
                                low_to(after + 4)
                        else:
                            dve.wait_ge(acc_full[t], FIRST_ACC[stage_name] + 1)
                            v.tensor_tensor(x[:, t], acc[:, t].rearrange("p h n -> p (h n)"), x[:, t], ALU.add)\
                                .then_inc(acc_free_dve[t], 1)
                            if t == 1:
                                low_to(after + 4)
                    elif t == 0:
                        dve.wait_ge(gain0_landed, 16)
                    dve.wait_ge(pre_std, 2 * n + t + 1)
                    step(v.reciprocal(rstd[:, 2 + t:3 + t], std[:, 2 + t:3 + t]))
                    for h in range(2):
                        part = slice(h * 512, (h + 1) * 512)
                        v.scalar_tensor_tensor(tmp[:, t, part], x[:, t, part], rstd[:, 2 + t:3 + t],
                                               gain_pre[:, part], ALU.mult, ALU.mult).then_inc(xn_ready, 1)
                    if n == 0 and t == 1:
                        low_to(after + 4)
                    if n < 5:
                        for h in range(2):
                            cols = slice(t * P, (t + 1) * P)
                            take_lo(f"t{n}", 2 * t + h, xT_lo[:, 4 * h:4 * h + 4, cols],
                                    xT_hi[:, 4 * h:4 * h + 4, cols],
                                    aux[:, 2 * t + h].rearrange("p (c q) -> p c q", c=4))
                    if t == 0:
                        low_to(after + 3)

            norm(*NORMS[0])
            dve.wait_ge(consts_in, 16 * 8)
            step(v.tensor_scalar(ls[2][:], logit[:], -1.0, None, ALU.mult))
            v.tensor_tensor(ls[0][:], logit[:], ls[2][:], ALU.min).then_inc(ls_neg, 1)
            dve.wait_ge(ls_exp, 1)
            step(v.tensor_scalar(ls[2][:], ls[1][:], 2.0, None, ALU.add))
            step(v.reciprocal(ls[3][:], ls[2][:]))
            step(v.tensor_tensor(ls[2][:], ls[1][:], ls[3][:], ALU.mult))
            step(v.tensor_tensor(ls[3][:], ls[2][:], ls[2][:], ALU.mult))
            step(v.tensor_scalar(ls[4][:], ls[3][:], 1.0 / 17, None, ALU.mult))
            for k in (15, 13, 11, 9, 7, 5, 3):
                step(v.scalar_tensor_tensor(ls[4][:], ls[4][:], 1.0 / k, ls[3][:], ALU.add, ALU.mult))
            step(v.scalar_tensor_tensor(ls[4][:], ls[4][:], 1.0, ls[2][:], ALU.add, ALU.mult))
            step(v.tensor_scalar(ls[0][:], logit[:], 0.0, None, ALU.min))
            step(v.scalar_tensor_tensor(ls[1][:], ls[4][:], -2.0, ls[0][:], ALU.mult, ALU.add))
            log_gamma = ls[1]
            step(v.tensor_scalar(lrate[:, 0], log_gamma[:, 2 * RH:], 8.0, None, ALU.mult))
            step(v.tensor_scalar(lrate[:, 1], log_gamma[:, 2 * RH:], 4.0, None, ALU.mult))

            def swiglu(which):
                st = f"{which}_in"
                g0, f0, q0 = FIRST_GROUP[st], FIRST_FILL[st], FIRST_SPLIT[st]
                gate0 = {"f1": 0, "f2": GATES_F2}[which]

                def up(j, par, t):
                    dve.wait_ge(gate_ready[t], gate0 + 1 + j)
                    if not (isinstance(j, int) and j < 2):
                        dve.wait_ge(bank_full, f0 - 1 + j)
                    v.tensor_tensor(prod[:, par, t], acc[:, t, par, 256:512], silu_g[:, t], ALU.mult)\
                        .then_inc(acc_free_dve[t], 1)

                def hidden_lo(j, par):
                    chunks = slice(2 * j, 2 * j + 2) if isinstance(j, int) else bass.ds(2 * j, 2)
                    dve.wait_ge(bank_hi, q0 + 1 + j)
                    v.tensor_tensor(hT_lo[:, chunks, :], aux[:, par].rearrange("p (c q) -> p c q", c=2),
                                    hT_hi[:, chunks, :].bitcast(F32), ALU.subtract).then_inc(bank_free, 1)

                def column(j, par, lows):
                    lows()
                    up(j, par, 0)
                    if not (isinstance(j, int) and j == 0):
                        hidden_lo(j - 1, 1 - par)
                    up(j, par, 1)

                up(0, 0, 0)
                up(1, 1, 0)
                low_to(g0 + 5)
                up(0, 0, 1)
                low_to(g0 + 6)
                up(1, 1, 1)
                hidden_lo(0, 0)
                with dve.Fori(1, 5) as i:
                    for b in range(2):
                        column(i * 2 + b, b, lambda: [low_in_loop(g0 + 6, i, 1, 2 * b + h) for h in range(2)])
                split[0] += 16
                column(10, 0, lambda: low_to(g0 + 24))
                low_to(g0 + 25)
                hidden_lo(10, 0)
                low_to(FIRST_GROUP[f"{which}_out"] + GROUPS[f"{which}_out"] + 1)

            GATES_F2 = 11 + 2
            swiglu("f1")
            norm(*NORMS[1])

            g0, c0 = FIRST_GROUP["mix_in"], FIRST_ACC["mix_in"]

            def copy_fill(name, n, copies):
                dve.wait_ge(bank_full, FIRST_FILL[name] + n + 1)
                for k, (dst, src) in enumerate(copies):
                    i = v.tensor_copy(dst, src)
                i.then_inc(bank_free, 1)

            def heads_of(bank):
                return aux[:, bank].rearrange("p (c q) -> p c q", c=4)

            def rotate(t, par, n):
                source = acc[:, t, par].rearrange("p (h s i) -> p h s i", h=RH, s=2)
                turned = rot_b[:, t].rearrange("p (h s i) -> p h s i", h=RH, s=2)
                v.tensor_tensor(stage[:, t].rearrange("p (a i) -> p a i", a=2 * RH),
                                acc[:, t, par].rearrange("p (a i) -> p a i", a=2 * RH),
                                rot[:, t, 0:1].to_broadcast([P, 2 * RH, 64]), ALU.mult)
                v.tensor_tensor(turned[:, :, 0], source[:, :, 1], rot[:, t, 2:3].to_broadcast([P, RH, 64]), ALU.mult)
                i = v.tensor_tensor(turned[:, :, 1], source[:, :, 0], rot[:, t, 1:2].to_broadcast([P, RH, 64]),
                                    ALU.mult)
                i.then_inc(acc_free_dve[t], 1)

            for c in range(13):
                for t in range(T):
                    par, slot = c % 2, 2 * c + t
                    low_to(g0 + 2 * c + 4 + t)
                    if 2 <= slot < 2 + RH:
                        dve.wait_ge(dist_in_s, 16)
                        for h in (slot - 2,):
                            step(v.tensor_scalar(decay[:, h], dist[:, 0], log_gamma[:, h:h + 1], None, ALU.mult))
                            v.scalar_tensor_tensor(decay[:, h].rearrange("p a q -> p (a q)"),
                                                   dist[:, 1].rearrange("p a q -> p (a q)"),
                                                   log_gamma[:, RH + h:RH + h + 1],
                                                   decay[:, h].rearrange("p a q -> p (a q)"), ALU.mult, ALU.add)\
                                .then_inc(decay_arg, 1)
                    if c in (3, 4):
                        dve.wait_ge(acc_full[t], c0 + c + 1)
                        if c == 3:
                            dve.wait_ge(bank_full, FIRST_FILL["nk"] + t + 1)
                        else:
                            dve.wait_ge(bank_full, FIRST_FILL["rq"] + t + 1)
                        rotate(t, par, T * (c - 3) + t)
                    if c in (7, 8):
                        dve.wait_ge(gate_ready[t], 11 + c - 6)
                        part = y_ret[:, t, (c - 7) * 512:(c - 6) * 512]
                        v.scalar_tensor_tensor(part, part, 1.0, acc[:, t, par], ALU.add, ALU.mult)\
                            .then_inc(acc_free_dve[t], 1)
                        if c == 8 and t == 1:
                            for tt in range(T):
                                dve.wait_ge(acc_free_dve[tt], ACC_ORDER[:c0 + c + 1].count("V"))
                    if slot == 3:
                        for tt in range(T):
                            cols = slice(tt * P, (tt + 1) * P)
                            if tt == 0:
                                dve.wait_ge(pad_set, 2)
                            copy_fill("nq", tt, [(nqT[e][64 * e:64 * e + 64, :, cols],
                                                  heads_of(tt)[64 * e:64 * e + 64]) for e in range(2)])
                    if slot == 5:
                        for tt in range(T):
                            copy_fill("nk", tt, [(nkT[:, :, tt * P:(tt + 1) * P], heads_of(tt))])
                    if 8 <= slot < 12:
                        name, dst = ("rq", rqT) if slot < 10 else ("rk", rkT)
                        copy_fill(name, t, [(dst[:, :, t * P:(t + 1) * P], heads_of(0))])
                    if 12 <= slot < 16:
                        h = slot - 12
                        dve.wait_ge(bank_full, FIRST_FILL["rs"] + h + 1)
                        if h == 0:
                            dve.wait_ge(decay_done, RH)
                        flat = decay[:, h].rearrange("p a q -> p (a q)")
                        v.scalar_tensor_tensor(flat, aux[:, 0], RQ ** -0.5, flat, ALU.mult, ALU.mult)\
                            .then_inc(bank_free, 1)
                    s = slot - 6
                    if 0 <= s - 1 < 16:
                        dve.wait_ge(pT_full, s)
                        if s - 1 >= 2:
                            dve.wait_ge(o_full, s - 2)
                        v.tensor_copy(probT[:, (s - 1) % 2].rearrange("p a q -> p (a q)"), aux[:, 2, 0:S])\
                            .then_inc(pT_copied, 1)
                    if 0 <= s - 2 < 16:
                        n = s - 2
                        dve.wait_ge(o_full, n + 1)
                        dve.wait_ge(p_ready, n + 1)
                        step(v.reciprocal(prob_rec[:, n:n + 1], prob_sum[:, n:n + 1]))
                        h = n % NH
                        v.tensor_scalar(y_na[:, n // NH, h * ND:(h + 1) * ND], aux[:, 3, 0:ND],
                                        prob_rec[:, n:n + 1], None, ALU.mult).then_inc(o_taken, 1)
                    if 0 <= s < 16:
                        dve.wait_ge(s_full, s + 1)
                        dve.wait_ge(bias_ready, s + 1)
                        if s >= 2:
                            dve.wait_ge(p_ready, s - 1)
                        v.tensor_tensor_reduce(out=neg_s[:, s % 2], in0=aux[:, 1, 0:S],
                                               in1=bias_m[:, s % 2].rearrange("p a q -> p (a q)"), scale=-1.0,
                                               scalar=3e38, op0=ALU.add, op1=ALU.min,
                                               accum_out=neg_max[:, s:s + 1]).then_inc(s_reduced, 1)
                    if 18 <= slot < 22:
                        h = slot - 18
                        dve.wait_ge(ret_sq, h + 1)
                        for tt in range(T):
                            part = y_ret[:, tt, h * RV:(h + 1) * RV]
                            i = v.tensor_tensor(part, part, aux[:, 0, tt * RV:(tt + 1) * RV], ALU.mult)
                        i.then_inc(bank_free, 1)
                        if h == RH - 1:
                            dve.wait_ge(bank_free, FIRST_FILL["rp"] + RH)
                    if slot == 22:
                        dve.wait_ge(ret_std_s, 1)
                        step(v.reciprocal(ret_rstd[:], ret_std[:]))
                        for tt in range(T):
                            for h in range(RH):
                                part = y_ret[:, tt, h * RV:(h + 1) * RV]
                                i = v.tensor_scalar(part, part, ret_rstd[:, tt, h:h + 1], None, ALU.mult)
                            i.then_inc(y_ret_ready, 1)
                    if slot == 24:
                        for tt in range(T):
                            cols = slice(tt * P, (tt + 1) * P)
                            take_lo("yna", tt, ynaT_lo[:, :, cols], ynaT_hi[:, :, cols], heads_of(1 + tt))
                    if slot in (24, 25):
                        tt = slot - 24
                        cols = slice(tt * P, (tt + 1) * P)
                        for h in range(2):
                            chunks = slice(4 * h, 4 * h + 4)
                            take_lo("yret", 2 * tt + h, yretT_lo[:, chunks, cols], yretT_hi[:, chunks, cols],
                                    heads_of(0 if h == 0 else 3))
            low_to(FIRST_GROUP["ret_out"] + 4)
            for t in range(T):
                dve.wait_ge(acc_full[t], FIRST_ACC["na_out"] + 1)
                dve.wait_ge(acc_free_act[t], ACC_ORDER[:FIRST_ACC["na_out"]].count("A"))
                v.scalar_tensor_tensor(m_na[:, t], m_na[:, t], 1.0, acc[:, t].rearrange("p h n -> p (h n)"),
                                       ALU.add, ALU.mult).then_inc(acc_free_dve[t], 1)
            for t in range(T):
                dve.wait_ge(acc_free_dve[t], ACC_ORDER[:FIRST_ACC["na_out"] + 1].count("V"))
                dve.wait_ge(ret_acc_full, t + 1)
                for h in range(2):
                    part = slice(h * 512, (h + 1) * 512)
                    step(v.scalar_tensor_tensor(m_ret[:, t, part], m_ret[:, t, part], 1.0, aux[:, 2 * t + h],
                                                ALU.add, ALU.mult))
                    v.tensor_tensor(m_ret[:, t, part], m_ret[:, t, part], m_na[:, t, part], ALU.add)\
                        .then_inc(merged_ready, 1)
                for h in range(2):
                    cols, chunks = slice(t * P, (t + 1) * P), slice(4 * h, 4 * h + 4)
                    take_lo("merged", 2 * t + h, xT_lo[:, chunks, cols], xT_hi[:, chunks, cols], heads_of(2 * t + h),
                            scale=0.5)
                if t == 0:
                    low_to(FIRST_GROUP["mix_out"] + 4)
            norm(*NORMS[2])

            swiglu("f2")
            norm(*NORMS[3])

            g0, c0, f0 = FIRST_GROUP["a_in"], FIRST_ACC["a_in"], FIRST_FILL["a_in"]
            gate0 = GATES_F2 + 11

            def conv_rest(f):
                dve.wait_ge(conv_head, 2 * f + 2)
                for lag in (1, 2, 3):
                    for k in range(2):
                        ch = 2 * f + k
                        i = v.scalar_tensor_tensor(u[:, ch, lag:], aux[:, f % 2, k * S:(k + 1) * S - lag],
                                                   conv_a[:, ch, 3 - lag:4 - lag], u[:, ch, lag:], ALU.mult, ALU.add)
                        if k == 1 and lag < 3:
                            step(i)
                i.then_inc(bank_free, 1)

            def rates(m):
                four = slice(4 * m, 4 * m + 4)
                dve.wait_ge(et_ready, 8 * (m + 1))
                step(v.scalar_tensor_tensor(ri[:, four, 0], av[:, four], 1.0, ri[:, four, 0], ALU.add, ALU.mult))
                v.scalar_tensor_tensor(av[:, four], ri[:, four, 0], 2.0, ri[:, four, 0], ALU.add, ALU.mult)\
                    .then_inc(v_ready, 1)
                dve.wait_ge(v_ready, m + 1)
                step(v.tensor_scalar(ri[:, four, 0], ri[:, four, 0], 1.0, None, ALU.add))

            def scans(m):
                four = slice(4 * m, 4 * m + 4)
                dve.wait_ge(mult_ready, m + 1)
                dve.wait_ge(iu_ready, 4 * m + 4)
                step(v.tensor_tensor(ri[:, four, 1], ri[:, four, 1], av[:, four], ALU.mult))
                for ch in range(4 * m, 4 * m + 4):
                    i = v.tensor_tensor_scan(u[:, ch], ri[:, ch, 0], ri[:, ch, 1], 0.0, ALU.mult, ALU.add)
                step(i)

            def gate_fill_bank(n):
                return (0, 1, 2, 3, 0, 1)[n]

            def gated(n):
                dve.wait_ge(bank_full, f0 + 6 + n + 1)
                if n >= 2:
                    dve.wait_ge(bank_free, f0 + 6 + n - 1)
                v.scalar_tensor_tensor(yg[:, n % 2], aux[:, gate_fill_bank(n)], 0.5,
                                       u[:, 2 * n:2 * n + 2].rearrange("p c q -> p (c q)"), ALU.mult, ALU.mult)\
                    .then_inc(yg_ready, 1)

            def gated_lo(n):
                take_lo("gate", n, yT_lo[:, 2 * n:2 * n + 2].rearrange("p c q -> p (c q)"),
                        yT_hi[:, 2 * n:2 * n + 2].rearrange("p c q -> p (c q)"), yg[:, n % 2])

            for c in range(6):
                for t in range(T):
                    if c != 5:
                        low_to(g0 + 2 * c + 4 + t)
                    if t == 0 and 1 <= c <= 3:
                        conv_rest(2 * c - 2)
                        conv_rest(2 * c - 1)
                    if c >= 3:
                        dve.wait_ge(gate_ready[t], gate0 + c - 2)
                        v.scalar_tensor_tensor(a_stage[:, t], a_stage[:, t], 1.0, acc[:, t, c % 2], ALU.add, ALU.mult)\
                            .then_inc(acc_free_dve[t], 1)
                    if (c, t) == (3, 1):
                        rates(0)
                    if (c, t) == (4, 1):
                        rates(1)
                    if (c, t) == (5, 0):
                        scans(0)
                        gated(0)
                        gated(1)
                        gated_lo(0)
                        gated_lo(1)
                        low_to(g0 + 2 * c + 4 + t)
            scans(1)
            gated(2)
            gated(3)
            gated_lo(2)
            low_to(FIRST_GROUP["a_out"] + 3)
            gated_lo(3)
            rates(2)
            low_to(FIRST_GROUP["a_out"] + 4)
            scans(2)
            gated(4)
            gated_lo(4)
            low_to(FIRST_GROUP["a_out"] + 5)
            gated(5)
            gated_lo(5)
            low_to(FIRST_GROUP["a_out"] + 6)
            low_to(FIRST_GROUP["b_in"] + 1)
            norm(*NORMS[4])

            g0, c0, f0, q0 = FIRST_GROUP["b_in"], FIRST_ACC["b_in"], FIRST_FILL["b_in"], FIRST_SPLIT["b_in"]
            gate0 = GATES_F2 + 11 + 3

            def b_products(j, par, t):
                dve.wait_ge(gate_ready[t], j * 2 + (gate0 + 2))
                if not (isinstance(j, int) and j < 2):
                    dve.wait_ge(bank_full, f0 - 1 + j)
                v.tensor_tensor(b_prod[:, par, t], acc[:, t, par, 0:2 * P], b_gate[:, t], ALU.mult)\
                    .then_inc(acc_free_dve[t], 1)

            def tap(j, k):
                if isinstance(j, int):
                    return conv_b[:, j, k:k + 1]
                return conv_b[:, bass.ds(j, 1), k:k + 1].rearrange("p a b -> p (a b)")

            def b_short_conv(j, par):
                dve.wait_ge(bank_full, f0 + 1 + j)
                if not (isinstance(j, int) and j == 0):
                    dve.wait_ge(b_y_ready, j)
                p = aux[:, par, S:2 * S]
                step(v.tensor_scalar(b_conv[:], p, tap(j, 2), None, ALU.mult))
                step(v.scalar_tensor_tensor(b_conv[:, 1:], p[:, 0:S - 1], tap(j, 1), b_conv[:, 1:], ALU.mult, ALU.add))
                step(v.scalar_tensor_tensor(b_conv[:, 2:], p[:, 0:S - 2], tap(j, 0), b_conv[:, 2:], ALU.mult, ALU.add))
                v.tensor_tensor(b_y[:, par], aux[:, par, 0:S], b_conv[:], ALU.mult).then_inc(b_y_ready, 1)

            def b_lo(j, par):
                dve.wait_ge(bank_hi, q0 + 1 + j)
                one = (slice(j, j + 1) if isinstance(j, int) else bass.ds(j, 1))
                v.tensor_tensor(yT_lo[:, one, :].rearrange("p a q -> p (a q)"), b_y[:, par],
                                yT_hi[:, one, :].rearrange("p a q -> p (a q)").bitcast(F32), ALU.subtract)\
                    .then_inc(bank_free, 1)

            def b_column(j, par, lows):
                lows()
                b_products(j, par, 0)
                if not (isinstance(j, int) and j == 0):
                    b_short_conv(j - 1, 1 - par)
                b_products(j, par, 1)
                if not (isinstance(j, int) and j == 0):
                    b_lo(j - 1, 1 - par)

            b_products(0, 0, 0)
            b_products(1, 1, 0)
            low_to(g0 + 5)
            b_products(0, 0, 1)
            low_to(g0 + 6)
            b_products(1, 1, 1)
            b_short_conv(0, 0)
            b_lo(0, 0)
            before, per_lap = step.n, 2 * 3
            with dve.Fori(1, 6) as i:
                step.base = (i - 1) * per_lap
                for b in range(2):
                    b_column(i * 2 + b, b, lambda: [low_in_loop(g0 + 6, i, 1, 2 * b + h) for h in range(2)])
                assert step.n == before + per_lap
            step.base = 0
            step.n = before + 5 * per_lap
            split[0] += 20
            low_to(FIRST_GROUP["b_out"] + 3)
            b_short_conv(11, 1)
            b_lo(11, 1)
            low_to(NG)
            norm(*NORMS[5])

        @block.tensor
        def _(pe):
            m = nc.tensor

            def product(dst, hi, lo, k, t, slot, unit, first, last):
                cols = slice(t * P, (t + 1) * P)
                w = slice(unit * UNIT, (unit + 1) * UNIT)
                m.matmul(dst, hi[:, k, cols], w_hi[:, slot, w], start=first, stop=False)
                m.matmul(dst, hi[:, k, cols], w_lo[:, slot, w], start=False, stop=False)
                return m.matmul(dst, lo[:, k, cols], w_hi[:, slot, w], start=False, stop=last)

            def column_tile(g, slot0, par, t, before_half=None):
                for half in range(2):
                    if before_half:
                        before_half(half)
                    if t == 0:
                        pe.wait_ge(lo_done, g + (half + 1))
                    for unit in range(4):
                        i = product(acc[:, t, par], xT_hi, xT_lo, 4 * half + unit, t, (slot0 + half) % RING, unit,
                                    half == 0 and unit == 0, half == 1 and unit == 3)
                    if t == 1 and half == 0:
                        i.then_inc(group_used, 1)
                i.then_inc(acc_full[t], 1)

            def wait_operand(fills):
                pe.wait_ge(bank_free, fills)

            def out_tile(st, n, t, hi, lo, chunks, target, done):
                g = FIRST_GROUP[st] + n
                if t == 0:
                    pe.wait_ge(lo_done, g + 1)
                for kk in range(2):
                    k = 2 * n + kk
                    for half in range(2):
                        i = product(target(t, half), hi, lo, k, t, g % RING, 2 * kk + half, k == 0, k == chunks - 1)
                if n == chunks // 2 - 1:
                    i.then_inc(*done(t))
                elif t == 1:
                    i.then_inc(group_used, 1)

            def acc_target(t, half):
                return acc[:, t, half]

            def out_stage(st, hi, lo, chunks, wait_chunk=lambda n: None, after_first=lambda: None):
                groups = chunks // 2
                blocks = [(0, 1)] + [(n,) for n in range(2, groups - 3)] + [tuple(range(groups - 3, groups))]
                for block in blocks:
                    for t in range(T):
                        if block[0] == 0:
                            wait_acc_free(pe, t, FIRST_ACC[st])
                        for n in block:
                            if t == 0:
                                wait_chunk(n)
                            out_tile(st, n, t, hi, lo, chunks, acc_target, lambda t: (acc_full[t], 1))
                    if block[0] == 0:
                        after_first()

            def norm_transposes(n):
                def run(t):
                    for h in range(2):
                        pe.wait_ge(xn_ready, 4 * n + 2 * t + h + 1)
                        if FIRST_FILL[f"t{n}"]:
                            pe.wait_ge(bank_free, FIRST_FILL[f"t{n}"])
                        for c in range(4):
                            i = m.transpose(aux[:, 2 * t + h, c * P:(c + 1) * P],
                                            tmp[:, t, (4 * h + c) * P:(4 * h + c + 1) * P], ident[:])
                        i.then_inc(bank_full, 1)
                return run

            def first_columns(n, st):
                run = norm_transposes(n)
                g0 = FIRST_GROUP[st]
                for t in range(T):
                    run(t)
                    wait_acc_free(pe, t, FIRST_ACC[st])
                    column_tile(g0, g0 % RING, 0, t, lambda half: wait_operand(FIRST_FILL[f"t{n}"] + 2 * t + half + 1))
                    column_tile(g0 + 2, (g0 + 2) % RING, 1, t)

            def swiglu(which, n):
                st = f"{which}_in"
                g0, c0, f0 = FIRST_GROUP[st], FIRST_ACC[st], FIRST_FILL[st]
                prods0 = ACC_ORDER[:c0].count("V")
                n_act = ACC_ORDER[:c0].count("A")
                n_dve = c0 - n_act

                def hidden_transposes(j, par):
                    for t in range(T):
                        pe.wait_ge(acc_free_dve[t], prods0 + 1 + j)
                    pe.wait_ge(bank_free, f0 if isinstance(j, int) and j < 2 else f0 - 1 + j)
                    for c in range(2):
                        for t in range(T):
                            i = m.transpose(aux[:, par, c * S + t * P:c * S + (t + 1) * P],
                                            prod[:, par, t, c * P:(c + 1) * P], ident[:])
                    i.then_inc(bank_full, 1)

                def column(j, par):
                    for t in range(T):
                        pe.wait_ge(acc_free_dve[t], n_dve - 1 + j)
                        column_tile(g0 + 2 * j, (g0 + 2 * par) % RING, par, t)
                        if t == 0:
                            hidden_transposes(j - 1, 1 - par)

                first_columns(n, st)
                hidden_transposes(0, 0)
                with pe.Fori(1, 5) as i:
                    for b in range(2):
                        column(i * 2 + b, b)
                column(10, 0)

                def wait_chunk(g):
                    pe.wait_ge(bank_free, f0 + g + 1)

                out_stage(f"{which}_out", hT_hi, hT_lo, FF // P, wait_chunk, lambda: hidden_transposes(10, 0))

            pe.wait_ge(ident_landed, 16)
            swiglu("f1", 0)

            g0, c0 = FIRST_GROUP["mix_in"], FIRST_ACC["mix_in"]
            fill = [FIRST_FILL["nq"]]

            def transposes(bank, source, n_free):
                pe.wait_ge(bank_free, n_free)
                for c in range(4):
                    i = m.transpose(aux[:, bank, c * P:(c + 1) * P], source[:, c * P:(c + 1) * P], ident[:])
                i.then_inc(bank_full, 1)

            def scores(s):
                t, h = s // NH, s % NH
                if s:
                    pe.wait_ge(s_reduced, s)
                else:
                    pe.wait_ge(bank_free, FIRST_FILL["nk"] + 2)
                m.matmul(aux[:, 1, 0:S], nqT[h % 2][:, h // 2, t * P:(t + 1) * P], nkT[:, h // 2, :],
                         start=True, stop=True).then_inc(s_full, 1)

            def prob_transposes(s):
                pe.wait_ge(p_ready, s + 1)
                if s:
                    pe.wait_ge(pT_copied, s)
                for k in range(T):
                    i = m.transpose(aux[:, 2, k * P:(k + 1) * P], prob[:, s % 2, k * P:(k + 1) * P], ident[:])
                i.then_inc(pT_full, 1)

            def attend(s):
                pe.wait_ge(pT_copied, s + 1)
                if s:
                    pe.wait_ge(o_taken, s)
                h = s % NH
                for k in range(T):
                    i = m.matmul(aux[:, 3, 0:ND], probT[:, s % 2, k, :], nv[:, k, h * ND:(h + 1) * ND],
                                 start=k == 0, stop=k == T - 1)
                i.then_inc(o_full, 1)

            def extras(slot):
                if slot == 3:
                    for t in range(T):
                        pe.wait_ge(acc_free_act[t], 1)
                        transposes(t, stage[:, t], FIRST_FILL["nq"])
                if slot == 5:
                    for t in range(T):
                        pe.wait_ge(acc_free_act[t], 2)
                        transposes(t, stage[:, t], FIRST_FILL["nk"])
                if 8 <= slot < 12:
                    t = slot % 2
                    n = slot - 8
                    pe.wait_ge(rot_done, n + 1)
                    transposes(0, stage[:, t], FIRST_FILL["rq"] + n)
                if 12 <= slot < 16:
                    h = slot - 12
                    pe.wait_ge(bank_free, FIRST_FILL["rs"] + h)
                    for k in range(T):
                        i = m.matmul(aux[:, 0, k * S:(k + 1) * S], rkT[:, h, k * P:(k + 1) * P], rqT[:, h, :],
                                     start=True, stop=True)
                    i.then_inc(bank_full, 1)
                if 18 <= slot < 22:
                    h = slot - 18
                    pe.wait_ge(bank_free, FIRST_FILL["rp"] + h)
                    if h == 0:
                        for t in range(T):
                            pe.wait_ge(acc_free_act[t], ACC_ORDER[:c0 + 7].count("A"))
                    for t in range(T):
                        for k in range(T):
                            i = m.matmul(aux[:, 0, t * RV:(t + 1) * RV], decay[:, h, k, t * P:(t + 1) * P],
                                         rv[:, k, h * RV:(h + 1) * RV], start=k == 0, stop=k == T - 1)
                    i.then_inc(bank_full, 1)
                s = slot - 6
                if 0 <= s < 16:
                    scores(s)
                if 0 <= s - 1 < 16:
                    prob_transposes(s - 1)
                if 0 <= s - 2 < 16:
                    attend(s - 2)
                if slot == 24:
                    pe.wait_ge(o_taken, 16)
                    for t in range(T):
                        transposes(1 + t, y_na[:, t], FIRST_FILL["yna"])
                if slot in (24, 25):
                    t = slot - 24
                    pe.wait_ge(y_ret_ready, t + 1)
                    for h in range(2):
                        transposes(0 if h == 0 else 3, y_ret[:, t, h * 512:(h + 1) * 512],
                                   FIRST_FILL["yret"] + 2 * t if t else FIRST_FILL["yna"])

            first_columns(1, "mix_in")
            extras(3)
            for c in range(2, 13):
                for t in range(T):
                    wait_acc_free(pe, t, c0 + c - 1)
                    column_tile(g0 + 2 * c, (g0 + 2 * c) % RING, c % 2, t)
                    extras(2 * c + t)

            for t in range(T):
                wait_acc_free(pe, t, FIRST_ACC["na_out"])
                if t == 0:
                    pe.wait_ge(bank_free, FIRST_FILL["yret"] + 4)
                for n in range(2):
                    out_tile("na_out", n, t, ynaT_hi, ynaT_lo, NH // 2, acc_target, lambda t: (acc_full[t], 1))

            def aux_target(t, half):
                return aux[:, 2 * t + half]

            for t in range(T):
                for n in range(4):
                    out_tile("ret_out", n, t, yretT_hi, yretT_lo, KD, aux_target, lambda t: (ret_acc_full, 1))

            def merged_transposes(t):
                for h in range(2):
                    pe.wait_ge(merged_ready, 2 * t + h + 1)
                    bank = 2 * t + h
                    for c in range(4):
                        i = m.transpose(aux[:, bank, c * P:(c + 1) * P],
                                        m_ret[:, t, (4 * h + c) * P:(4 * h + c + 1) * P], ident[:])
                    i.then_inc(bank_full, 1)

            merged_transposes(0)
            for t in range(T):
                wait_acc_free(pe, t, FIRST_ACC["mix_out"])
                for n in range(4):
                    pe.wait_ge(bank_free, FIRST_FILL["merged"] + 2 * t + n // 2 + 1)
                    out_tile("mix_out", n, t, xT_hi, xT_lo, KD, acc_target, lambda t: (acc_full[t], 1))
                    if t == 0 and n == 1:
                        merged_transposes(1)

            swiglu("f2", 2)

            g0, c0, f0 = FIRST_GROUP["a_in"], FIRST_ACC["a_in"], FIRST_FILL["a_in"]

            def pair_transposes(c, banks):
                for k in range(2):
                    f = 2 * c + k
                    pe.wait_ge(bank_free, f0 + max(0, f - 1) if f < 8 else f0 + 6 if f < 10 else f0 + f - 3)
                    for j in range(2):
                        for t in range(T):
                            col = (2 * k + j) * P
                            i = m.transpose(aux[:, banks[k], j * S + t * P:j * S + (t + 1) * P],
                                            a_stage[:, t, col:col + P], ident[:])
                    i.then_inc(bank_full, 1)

            def lru_gates(ch):
                pe.wait_ge(bank_free, f0 + ch // 2 + 1)
                if ch >= 2:
                    pe.wait_ge(g_taken, ch - 1)
                if ch == 0:
                    pe.wait_ge(gate_w_in_s, 16)
                for k in range(2):
                    i = m.matmul(aux[:, 2 + ch % 2, k * S:(k + 1) * S], gate_w[:, ch, k], u[:, ch], start=True, stop=True)
                i.then_inc(g_full, 1)

            def staged_transposes(c):
                for t in range(T):
                    wait_acc_free(pe, t, c0 + c + 1)
                if c == 4:
                    pe.wait_ge(g_taken, CH)
                pair_transposes(c, (2, 3) if c == 4 else (0, 1))

            first_columns(3, "a_in")
            staged_transposes(0)
            for c in range(2, 6):
                for t in range(T):
                    wait_acc_free(pe, t, c0 + c - 1)

                    def before_half(half):
                        if (t, half) == ((1, 0) if c in (2, 5) else (0, 1)):
                            staged_transposes(c - 1)
                        first = {(2, 1, 1): 0, (3, 0, 0): 2, (3, 0, 1): 4, (3, 1, 0): 6, (4, 0, 0): 8,
                                 (4, 0, 1): 10}.get((c, t, half))
                        if first is not None:
                            lru_gates(first)
                            lru_gates(first + 1)

                    column_tile(g0 + 2 * c, (g0 + 2 * c) % RING, c % 2, t, before_half)
            out_stage("a_out", yT_hi, yT_lo, CH, lambda n: pe.wait_ge(bank_free, f0 + 6 + n + 1),
                      lambda: staged_transposes(5))

            g0, c0, f0 = FIRST_GROUP["b_in"], FIRST_ACC["b_in"], FIRST_FILL["b_in"]
            n_dve = ACC_ORDER[:c0].count("V")

            def b_transposes(j, par):
                for t in range(T):
                    pe.wait_ge(acc_free_dve[t], n_dve + 1 + j)
                if isinstance(j, int) and j < 2:
                    pe.wait_ge(bank_free, f0)
                else:
                    pe.wait_ge(b_y_ready, j - 1)
                for k in range(2):
                    for t in range(T):
                        i = m.transpose(aux[:, par, k * S + t * P:k * S + (t + 1) * P],
                                        b_prod[:, par, t, k * P:(k + 1) * P], ident[:])
                i.then_inc(bank_full, 1)

            def b_column(j, par):
                for t in range(T):
                    pe.wait_ge(acc_free_dve[t], n_dve - 1 + j)
                    column_tile(g0 + 2 * j, (g0 + 2 * par) % RING, par, t)
                    if t == 0:
                        b_transposes(j - 1, 1 - par)

            first_columns(4, "b_in")
            b_transposes(0, 0)
            with pe.Fori(1, 6) as i:
                for b in range(2):
                    b_column(i * 2 + b, b)
            out_stage("b_out", yT_hi, yT_lo, CH, lambda n: pe.wait_ge(bank_free, f0 + 2 * n + 2),
                      lambda: b_transposes(11, 1))


def _stream(inputs):
    def columns(w, order):
        w = w.reshape(KD, P, -1)[:, :, order]
        w = w.reshape(2, 4, P, order.shape[0], UNIT).transpose(3, 0, 2, 1, 4)
        return w.reshape(-1, P, GROUP)

    def rows(w):
        return w.reshape(-1, 2, P, DM).transpose(0, 2, 1, 3).reshape(-1, P, GROUP)

    def blocks(parts, width, at):
        each = at[1] // width
        return np.array([[p * at[1] + b * width + i for p in parts for i in range(width)] for b in range(each)])

    ff = blocks((0, 1), 256, (0, FF))
    mix_starts = {"rq": 0, "rk": 512, "rv": 1024, "rg": 2048, "nq": 3072, "nk": 3584, "nv": 4096,
                  "gr": 4608, "gn": 5632}
    mix = np.array([np.arange(mix_starts[n] + 512 * c, mix_starts[n] + 512 * (c + 1))
                    for n, c in (("nq", 0), ("nk", 0), ("nv", 0), ("rq", 0), ("rk", 0), ("rv", 0), ("rv", 1),
                                 ("rg", 0), ("rg", 1), ("gr", 0), ("gr", 1), ("gn", 0), ("gn", 1))])
    a_cols = np.array([np.arange(W2 + 512 * c, W2 + 512 * (c + 1)) for c in range(3)]
                      + [np.arange(512 * c, 512 * (c + 1)) for c in range(3)])
    b_cols = blocks((0, 1, 3, 2), P, (0, W2))
    a = {k: np.asarray(v) for k, v in inputs.items()}
    return np.concatenate([
        columns(a["ffn1_w_in"][0], ff), rows(a["ffn1_w_out"][0]), columns(a["w_mix_in"][0], mix),
        rows(a["w_na_out"][0]), rows(a["w_ret_out"][0]), rows(a["w_mix_out"][0]),
        columns(a["ffn2_w_in"][0], ff), rows(a["ffn2_w_out"][0]), columns(a["a_w_in_2"][0], a_cols),
        rows(a["a_w_out_2"][0]), columns(a["b_w_in_2"][0], b_cols), rows(a["b_w_out_2"][0])])


def _bias_windows(rel):
    rows = rel[:, REL_R // 2 - (GR - 1):REL_R // 2 + GR]
    padded = np.pad(rows, ((0, 0), (0, 0), (GW - 1 - REL_C // 2, GW - 1 - REL_C // 2)))
    return np.stack([padded[:, :, GW - 1 - c:2 * GW - 1 - c] for c in range(GW)])


def _by_chunk(v):
    v = np.asarray(v)
    return np.moveaxis(v.reshape(v.shape[:-1] + (CH, P)), (-1, -2), (0, 1))


def kernel(**inputs):
    import concourse.bacc as bacc
    from concourse.bass_utils import run_bass_kernel_spmd

    f = np.float32
    inv = (f(1.0) / (f(10000.0) ** np.linspace(0.0, 1.0, 64, dtype=f))).astype(f)
    angle = np.arange(S, dtype=f)[:, None] * inv[None, :]
    rot = np.stack([np.cos(angle), np.sin(angle), -np.sin(angle)], axis=1).astype(f)
    rot = rot.reshape(T, P, 3, 64).transpose(1, 0, 2, 3)
    col = np.arange(P) % GW
    start = np.clip(col - WIN // 2, 0, GW - WIN)[:, None]
    key = np.arange(GW)[None, :]
    colmask = np.where((key >= start) & (key < start + WIN), f(0), f(-BIG)).astype(f)
    diff = (np.arange(S)[None, :] - np.arange(S)[:, None]).astype(f)
    dist = np.stack([np.maximum(diff, 0), np.maximum(-diff, 0)]).reshape(2, T, P, S).transpose(2, 0, 1, 3)

    a = {k: np.asarray(v) for k, v in inputs.items()}
    arrays = {
        "weights": _stream(inputs),
        "x_in": a["x"][0],
        "gains": np.concatenate([a["ffn1_pre_norm"], a["ffn1_post_norm"], a["mix_pre_norm"], a["mix_post_norm"],
                                 a["ffn2_pre_norm"], a["ffn2_post_norm"], a["norm_g_2"], a["final_g_2"][None]]),
        "ident_in": np.eye(P, dtype=f),
        "rot_in": rot,
        "colmask_in": colmask,
        "dist_in": dist,
        "decay_in": np.concatenate([a["ret_decay_fwd"], a["ret_decay_bwd"]], axis=1),
        "lam_in": _by_chunk(a["a_lambda_2"][0]),
        "bias_in": _bias_windows(a["na_rel_bias"][0]),
        "gate_w_in": a["a_gate_w_2"][0].reshape(CH, P, 2, P).transpose(1, 0, 2, 3),
        "gate_b_in": a["a_gate_b_2"][0].reshape(CH, 2, P).transpose(2, 0, 1),
        "conv_a_in": _by_chunk(a["a_conv_w_2"][0]),
        "conv_ab_in": _by_chunk(a["a_conv_b_2"][0]),
        "conv_b_in": _by_chunk(a["b_conv_w_2"][0]),
    }
    nc = bacc.Bacc("TRN2", target_bir_lowering=False, num_devices=1)
    args = {}
    for name, value in arrays.items():
        arrays[name] = np.ascontiguousarray(value)
        args[name] = nc.dram_tensor(name, arrays[name].shape, F32, kind="ExternalInput").ap()
    args["out"] = nc.dram_tensor("out", (S, DM), F32, kind="ExternalOutput").ap()
    build(nc, **args)
    result = run_bass_kernel_spmd(nc, [arrays], core_ids=[0])
    return np.asarray(result.results[0]["out"]).reshape(1, S, DM)
```

```python
from contextlib import ExitStack

import numpy as np

import concourse.bass as bass
from concourse import mybir

F32 = mybir.dt.float32
F32R = mybir.dt.float32r
ALU = mybir.AluOpType
ACT = mybir.ActivationFunctionType

P = 128
S = 256
T = S // P
DM = 1024
KD = DM // P
FF = 2816
W2 = 1536
CH = W2 // P
RH, RQ, RV = 4, 128, 256
NH, ND = 8, 64
GW, GR = 64, S // 64
WIN = 16
REL_R, REL_C = 15, 31
EPS = 1e-6
BIG = 1e30
UNIT = 512
GROUP = 4 * UNIT
RING = 4

STAGES = [("f1_in", 22), ("f1_out", 11), ("mix_in", 26), ("na_out", 2), ("ret_out", 4), ("mix_out", 4),
          ("f2_in", 22), ("f2_out", 11), ("a_in", 12), ("a_out", 6), ("b_in", 24), ("b_out", 6)]
NG = sum(n for _, n in STAGES)
FIRST_GROUP = {name: sum(n for _, n in STAGES[:i]) for i, (name, _) in enumerate(STAGES)}
GROUPS = dict(STAGES)

ACC_READERS = {"f1_in": "V" * 11, "f1_out": "V", "mix_in": "AAAVVAAVVAAAA", "na_out": "V", "mix_out": "V",
               "f2_in": "V" * 11, "f2_out": "V", "a_in": "AAAVVV", "a_out": "V", "b_in": "V" * 12, "b_out": "V"}
ACC_ORDER = "".join(ACC_READERS.values())
FIRST_ACC = {}
for _name in ACC_READERS:
    FIRST_ACC[_name] = sum(len(v) for k, v in ACC_READERS.items() if k in FIRST_ACC)

FILL_COUNTS = [("t0", 4), ("f1_in", 11), ("t1", 4), ("nq", 2), ("nk", 2), ("rq", 2), ("rk", 2), ("rs", 4), ("rp", 4),
               ("yna", 2), ("yret", 4), ("merged", 4), ("t2", 4), ("f2_in", 11), ("t3", 4),
               ("a_in", 12), ("t4", 4), ("b_in", 12)]
FIRST_FILL = {name: sum(n for _, n in FILL_COUNTS[:i]) for i, (name, _) in enumerate(FILL_COUNTS)}
SPLIT_COUNTS = [("t0", 4), ("f1_in", 11), ("t1", 4), ("yna", 2), ("yret", 4), ("merged", 4), ("t2", 4),
                ("f2_in", 11), ("t3", 4), ("gate", 6), ("t4", 4), ("b_in", 12)]
FIRST_SPLIT = {name: sum(n for _, n in SPLIT_COUNTS[:i]) for i, (name, _) in enumerate(SPLIT_COUNTS)}

RELEASE = []
for _name, _n in STAGES:
    for _g in range(_n):
        if _name.endswith("_in") and _g % 2 or _name.endswith("_out") and _g == _n - 1:
            if _name == "ret_out":
                RELEASE.append(("ret", T))
            else:
                RELEASE.append(("acc", FIRST_ACC[_name] + (_g // 2 if _name.endswith("_in") else 0) + 1))
        else:
            RELEASE.append(("used", 1 + sum(kind == "used" for kind, _ in RELEASE)))

NORMS = [(0, False, 0.0, None), (1, True, 0.5, "f1_out"), (2, True, 1.0, "mix_out"), (3, True, 0.5, "f2_out"),
         (4, False, 1.0, "a_out"), (5, False, 1.0, "b_out")]


NEXT_GROUP = [FIRST_GROUP[name] for name in ("f1_in", "mix_in", "f2_in", "a_in", "b_in")] + [NG]


class Chain:

    def __init__(self, engine, semaphore):
        self.engine, self.semaphore, self.base, self.n = engine, semaphore, 0, 0

    def __call__(self, instruction):
        instruction.then_inc(self.semaphore, 1)
        self.n += 1
        self.engine.wait_ge(self.semaphore, self.base + self.n)


def build(nc, weights, x_in, gains, ident_in, rot_in, colmask_in, dist_in, decay_in, lam_in, bias_in, gate_w_in,
          gate_b_in, conv_a_in, conv_ab_in, conv_b_in, out):
    with ExitStack() as ctx:
        base = nc.sbuf_base + (-nc.sbuf_base) % 32
        cursor = [base]

        def at(name, shape, dt, offset):
            return nc.alloc_sbuf_tensor_at(name, shape, dt, offset=offset)

        def sb(name, shape, dt=F32):
            size = 4 * int(np.prod(shape[1:]))
            size += -size % 32
            tensor = at(name, shape, dt, cursor[0])
            cursor[0] += size
            return tensor

        def sem(name):
            return ctx.enter_context(nc.semaphore(name))

        raw = sb("raw", [P, RING, GROUP])
        w_hi = sb("w_hi", [P, RING, GROUP], F32R)
        w_lo = sb("w_lo", [P, RING, GROUP], F32R)
        xT_hi = sb("xT_hi", [P, KD, S], F32R)
        xT_lo = sb("xT_lo", [P, KD, S], F32R)
        x = sb("x", [P, T, DM])
        gain_post = sb("gain_post", [P, DM])
        gain_pre = sb("gain_pre", [P, DM])
        ident = sb("ident", [P, P])
        rot = sb("rot", [P, T, 3, 64])
        colmask = sb("colmask", [P, GW])
        conv_a = sb("conv_a", [P, CH, 4])
        conv_ab = sb("conv_ab", [P, CH])
        conv_b = sb("conv_b", [P, CH, 3])
        gate_b = sb("gate_b", [P, CH, 2])
        logit = sb("logit", [P, 2 * RH + CH])
        ls = [sb(f"ls{i}", [P, 2 * RH + CH]) for i in range(5)]
        lrate = sb("lrate", [P, CH])
        eps1 = sb("eps1", [P, 1])
        eps4 = sb("eps4", [P, 1])
        zero = sb("zero", [P, 1])
        spare = sb("spare", [P, 1])
        sumsq = sb("sumsq", [P, 4])
        std = sb("std", [P, 4])
        rstd = sb("rstd", [P, 4])
        ret_sumsq = sb("ret_sumsq", [P, T, RH])
        ret_std = sb("ret_std", [P, T, RH])
        ret_rstd = sb("ret_rstd", [P, T, RH])
        neg_max = sb("neg_max", [P, T * NH])
        prob_sum = sb("prob_sum", [P, T * NH])
        prob_rec = sb("prob_rec", [P, T * NH])

        area = cursor[0]
        temp_at = nc.sbuf_usable_end - 4 * T * DM - 64
        temp_at = temp_at() if callable(temp_at) else temp_at
        temp_at -= temp_at % 32
        assert temp_at - area >= 67584, temp_at - area
        tmp = at("tmp", [P, T, DM], F32, temp_at)
        hT_hi = at("hT_hi", [P, FF // P, S], F32R, area)
        hT_lo = at("hT_lo", [P, FF // P, S], F32R, area + 22528)
        silu_g = at("silu_g", [P, T, 256], F32, area + 45056)
        prod = at("prod", [P, 2, T, 256], F32, area + 47104)
        nqT = [at(f"nqT{i}", [P, NH // 2, S], F32, area + 4096 * i) for i in range(2)]
        nkT = at("nkT", [P, NH // 2, S], F32, area + 8192)
        nv = at("nv", [P, T, NH * ND], F32, area + 12288)
        yretT_hi = at("yretT_hi", [P, KD, S], F32R, area)
        yretT_lo = at("yretT_lo", [P, KD, S], F32R, area + 8192)
        rqT = at("rqT", [P, RH, S], F32, area + 16384)
        rkT = at("rkT", [P, RH, S], F32, area + 20480)
        m_ret = at("m_ret", [P, T, DM], F32, area + 16384)
        rv = at("rv", [P, T, RH * RV], F32, area + 24576)
        ynaT_hi = at("ynaT_hi", [P, NH // 2, S], F32R, area + 24576)
        ynaT_lo = at("ynaT_lo", [P, NH // 2, S], F32R, area + 28672)
        decay = at("decay", [P, RH, T, S], F32, area + 32768)
        m_na = at("m_na", [P, T, DM], F32, area + 32768)
        y_ret = at("y_ret", [P, T, RH * RV], F32, area + 40960)
        y_na = at("y_na", [P, T, NH * ND], F32, area + 49152)
        stage = at("stage", [P, T, 512], F32, area + 53248)
        rot_b = at("rot_b", [P, T, 512], F32, area + 57344)
        dist = at("dist", [P, 2, T, S], F32, temp_at + 4096)
        bias_raw = at("bias_raw", [P, 2, GR, GW], F32, area + 61440)
        bias_m = at("bias_m", [P, 2, GR, GW], F32, area + 63488)
        neg_s = at("neg_s", [P, 2, S], F32, area + 65536)
        prob = at("prob", [P, 2, S], F32, temp_at)
        probT = at("probT", [P, 2, T, P], F32, temp_at + 2048)
        u = at("u", [P, CH, S], F32, area)
        ri = at("ri", [P, CH, 2, S], F32, area + 12288)
        av = at("av", [P, CH, S], F32, area + 36864)
        gate_w = at("gate_w", [P, CH, 2, P], F32, area + 51200)
        a_stage = at("a_stage", [P, T, 512], F32, area + 63488)
        yg = at("yg", [P, 2, 512], F32, temp_at)
        a_square = at("a_square", [P, 4, S], F32, temp_at + 4096)
        yT_hi = at("yT_hi", [P, CH, S], F32R, area + 51200)
        yT_lo = at("yT_lo", [P, CH, S], F32R, area + 12288)
        b_gate = at("b_gate", [P, T, 256], F32, area)
        b_prod = at("b_prod", [P, 2, T, 256], F32, area + 2048)
        b_conv = at("b_conv", [P, S], F32, area + 6144)
        b_y = at("b_y", [P, 2, S], F32, area + 7168)

        acc = ctx.enter_context(nc.psum_tensor("acc", [P, T, 2, UNIT], F32))
        aux = ctx.enter_context(nc.psum_tensor("aux", [P, 4, UNIT], F32))

        landed = [sem(f"landed{i}") for i in range(RING)]
        half_landed, half_hi, half_lo = sem("half_landed"), sem("half_hi"), sem("half_lo")
        hi_done = sem("hi_done")
        lo_done = sem("lo_done")
        group_used = sem("group_used")
        acc_full = [sem(f"acc_full{t}") for t in range(T)]
        acc_free_act = [sem(f"acc_free_act{t}") for t in range(T)]
        acc_free_dve = [sem(f"acc_free_dve{t}") for t in range(T)]
        gate_ready = [sem(f"gate_ready{t}") for t in range(T)]
        bank_full = sem("bank_full")
        bank_hi = sem("bank_hi")
        bank_free = sem("bank_free")
        consts_in = sem("consts_in")
        x_landed = [sem(f"x_landed{t}") for t in range(T)]
        ident_landed = sem("ident_landed")
        gain0_landed = sem("gain0_landed")
        gains_in = sem("gains_in")
        post_std = sem("post_std")
        pre_std = sem("pre_std")
        sqrt_loaded = sem("sqrt_loaded")
        x_ready = sem("x_ready")
        xn_ready = sem("xn_ready")
        act_step = sem("act_step")
        dve_step = sem("dve_step")
        pool_step = sem("pool_step")
        eps_set = sem("eps_set")
        ls_neg = sem("ls_neg")
        ls_exp = sem("ls_exp")
        decay_arg = sem("decay_arg")
        decay_done = sem("decay_done")
        dist_in_s = sem("dist_in_s")
        bias_in_s = [sem(f"bias_in{i}") for i in range(2)]
        bias_ready = sem("bias_ready")
        pad_set = sem("pad_set")
        rot_done = sem("rot_done")
        s_full = sem("s_full")
        s_reduced = sem("s_reduced")
        p_ready = sem("p_ready")
        pT_full = sem("pT_full")
        pT_copied = sem("pT_copied")
        o_full = sem("o_full")
        o_taken = sem("o_taken")
        ret_sq = sem("ret_sq")
        ret_std_s = sem("ret_std_s")
        y_ret_ready = sem("y_ret_ready")
        ret_acc_full = sem("ret_acc_full")
        merged_ready = sem("merged_ready")
        gate_w_in_s = sem("gate_w_in_s")
        conv_head = sem("conv_head")
        g_full = sem("g_full")
        g_taken = sem("g_taken")
        iu_ready = sem("iu_ready")
        et_ready = sem("et_ready")
        squares_ready = sem("squares_ready")
        v_ready = sem("v_ready")
        mult_ready = sem("mult_ready")
        yg_ready = sem("yg_ready")
        b_y_ready = sem("b_y_ready")
        stored = sem("stored")

        def wait_acc_free(pe, t, n):
            a = ACC_ORDER[:n].count("A")
            v = n - a
            if a:
                pe.wait_ge(acc_free_act[t], a)
            if v:
                pe.wait_ge(acc_free_dve[t], v)

        def act_frees(t, instruction):
            instruction.then_inc(acc_free_act[t], 1)

        block = ctx.enter_context(nc.Block())

        @block.sync
        def _(sp):
            sp.dma_start(x[:, 0, :], x_in[0:P, :]).then_inc(x_landed[0], 16)
            sp.dma_start(gain_pre[:], gains[0:1, :].partition_broadcast(P)).then_inc(gain0_landed, 16)
            for g in range(RING):
                if g == 0:
                    sp.dma_start(raw[:, 0, 0:GROUP // 2], weights[0][:, 0:GROUP // 2]).then_inc(half_landed, 16)
                    sp.dma_start(raw[:, 0, GROUP // 2:], weights[0][:, GROUP // 2:]).then_inc(landed[0], 16)
                else:
                    sp.dma_start(raw[:, g, :], weights[g]).then_inc(landed[g], 16)
                if g == 1:
                    sp.dma_start(x[:, 1, :], x_in[P:2 * P, :]).then_inc(x_landed[1], 16)
            with sp.Fori(1, NG // RING) as lap:
                for s in range(RING):
                    sp.wait_ge(lo_done, lap * RING + (s + 1 - RING))
                    sp.dma_start(raw[:, s, :], weights[bass.ds(lap * RING + s, 1)].rearrange("a p n -> p (a n)"))\
                        .then_inc(landed[s], 16)
            for g in range(NG // RING * RING, NG):
                sp.wait_ge(lo_done, g + 1 - RING)
                sp.dma_start(raw[:, g % RING, :], weights[g]).then_inc(landed[g % RING], 16)
            for t in range(T):
                for h in range(2):
                    sp.wait_ge(xn_ready, 2 * 2 * 5 + 2 * t + h + 1)
                    part = slice(h * DM // 2, (h + 1) * DM // 2)
                    sp.dma_start(out[t * P:(t + 1) * P, part], tmp[:, t, part]).then_inc(stored, 16)
            sp.wait_ge(stored, 16 * 2 * T)

        @block.gpsimd
        def _(pool):
            g = nc.gpsimd
            step = Chain(pool, pool_step)
            g.memset(eps1[:], EPS).then_inc(eps_set, 1)
            g.memset(eps4[:], 4 * EPS).then_inc(eps_set, 1)
            g.memset(zero[:], 0.0).then_inc(eps_set, 1)

            def load_gains(n, post, pre):
                if post is not None:
                    pool.dma_start(gain_post[:], gains[post:post + 1, :].partition_broadcast(P)).then_inc(gains_in, 16)
                pool.dma_start(gain_pre[:], gains[pre:pre + 1, :].partition_broadcast(P)).then_inc(gains_in, 16)

            for dst, src in ((colmask, colmask_in), (conv_a, conv_a_in), (conv_ab, conv_ab_in),
                             (conv_b, conv_b_in), (gate_b, gate_b_in), (rot, rot_in)):
                pool.dma_start(dst[:], src).then_inc(consts_in, 16)
            pool.dma_start(logit[:, 0:2 * RH], decay_in.partition_broadcast(P)).then_inc(consts_in, 16)
            pool.dma_start(logit[:, 2 * RH:], lam_in).then_inc(consts_in, 16)
            pool.wait_ge(xn_ready, 4)
            load_gains(1, 1, 2)

            def load_bias(s):
                t, h = s // NH, s % NH
                if s >= 2:
                    pool.wait_ge(bias_ready, s - 1)
                for r in range(2):
                    first = GR - 1 - 2 * t - r
                    pool.dma_start(bias_raw[r * GW:(r + 1) * GW, s % 2], bias_in[:, h, first:first + GR, :])\
                        .then_inc(bias_in_s[s % 2], 16)

            load_bias(0)
            load_bias(1)
            pool.wait_ge(xn_ready, 8)
            load_gains(2, 3, 4)
            pool.wait_ge(bank_full, FIRST_FILL["t1"] + 4)
            pool.dma_start(dist[:], dist_in).then_inc(dist_in_s, 16)
            g.memset(nqT[0][64:128], 0.0).then_inc(pad_set, 1)
            pool.wait_ge(pad_set, 1)
            g.memset(nqT[1][0:64], 0.0).then_inc(pad_set, 1)
            pool.wait_ge(pad_set, 2)

            def mask_bias(s):
                pool.wait_ge(bias_in_s[s % 2], 32 * (s // 2 + 1))
                if s == 0:
                    pool.wait_ge(consts_in, 16 * 8)
                if s >= 2:
                    pool.wait_ge(s_reduced, s - 1)
                g.tensor_tensor(bias_m[:, s % 2], bias_raw[:, s % 2],
                                colmask[:].unsqueeze(1).to_broadcast([P, GR, GW]), ALU.add).then_inc(bias_ready, 1)
                if s + 2 < T * NH:
                    load_bias(s + 2)

            mask_bias(0)
            mask_bias(1)
            for n in range(2 * T):
                t = n % T
                pool.wait_ge(acc_free_dve[t], ACC_ORDER[:FIRST_ACC["mix_in"] + 4 + n // T].count("V"))
                g.tensor_tensor(stage[:, t], stage[:, t], rot_b[:, t], ALU.add).then_inc(rot_done, 1)
                mask_bias(n + 2)
            for s in range(2 * T + 2, T * NH):
                mask_bias(s)
            pool.wait_ge(xn_ready, 12)
            load_gains(3, 5, 6)
            pool.wait_ge(x_ready, 2 * 2 + 1)
            pool.dma_start(gate_w[:], gate_w_in).then_inc(gate_w_in_s, 16)
            pool.wait_ge(xn_ready, 16)
            load_gains(4, None, 7)
            def input_gates(chunks):
                for ch in chunks:
                    pool.wait_ge(g_taken, ch + 1)
                    step(g.tensor_tensor(ri[:, ch, 1], ri[:, ch, 1], u[:, ch], ALU.mult))
                    g.tensor_tensor(ri[:, ch, 1], ri[:, ch, 1], u[:, ch], ALU.add).then_inc(iu_ready, 1)

            def squares(m):
                pool.wait_ge(et_ready, 8 * (m + 1))
                if m:
                    pool.wait_ge(v_ready, m)
                four = av[:, 4 * m:4 * m + 4]
                g.tensor_tensor(a_square[:], four, four, ALU.mult).then_inc(squares_ready, 1)

            input_gates(range(10))
            squares(0)
            input_gates(range(10, CH))
            squares(1)
            squares(2)
            late = FIRST_GROUP["a_out"] + 4
            pool.wait_ge(hi_done, late + 1)
            pool.wait_ge(lo_done, late)
            g.tensor_tensor(w_lo[:, late % RING], raw[:, late % RING], w_hi[:, late % RING].bitcast(F32), ALU.subtract)\
                .then_inc(lo_done, 1)
            pool.wait_ge(xn_ready, 20)
            load_gains(5, None, 8)

        @block.scalar
        def _(act):
            a = nc.scalar
            step = Chain(act, act_step)
            split = [0]

            def round_group(g, slot=None, wait_used=True):
                slot = g % RING if slot is None else slot
                lap = g // RING if isinstance(g, int) else None
                act.wait_ge(landed[slot], 16 * (lap + 1))
                if g >= RING:
                    kind, n = RELEASE[g - RING]
                    act.wait_ge({"used": group_used, "acc": acc_full[1], "ret": ret_acc_full}[kind], n)
                a.activation(w_hi[:, slot], raw[:, slot], ACT.Copy).then_inc(hi_done, 1)

            def round_to(n):
                while split[0] < min(n, NG):
                    round_group(split[0])
                    split[0] += 1

            def round_in_loop(base_group, i, i0, b, per=4):
                slot = (base_group + b) % RING
                lap0 = (base_group + b) // RING
                act.wait_ge(landed[slot], (i * (16 * per // RING)) + (16 * (lap0 + 1) - i0 * (16 * per // RING)))
                kind, n = RELEASE[base_group + b - RING]
                act.wait_ge({"used": group_used, "acc": acc_full[1]}[kind], i * (per // 2) + (n - i0 * (per // 2)))
                a.activation(w_hi[:, slot], raw[:, slot], ACT.Copy).then_inc(hi_done, 1)

            def take_hi(stage_name, n, dst, bank, source=None, scale=1.0):
                act.wait_ge(bank_full, FIRST_FILL[stage_name] + n + 1)
                a.activation(dst, source if source is not None else aux[:, bank], ACT.Copy, scale=scale)\
                    .then_inc(bank_hi, 1)

            def norm(n, post, factor, stage_name):
                def root(t, which):
                    c = which * 2 + t
                    step(a.activation(tmp[:, t], acc[:, t] if which == 0 else x[:, t], ACT.Square,
                                      accum_out=sumsq[:, c:c + 1]))
                    a.activation(std[:, c:c + 1], sumsq[:, c:c + 1], ACT.Sqrt, bias=eps1[:], scale=1.0 / DM)\
                        .then_inc(post_std if which == 0 else pre_std, 1)

                def first(t):
                    if post:
                        act.wait_ge(acc_full[t], FIRST_ACC[stage_name] + 1)
                        root(t, 0)

                def second(t):
                    if post:
                        act.wait_ge(x_ready, 2 * (n - 1) + t + 1)
                    elif n:
                        act.wait_ge(acc_free_dve[t], ACC_ORDER[:FIRST_ACC[stage_name] + 1].count("V"))
                    else:
                        act.wait_ge(x_landed[t], 16)
                    root(t, 1)

                def parts(t):
                    if n == 5:
                        return
                    for h in range(2):
                        take_hi(f"t{n}", 2 * t + h, xT_hi[:, 4 * h:4 * h + 4, t * P:(t + 1) * P], 2 * t + h,
                                source=aux[:, 2 * t + h].rearrange("p (c q) -> p c q", c=4))

                after = NEXT_GROUP[n]
                if n == 0:
                    second(0)
                    parts(0)
                    act.wait_ge(half_landed, 16)
                    a.activation(w_hi[:, 0, 0:GROUP // 2], raw[:, 0, 0:GROUP // 2], ACT.Copy).then_inc(half_hi, 1)
                    act.wait_ge(landed[0], 16)
                    a.activation(w_hi[:, 0, GROUP // 2:], raw[:, 0, GROUP // 2:], ACT.Copy).then_inc(hi_done, 1)
                    split[0] = 1
                    round_to(2)
                    second(1)
                    parts(1)
                    round_to(4)
                    return
                first(0)
                round_to(after + (1 if post else 2))
                second(0)
                round_to(after + (2 if post else 3))
                parts(0)
                first(1)
                round_to(after + 4)
                second(1)
                parts(1)

            def load_sqrt():
                a.activation(spare[:], zero[:], ACT.Sqrt).then_inc(sqrt_loaded, 1)
                loads[0] += 1
                act.wait_ge(sqrt_loaded, loads[0])

            loads = [0]
            act.dma_start(ident[:], ident_in).then_inc(ident_landed, 16)
            act.wait_ge(eps_set, 3)
            load_sqrt()
            norm(*NORMS[0])
            act.wait_ge(ls_neg, 1)
            a.activation(ls[1][:], ls[0][:], ACT.Exp).then_inc(ls_exp, 1)

            def swiglu(which, normed):
                st = f"{which}_in"
                g0, c0, f0 = FIRST_GROUP[st], FIRST_ACC[st], FIRST_FILL[st]
                prods0 = ACC_ORDER[:c0].count("V")

                def silu(j, par, t):
                    act.wait_ge(acc_full[t], c0 + 1 + j)
                    if not (isinstance(j, int) and j == 0 and prods0 == 0):
                        act.wait_ge(acc_free_dve[t], prods0 + j)
                    a.activation(silu_g[:, t], acc[:, t, par, 0:256], ACT.Silu).then_inc(gate_ready[t], 1)

                def hidden_hi(j, par):
                    act.wait_ge(bank_full, f0 + 1 + j)
                    dst = hT_hi[:, bass.ds(2 * j, 2), :] if not isinstance(j, int) else hT_hi[:, 2 * j:2 * j + 2, :]
                    a.activation(dst, aux[:, par].rearrange("p (c q) -> p c q", c=2), ACT.Copy).then_inc(bank_hi, 1)

                def column(j, par, rounds):
                    rounds()
                    silu(j, par, 0)
                    if not (isinstance(j, int) and j == 0):
                        hidden_hi(j - 1, 1 - par)
                    silu(j, par, 1)

                if g0 == 0:
                    silu(0, 0, 0)
                    round_to(g0 + 5)
                    silu(0, 0, 1)
                    silu(1, 1, 0)
                else:
                    silu(0, 0, 0)
                    silu(1, 1, 0)
                    round_to(g0 + 5)
                    silu(0, 0, 1)
                round_to(g0 + 6)
                silu(1, 1, 1)
                hidden_hi(0, 0)
                with act.Fori(1, 5) as i:
                    for b in range(2):
                        column(i * 2 + b, b, lambda: [round_in_loop(g0 + 6, i, 1, 2 * b + h) for h in range(2)])
                split[0] += 16
                column(10, 0, lambda: round_to(g0 + 24))
                round_to(g0 + 25)
                hidden_hi(10, 0)
                g1, n1 = FIRST_GROUP[f"{which}_out"], GROUPS[f"{which}_out"]
                round_to(g1 + n1)
                load_sqrt()

            swiglu("f1", 0)
            norm(*NORMS[1])

            g0, c0 = FIRST_GROUP["mix_in"], FIRST_ACC["mix_in"]
            gates = [11, 11]

            def exp_step(s):
                act.wait_ge(s_reduced, s + 1)
                if s >= 2:
                    act.wait_ge(pT_full, s - 1)
                a.activation(prob[:, s % 2], neg_s[:, s % 2], ACT.Exp, bias=neg_max[:, s:s + 1], scale=-1.0,
                             accum_out=prob_sum[:, s:s + 1]).then_inc(p_ready, 1)

            def ret_squares(h):
                act.wait_ge(bank_full, FIRST_FILL["rp"] + h + 1)
                for t in range(T):
                    i = a.activation(rot_b[:, t, 0:RV], aux[:, 0, t * RV:(t + 1) * RV], ACT.Square,
                                     accum_out=ret_sumsq[:, t, h:h + 1])
                    if t == 0:
                        step(i)
                    else:
                        i.then_inc(ret_sq, 1)
                act.wait_ge(ret_sq, h + 1)

            for c in range(13):
                for t in range(T):
                    par = c % 2
                    slot = 2 * c + t
                    round_to(g0 + 2 * c + 4 + t)
                    source = acc[:, t, par]
                    act.wait_ge(acc_full[t], c0 + c + 1)
                    if c < 2:
                        if c:
                            act.wait_ge(bank_full, FIRST_FILL["nq"] + t + 1)
                        i = a.activation(stage[:, t], source, ACT.Copy, scale=ND ** -0.5 if c == 0 else 1.0)
                        act_frees(t, i)
                    elif c == 2:
                        act_frees(t, a.activation(nv[:, t], source, ACT.Copy))
                    elif c in (5, 6):
                        act_frees(t, a.activation(rv[:, t, (c - 5) * 512:(c - 4) * 512], source, ACT.Copy))
                    elif c in (7, 8):
                        i = a.activation(y_ret[:, t, (c - 7) * 512:(c - 6) * 512], source, ACT.Tanh, scale=0.5)
                        i.then_inc(gate_ready[t], 1)
                    elif c >= 9:
                        dst, col = (m_ret, c - 9) if c < 11 else (m_na, c - 11)
                        act_frees(t, a.activation(dst[:, t, col * 512:(col + 1) * 512], source, ACT.Tanh, scale=0.5))
                    if 3 <= slot < 3 + RH:
                        h = slot - 3
                        act.wait_ge(decay_arg, h + 1)
                        a.activation(decay[:, h], decay[:, h], ACT.Exp).then_inc(decay_done, 1)
                    if 6 <= slot < 6 + 16:
                        exp_step(slot - 6)
                    if 18 <= slot < 22:
                        ret_squares(slot - 18)
                    if slot == 22:
                        a.activation(ret_std[:], ret_sumsq[:], ACT.Sqrt, bias=eps4[:], scale=4.0 / RV)\
                            .then_inc(ret_std_s, 1)
                    if slot == 24:
                        for tt in range(T):
                            take_hi("yna", tt, ynaT_hi[:, :, tt * P:(tt + 1) * P], 1 + tt,
                                    source=aux[:, 1 + tt].rearrange("p (c q) -> p c q", c=4))
                    if slot in (24, 25):
                        tt = slot - 24
                        for h in range(2):
                            bank = 0 if h == 0 else 3
                            take_hi("yret", 2 * tt + h, yretT_hi[:, 4 * h:4 * h + 4, tt * P:(tt + 1) * P], bank,
                                    source=aux[:, bank].rearrange("p (c q) -> p c q", c=4))
            round_to(FIRST_GROUP["mix_out"] + 1)
            for t in range(T):
                for h in range(2):
                    take_hi("merged", 2 * t + h, xT_hi[:, 4 * h:4 * h + 4, t * P:(t + 1) * P], 2 * t + h,
                            source=aux[:, 2 * t + h].rearrange("p (c q) -> p c q", c=4), scale=0.5)
                if t == 0:
                    round_to(FIRST_GROUP["mix_out"] + 4)
            load_sqrt()
            norm(*NORMS[2])

            swiglu("f2", 0)
            norm(*NORMS[3])

            g0, c0, f0 = FIRST_GROUP["a_in"], FIRST_ACC["a_in"], FIRST_FILL["a_in"]

            def conv_start(f):
                act.wait_ge(bank_full, f0 + f + 1)
                for k in range(2):
                    ch = 2 * f + k
                    a.activation(u[:, ch], aux[:, f % 2, k * S:(k + 1) * S], ACT.Identity,
                                 bias=conv_ab[:, ch:ch + 1], scale=conv_a[:, ch, 3:4]).then_inc(conv_head, 1)

            def gates_of(ch):
                act.wait_ge(g_full, ch + 1)
                for k in range(2):
                    i = a.activation(ri[:, ch, k], aux[:, 2 + ch % 2, k * S:(k + 1) * S],
                                     ACT.Tanh if k else ACT.Sigmoid, bias=gate_b[:, ch, k:k + 1],
                                     scale=0.5 if k else 1.0)
                    if k == 1:
                        i.then_inc(g_taken, 1)

            def exp_tanh(ch):
                act.wait_ge(g_taken, ch + 1)
                a.activation(av[:, ch], ri[:, ch, 0], ACT.Exp, scale=lrate[:, ch:ch + 1]).then_inc(et_ready, 1)
                a.activation(ri[:, ch, 0], ri[:, ch, 0], ACT.Tanh, scale=lrate[:, ch:ch + 1]).then_inc(et_ready, 1)

            def gated_hi(n):
                act.wait_ge(yg_ready, n + 1)
                a.activation(yT_hi[:, 2 * n:2 * n + 2, :], yg[:, n % 2].rearrange("p (c q) -> p c q", c=2), ACT.Copy)\
                    .then_inc(bank_hi, 1)

            def root(m):
                act.wait_ge(v_ready, m + 1)
                a.activation(ri[:, 4 * m:4 * m + 4, 0], ri[:, 4 * m:4 * m + 4, 0], ACT.Sqrt,
                             bias=zero[:], scale=-1.0).then_inc(mult_ready, 1)

            def stage_columns(c, t):
                act.wait_ge(acc_full[t], c0 + c + 1)
                if c:
                    act.wait_ge(bank_full, f0 + 2 * c)
                if c < 3:
                    act_frees(t, a.activation(a_stage[:, t], acc[:, t, c % 2], ACT.Copy))
                else:
                    a.activation(a_stage[:, t], acc[:, t, c % 2], ACT.Tanh, scale=0.5).then_inc(gate_ready[t], 1)

            def each(do, *numbers):
                for number in numbers:
                    do(number)

            def round_for(c, t):
                round_to(g0 + 2 * c + 4 + t)

            for t in range(T):
                round_for(0, t)
                stage_columns(0, t)
            round_for(1, 0)
            stage_columns(1, 0)
            each(conv_start, 0, 1)
            stage_columns(1, 1)
            round_for(1, 1)
            round_for(2, 0)
            each(gates_of, 0, 1)
            stage_columns(2, 0)
            each(conv_start, 2, 3)
            each(gates_of, 2, 3)
            round_for(2, 1)
            stage_columns(2, 1)
            round_for(3, 0)
            each(conv_start, 4, 5)
            stage_columns(3, 0)
            each(gates_of, 4, 5)
            each(gates_of, 6, 7)
            stage_columns(3, 1)
            round_for(3, 1)
            each(gates_of, 8, 9)
            round_for(4, 0)
            each(gates_of, 10, 11)
            each(exp_tanh, 0, 1, 2, 3)
            stage_columns(4, 0)
            each(exp_tanh, 4, 5, 6, 7)
            root(0)
            round_for(4, 1)
            stage_columns(4, 1)
            each(gated_hi, 0, 1)
            stage_columns(5, 0)
            round_for(5, 0)
            each(exp_tanh, 8, 9)
            stage_columns(5, 1)
            each(exp_tanh, 10, 11)
            round_for(5, 1)
            root(1)
            round_to(FIRST_GROUP["a_out"] + 4)
            each(gated_hi, 2, 3)
            round_to(FIRST_GROUP["a_out"] + 5)
            root(2)
            round_to(FIRST_GROUP["a_out"] + 6)
            each(gated_hi, 4, 5)
            round_to(FIRST_GROUP["b_in"] + 1)
            load_sqrt()
            norm(*NORMS[4])

            g0, c0, f0 = FIRST_GROUP["b_in"], FIRST_ACC["b_in"], FIRST_FILL["b_in"]
            prods0 = ACC_ORDER[:c0].count("V")

            def b_gates(j, par, t):
                act.wait_ge(acc_full[t], c0 + 1 + j)
                act.wait_ge(acc_free_dve[t], prods0 + j)
                a.activation(b_gate[:, t, 0:P], acc[:, t, par, 2 * P:3 * P], ACT.Silu).then_inc(gate_ready[t], 1)
                a.activation(b_gate[:, t, P:2 * P], acc[:, t, par, 3 * P:4 * P], ACT.Copy).then_inc(gate_ready[t], 1)

            def b_hi(j, par):
                act.wait_ge(b_y_ready, 1 + j)
                dst = yT_hi[:, j, :] if isinstance(j, int) else yT_hi[:, bass.ds(j, 1), :].rearrange("p a q -> p (a q)")
                a.activation(dst, b_y[:, par], ACT.Copy).then_inc(bank_hi, 1)

            def b_column(j, par, rounds):
                rounds()
                b_gates(j, par, 0)
                if not (isinstance(j, int) and j == 0):
                    b_hi(j - 1, 1 - par)
                b_gates(j, par, 1)

            b_gates(0, 0, 0)
            b_gates(1, 1, 0)
            round_to(g0 + 5)
            b_gates(0, 0, 1)
            round_to(g0 + 6)
            b_gates(1, 1, 1)
            b_hi(0, 0)
            with act.Fori(1, 6) as i:
                for b in range(2):
                    b_column(i * 2 + b, b, lambda: [round_in_loop(g0 + 6, i, 1, 2 * b + h) for h in range(2)])

            split[0] += 20
            round_to(FIRST_GROUP["b_out"] + 5)
            b_hi(11, 1)
            round_to(NG)
            load_sqrt()
            norm(*NORMS[5])

        @block.vector
        def _(dve):
            v = nc.vector
            step = Chain(dve, dve_step)
            split = [0]

            def low_group(g, slot):
                dve.wait_ge(hi_done, g + 1)
                v.tensor_tensor(w_lo[:, slot], raw[:, slot], w_hi[:, slot].bitcast(F32), ALU.subtract)\
                    .then_inc(lo_done, 1)

            def low_to(n):
                while split[0] < min(n, NG):
                    low_group(split[0], split[0] % RING)
                    split[0] += 1

            def low_half(g, half):
                assert split[0] == g
                slot, part = g % RING, slice(half * GROUP // 2, (half + 1) * GROUP // 2)
                if g == 0 and half == 0:
                    dve.wait_ge(half_hi, 1)
                else:
                    dve.wait_ge(hi_done, g + 1)
                i = v.tensor_tensor(w_lo[:, slot, part], raw[:, slot, part], w_hi[:, slot, part].bitcast(F32),
                                    ALU.subtract)
                if half:
                    i.then_inc(lo_done, 1)
                    split[0] += 1
                elif g == 0:
                    i.then_inc(half_lo, 1)

            def low_in_loop(base_group, i, i0, b, per=4):
                low_group(i * per + (base_group + b - i0 * per), (base_group + b) % RING)

            def take_lo(stage_name, q, dst, hi, source, scale=None):
                dve.wait_ge(bank_hi, FIRST_SPLIT[stage_name] + q + 1)
                if scale is None:
                    i = v.tensor_tensor(dst, source, hi.bitcast(F32), ALU.subtract)
                else:
                    i = v.scalar_tensor_tensor(dst, source, scale, hi.bitcast(F32), ALU.mult, ALU.subtract)
                i.then_inc(bank_free, 1)

            def norm(n, post, factor, stage_name):
                posts = {1: 0, 2: 1, 3: 2}
                after = NEXT_GROUP[n]
                for t in range(T):
                    if n:
                        if t == 0:
                            dve.wait_ge(gains_in, (32, 64, 96, 112, 128)[n - 1])
                        if post:
                            dve.wait_ge(post_std, 2 * posts[n] + t + 1)
                            step(v.reciprocal(rstd[:, t:t + 1], std[:, t:t + 1]))
                            i = v.scalar_tensor_tensor(tmp[:, t], acc[:, t].rearrange("p h n -> p (h n)"),
                                                       rstd[:, t:t + 1], gain_post[:], ALU.mult, ALU.mult)
                            i.then_inc(acc_free_dve[t], 1)
                            dve.wait_ge(acc_free_dve[t], ACC_ORDER[:FIRST_ACC[stage_name] + 1].count("V"))
                            v.scalar_tensor_tensor(x[:, t], tmp[:, t], factor, x[:, t], ALU.mult, ALU.add)\
                                .then_inc(x_ready, 1)
                        else:
                            dve.wait_ge(acc_full[t], FIRST_ACC[stage_name] + 1)
                            v.tensor_tensor(x[:, t], acc[:, t].rearrange("p h n -> p (h n)"), x[:, t], ALU.add)\
                                .then_inc(acc_free_dve[t], 1)
                        if t == 1:
                            low_to(after + 3)
                        elif post:
                            low_to(after + 1)
                        elif n < 5:
                            low_half(after + 1, 0)
                    elif t == 0:
                        dve.wait_ge(gain0_landed, 16)
                    dve.wait_ge(pre_std, 2 * n + t + 1)
                    step(v.reciprocal(rstd[:, 2 + t:3 + t], std[:, 2 + t:3 + t]))
                    for h in range(2):
                        part = slice(h * 512, (h + 1) * 512)
                        v.scalar_tensor_tensor(tmp[:, t, part], x[:, t, part], rstd[:, 2 + t:3 + t],
                                               gain_pre[:, part], ALU.mult, ALU.mult).then_inc(xn_ready, 1)
                    if n and t == 1:
                        low_to(after + 4)
                    elif post:
                        low_to(after + 2)
                    elif n == 4:
                        low_half(after + 1, 1)
                    if n < 5:
                        for h in range(2):
                            cols = slice(t * P, (t + 1) * P)
                            take_lo(f"t{n}", 2 * t + h, xT_lo[:, 4 * h:4 * h + 4, cols],
                                    xT_hi[:, 4 * h:4 * h + 4, cols],
                                    aux[:, 2 * t + h].rearrange("p (c q) -> p c q", c=4))
                    if n == 0 and t == 0:
                        low_half(0, 0)
                        low_half(0, 1)
                        low_to(2)
                    if n == 0 and t == 1:
                        low_to(4)

            norm(*NORMS[0])
            dve.wait_ge(consts_in, 16 * 8)
            step(v.tensor_scalar(ls[2][:], logit[:], -1.0, None, ALU.mult))
            v.tensor_tensor(ls[0][:], logit[:], ls[2][:], ALU.min).then_inc(ls_neg, 1)
            dve.wait_ge(ls_exp, 1)
            step(v.tensor_scalar(ls[2][:], ls[1][:], 2.0, None, ALU.add))
            step(v.reciprocal(ls[3][:], ls[2][:]))
            step(v.tensor_tensor(ls[2][:], ls[1][:], ls[3][:], ALU.mult))
            step(v.tensor_tensor(ls[3][:], ls[2][:], ls[2][:], ALU.mult))
            step(v.tensor_scalar(ls[4][:], ls[3][:], 1.0 / 17, None, ALU.mult))
            for k in (15, 13, 11, 9, 7, 5, 3):
                step(v.scalar_tensor_tensor(ls[4][:], ls[4][:], 1.0 / k, ls[3][:], ALU.add, ALU.mult))
            step(v.scalar_tensor_tensor(ls[4][:], ls[4][:], 1.0, ls[2][:], ALU.add, ALU.mult))
            step(v.tensor_scalar(ls[0][:], logit[:], 0.0, None, ALU.min))
            step(v.scalar_tensor_tensor(ls[1][:], ls[4][:], -2.0, ls[0][:], ALU.mult, ALU.add))
            log_gamma = ls[1]
            step(v.tensor_scalar(lrate[:], log_gamma[:, 2 * RH:], 8.0, None, ALU.mult))
            step(v.tensor_scalar(gate_b[:, :, 1], gate_b[:, :, 1], 0.5, None, ALU.mult))

            def swiglu(which):
                st = f"{which}_in"
                g0, f0, q0 = FIRST_GROUP[st], FIRST_FILL[st], FIRST_SPLIT[st]
                gate0 = {"f1": 0, "f2": GATES_F2}[which]

                def up(j, par, t):
                    dve.wait_ge(gate_ready[t], gate0 + 1 + j)
                    if not (isinstance(j, int) and j < 2):
                        dve.wait_ge(bank_full, f0 - 1 + j)
                    v.tensor_tensor(prod[:, par, t], acc[:, t, par, 256:512], silu_g[:, t], ALU.mult)\
                        .then_inc(acc_free_dve[t], 1)

                def hidden_lo(j, par):
                    chunks = slice(2 * j, 2 * j + 2) if isinstance(j, int) else bass.ds(2 * j, 2)
                    dve.wait_ge(bank_hi, q0 + 1 + j)
                    v.tensor_tensor(hT_lo[:, chunks, :], aux[:, par].rearrange("p (c q) -> p c q", c=2),
                                    hT_hi[:, chunks, :].bitcast(F32), ALU.subtract).then_inc(bank_free, 1)

                def column(j, par, lows):
                    lows()
                    up(j, par, 0)
                    if not (isinstance(j, int) and j == 0):
                        hidden_lo(j - 1, 1 - par)
                    up(j, par, 1)

                if g0 == 0:
                    up(0, 0, 0)
                    low_to(g0 + 5)
                    up(0, 0, 1)
                    up(1, 1, 0)
                else:
                    up(0, 0, 0)
                    up(1, 1, 0)
                    low_to(g0 + 5)
                    up(0, 0, 1)
                low_to(g0 + 6)
                up(1, 1, 1)
                hidden_lo(0, 0)
                with dve.Fori(1, 5) as i:
                    for b in range(2):
                        column(i * 2 + b, b, lambda: [low_in_loop(g0 + 6, i, 1, 2 * b + h) for h in range(2)])
                split[0] += 16
                column(10, 0, lambda: low_to(g0 + 24))
                low_to(g0 + 25)
                hidden_lo(10, 0)
                low_to(FIRST_GROUP[f"{which}_out"] + GROUPS[f"{which}_out"])

            GATES_F2 = 11 + 2
            swiglu("f1")
            norm(*NORMS[1])

            g0, c0 = FIRST_GROUP["mix_in"], FIRST_ACC["mix_in"]

            def copy_fill(name, n, copies):
                dve.wait_ge(bank_full, FIRST_FILL[name] + n + 1)
                for k, (dst, src) in enumerate(copies):
                    i = v.tensor_copy(dst, src)
                i.then_inc(bank_free, 1)

            def heads_of(bank):
                return aux[:, bank].rearrange("p (c q) -> p c q", c=4)

            def rotate(t, par, n):
                source = acc[:, t, par].rearrange("p (h s i) -> p h s i", h=RH, s=2)
                turned = rot_b[:, t].rearrange("p (h s i) -> p h s i", h=RH, s=2)
                v.tensor_tensor(stage[:, t].rearrange("p (a i) -> p a i", a=2 * RH),
                                acc[:, t, par].rearrange("p (a i) -> p a i", a=2 * RH),
                                rot[:, t, 0:1].to_broadcast([P, 2 * RH, 64]), ALU.mult)
                v.tensor_tensor(turned[:, :, 0], source[:, :, 1], rot[:, t, 2:3].to_broadcast([P, RH, 64]), ALU.mult)
                i = v.tensor_tensor(turned[:, :, 1], source[:, :, 0], rot[:, t, 1:2].to_broadcast([P, RH, 64]),
                                    ALU.mult)
                i.then_inc(acc_free_dve[t], 1)

            for c in range(13):
                for t in range(T):
                    par, slot = c % 2, 2 * c + t
                    if 2 <= slot < 2 + RH:
                        dve.wait_ge(dist_in_s, 16)
                        for h in (slot - 2,):
                            step(v.tensor_scalar(decay[:, h], dist[:, 0], log_gamma[:, h:h + 1], None, ALU.mult))
                            v.scalar_tensor_tensor(decay[:, h].rearrange("p a q -> p (a q)"),
                                                   dist[:, 1].rearrange("p a q -> p (a q)"),
                                                   log_gamma[:, RH + h:RH + h + 1],
                                                   decay[:, h].rearrange("p a q -> p (a q)"), ALU.mult, ALU.add)\
                                .then_inc(decay_arg, 1)
                    if slot == 3:
                        for tt in range(T):
                            cols = slice(tt * P, (tt + 1) * P)
                            if tt == 0:
                                dve.wait_ge(pad_set, 2)
                            copy_fill("nq", tt, [(nqT[e][64 * e:64 * e + 64, :, cols],
                                                  heads_of(tt)[64 * e:64 * e + 64]) for e in range(2)])
                    if slot == 5:
                        for tt in range(T):
                            copy_fill("nk", tt, [(nkT[:, :, tt * P:(tt + 1) * P], heads_of(tt))])
                    low_to(g0 + 2 * c + 4 + t)
                    if c in (3, 4):
                        dve.wait_ge(acc_full[t], c0 + c + 1)
                        if c == 3:
                            dve.wait_ge(bank_full, FIRST_FILL["nk"] + t + 1)
                        else:
                            dve.wait_ge(bank_full, FIRST_FILL["rq"] + t + 1)
                        rotate(t, par, T * (c - 3) + t)
                    if c in (7, 8):
                        dve.wait_ge(gate_ready[t], 11 + c - 6)
                        part = y_ret[:, t, (c - 7) * 512:(c - 6) * 512]
                        v.scalar_tensor_tensor(part, part, 1.0, acc[:, t, par], ALU.add, ALU.mult)\
                            .then_inc(acc_free_dve[t], 1)
                        if c == 8 and t == 1:
                            for tt in range(T):
                                dve.wait_ge(acc_free_dve[tt], ACC_ORDER[:c0 + c + 1].count("V"))
                    if 8 <= slot < 12:
                        name, dst = ("rq", rqT) if slot < 10 else ("rk", rkT)
                        copy_fill(name, t, [(dst[:, :, t * P:(t + 1) * P], heads_of(0))])
                    if 12 <= slot < 16:
                        h = slot - 12
                        dve.wait_ge(bank_full, FIRST_FILL["rs"] + h + 1)
                        if h == 0:
                            dve.wait_ge(decay_done, RH)
                        flat = decay[:, h].rearrange("p a q -> p (a q)")
                        v.scalar_tensor_tensor(flat, aux[:, 0], RQ ** -0.5, flat, ALU.mult, ALU.mult)\
                            .then_inc(bank_free, 1)
                    s = slot - 6
                    if 0 <= s - 1 < 16:
                        dve.wait_ge(pT_full, s)
                        if s - 1 >= 2:
                            dve.wait_ge(o_full, s - 2)
                        v.tensor_copy(probT[:, (s - 1) % 2].rearrange("p a q -> p (a q)"), aux[:, 2, 0:S])\
                            .then_inc(pT_copied, 1)
                    if 0 <= s - 2 < 16:
                        n = s - 2
                        dve.wait_ge(o_full, n + 1)
                        dve.wait_ge(p_ready, n + 1)
                        step(v.reciprocal(prob_rec[:, n:n + 1], prob_sum[:, n:n + 1]))
                        h = n % NH
                        v.tensor_scalar(y_na[:, n // NH, h * ND:(h + 1) * ND], aux[:, 3, 0:ND],
                                        prob_rec[:, n:n + 1], None, ALU.mult).then_inc(o_taken, 1)
                    if 0 <= s < 16:
                        dve.wait_ge(s_full, s + 1)
                        dve.wait_ge(bias_ready, s + 1)
                        if s >= 2:
                            dve.wait_ge(p_ready, s - 1)
                        v.tensor_tensor_reduce(out=neg_s[:, s % 2], in0=aux[:, 1, 0:S],
                                               in1=bias_m[:, s % 2].rearrange("p a q -> p (a q)"), scale=-1.0,
                                               scalar=3e38, op0=ALU.add, op1=ALU.min,
                                               accum_out=neg_max[:, s:s + 1]).then_inc(s_reduced, 1)
                    if 18 <= slot < 22:
                        h = slot - 18
                        dve.wait_ge(ret_sq, h + 1)
                        for tt in range(T):
                            part = y_ret[:, tt, h * RV:(h + 1) * RV]
                            i = v.tensor_tensor(part, part, aux[:, 0, tt * RV:(tt + 1) * RV], ALU.mult)
                        i.then_inc(bank_free, 1)
                        if h == RH - 1:
                            dve.wait_ge(bank_free, FIRST_FILL["rp"] + RH)
                    if slot == 22:
                        dve.wait_ge(ret_std_s, 1)
                        step(v.reciprocal(ret_rstd[:], ret_std[:]))
                        for tt in range(T):
                            for h in range(RH):
                                part = y_ret[:, tt, h * RV:(h + 1) * RV]
                                i = v.tensor_scalar(part, part, ret_rstd[:, tt, h:h + 1], None, ALU.mult)
                            i.then_inc(y_ret_ready, 1)
                    if slot == 24:
                        for tt in range(T):
                            cols = slice(tt * P, (tt + 1) * P)
                            take_lo("yna", tt, ynaT_lo[:, :, cols], ynaT_hi[:, :, cols], heads_of(1 + tt))
                    if slot in (24, 25):
                        tt = slot - 24
                        cols = slice(tt * P, (tt + 1) * P)
                        for h in range(2):
                            chunks = slice(4 * h, 4 * h + 4)
                            take_lo("yret", 2 * tt + h, yretT_lo[:, chunks, cols], yretT_hi[:, chunks, cols],
                                    heads_of(0 if h == 0 else 3))
            low_to(FIRST_GROUP["ret_out"] + 4)
            for t in range(T):
                dve.wait_ge(acc_full[t], FIRST_ACC["na_out"] + 1)
                dve.wait_ge(acc_free_act[t], ACC_ORDER[:FIRST_ACC["na_out"]].count("A"))
                v.scalar_tensor_tensor(m_na[:, t], m_na[:, t], 1.0, acc[:, t].rearrange("p h n -> p (h n)"),
                                       ALU.add, ALU.mult).then_inc(acc_free_dve[t], 1)
            for t in range(T):
                dve.wait_ge(acc_free_dve[t], ACC_ORDER[:FIRST_ACC["na_out"] + 1].count("V"))
                if t == 1:
                    low_to(FIRST_GROUP["mix_out"] + 2)
                dve.wait_ge(ret_acc_full, t + 1)
                for h in range(2):
                    part = slice(h * 512, (h + 1) * 512)
                    step(v.scalar_tensor_tensor(m_ret[:, t, part], m_ret[:, t, part], 1.0, aux[:, 2 * t + h],
                                                ALU.add, ALU.mult))
                    v.tensor_tensor(m_ret[:, t, part], m_ret[:, t, part], m_na[:, t, part], ALU.add)\
                        .then_inc(merged_ready, 1)
                if t == 0:
                    low_to(FIRST_GROUP["mix_out"] + 1)
                else:
                    low_to(FIRST_GROUP["mix_out"] + 4)
                for h in range(2):
                    cols, chunks = slice(t * P, (t + 1) * P), slice(4 * h, 4 * h + 4)
                    take_lo("merged", 2 * t + h, xT_lo[:, chunks, cols], xT_hi[:, chunks, cols], heads_of(2 * t + h),
                            scale=0.5)
            norm(*NORMS[2])

            swiglu("f2")
            norm(*NORMS[3])

            g0, c0, f0 = FIRST_GROUP["a_in"], FIRST_ACC["a_in"], FIRST_FILL["a_in"]
            gate0 = GATES_F2 + 11

            def conv_rest(f):
                dve.wait_ge(conv_head, 2 * f + 2)
                for lag in (1, 2, 3):
                    for k in range(2):
                        ch = 2 * f + k
                        i = v.scalar_tensor_tensor(u[:, ch, lag:], aux[:, f % 2, k * S:(k + 1) * S - lag],
                                                   conv_a[:, ch, 3 - lag:4 - lag], u[:, ch, lag:], ALU.mult, ALU.add)
                        if k == 1 and lag < 3:
                            step(i)
                i.then_inc(bank_free, 1)

            def rates(m):
                dve.wait_ge(squares_ready, m + 1)
                v.scalar_tensor_tensor(ri[:, 4 * m:4 * m + 4, 0], a_square[:], 1.0, ri[:, 4 * m:4 * m + 4, 0],
                                       ALU.add, ALU.mult).then_inc(v_ready, 1)

            def scans(m):
                four = slice(4 * m, 4 * m + 4)
                dve.wait_ge(mult_ready, m + 1)
                dve.wait_ge(iu_ready, 4 * m + 4)
                step(v.scalar_tensor_tensor(ri[:, four, 1], ri[:, four, 1], 0.5, ri[:, four, 0], ALU.mult, ALU.mult))
                for ch in range(4 * m, 4 * m + 4):
                    i = v.tensor_tensor_scan(u[:, ch], av[:, ch], ri[:, ch, 1], 0.0, ALU.mult, ALU.add)
                step(i)

            def gate_fill_bank(n):
                return (0, 1, 2, 3, 0, 1)[n]

            def gated(n):
                dve.wait_ge(bank_full, f0 + 6 + n + 1)
                if n >= 2:
                    dve.wait_ge(bank_free, f0 + 6 + n - 1)
                v.scalar_tensor_tensor(yg[:, n % 2], aux[:, gate_fill_bank(n)], 0.5,
                                       u[:, 2 * n:2 * n + 2].rearrange("p c q -> p (c q)"), ALU.mult, ALU.mult)\
                    .then_inc(yg_ready, 1)

            def gated_lo(n):
                take_lo("gate", n, yT_lo[:, 2 * n:2 * n + 2].rearrange("p c q -> p (c q)"),
                        yT_hi[:, 2 * n:2 * n + 2].rearrange("p c q -> p (c q)"), yg[:, n % 2])

            def low_for(c, t):
                low_to(g0 + 2 * c + 4 + t)

            def branch_gate(c, t):
                dve.wait_ge(gate_ready[t], gate0 + c - 2)
                v.scalar_tensor_tensor(a_stage[:, t], a_stage[:, t], 1.0, acc[:, t, c % 2], ALU.add, ALU.mult)\
                    .then_inc(acc_free_dve[t], 1)

            low_for(0, 0)
            low_for(0, 1)
            for c in (1, 2, 3):
                low_for(c, 0)
                conv_rest(2 * c - 2)
                conv_rest(2 * c - 1)
                if c < 3:
                    low_for(c, 1)
            branch_gate(3, 0)
            branch_gate(3, 1)
            low_for(3, 1)
            low_for(4, 0)
            rates(0)
            branch_gate(4, 0)
            scans(0)
            gated(0)
            branch_gate(4, 1)
            gated(1)
            low_for(4, 1)
            gated_lo(0)
            branch_gate(5, 0)
            gated_lo(1)
            low_for(5, 0)
            branch_gate(5, 1)
            rates(1)
            low_to(FIRST_GROUP["a_out"] + 3)
            scans(1)
            gated(2)
            gated(3)
            gated_lo(2)
            rates(2)
            gated_lo(3)
            low_to(FIRST_GROUP["a_out"] + 4)
            scans(2)
            gated(4)
            gated(5)
            gated_lo(4)
            split[0] += 1
            dve.wait_ge(lo_done, split[0])
            gated_lo(5)
            low_to(FIRST_GROUP["a_out"] + 6)
            low_to(FIRST_GROUP["b_in"] + 1)
            norm(*NORMS[4])

            g0, c0, f0, q0 = FIRST_GROUP["b_in"], FIRST_ACC["b_in"], FIRST_FILL["b_in"], FIRST_SPLIT["b_in"]
            gate0 = GATES_F2 + 11 + 3

            def b_products(j, par, t):
                dve.wait_ge(gate_ready[t], j * 2 + (gate0 + 2))
                if not (isinstance(j, int) and j < 2):
                    dve.wait_ge(bank_full, f0 - 1 + j)
                v.tensor_tensor(b_prod[:, par, t], acc[:, t, par, 0:2 * P], b_gate[:, t], ALU.mult)\
                    .then_inc(acc_free_dve[t], 1)

            def tap(j, k):
                if isinstance(j, int):
                    return conv_b[:, j, k:k + 1]
                return conv_b[:, bass.ds(j, 1), k:k + 1].rearrange("p a b -> p (a b)")

            def b_short_conv(j, par):
                dve.wait_ge(bank_full, f0 + 1 + j)
                if not (isinstance(j, int) and j == 0):
                    dve.wait_ge(b_y_ready, j)
                p = aux[:, par, S:2 * S]
                step(v.tensor_scalar(b_conv[:], p, tap(j, 2), None, ALU.mult))
                step(v.scalar_tensor_tensor(b_conv[:, 1:], p[:, 0:S - 1], tap(j, 1), b_conv[:, 1:], ALU.mult, ALU.add))
                step(v.scalar_tensor_tensor(b_conv[:, 2:], p[:, 0:S - 2], tap(j, 0), b_conv[:, 2:], ALU.mult, ALU.add))
                v.tensor_tensor(b_y[:, par], aux[:, par, 0:S], b_conv[:], ALU.mult).then_inc(b_y_ready, 1)

            def b_lo(j, par):
                dve.wait_ge(bank_hi, q0 + 1 + j)
                one = (slice(j, j + 1) if isinstance(j, int) else bass.ds(j, 1))
                v.tensor_tensor(yT_lo[:, one, :].rearrange("p a q -> p (a q)"), b_y[:, par],
                                yT_hi[:, one, :].rearrange("p a q -> p (a q)").bitcast(F32), ALU.subtract)\
                    .then_inc(bank_free, 1)

            def b_column(j, par, lows):
                lows()
                b_products(j, par, 0)
                if not (isinstance(j, int) and j == 0):
                    b_short_conv(j - 1, 1 - par)
                b_products(j, par, 1)
                if not (isinstance(j, int) and j == 0):
                    b_lo(j - 1, 1 - par)

            b_products(0, 0, 0)
            b_products(1, 1, 0)
            low_to(g0 + 5)
            b_products(0, 0, 1)
            low_to(g0 + 6)
            b_products(1, 1, 1)
            b_short_conv(0, 0)
            b_lo(0, 0)
            before, per_lap = step.n, 2 * 3
            with dve.Fori(1, 6) as i:
                step.base = (i - 1) * per_lap
                for b in range(2):
                    b_column(i * 2 + b, b, lambda: [low_in_loop(g0 + 6, i, 1, 2 * b + h) for h in range(2)])
                assert step.n == before + per_lap
            step.base = 0
            step.n = before + 5 * per_lap
            split[0] += 20
            low_to(FIRST_GROUP["b_out"] + 4)
            b_short_conv(11, 1)
            b_lo(11, 1)
            low_to(NG)
            norm(*NORMS[5])

        @block.tensor
        def _(pe):
            m = nc.tensor

            def product(dst, hi, lo, k, t, slot, unit, first, last):
                cols = slice(t * P, (t + 1) * P)
                w = slice(unit * UNIT, (unit + 1) * UNIT)
                m.matmul(dst, hi[:, k, cols], w_hi[:, slot, w], start=first, stop=False)
                m.matmul(dst, hi[:, k, cols], w_lo[:, slot, w], start=False, stop=False)
                return m.matmul(dst, lo[:, k, cols], w_hi[:, slot, w], start=False, stop=last)

            def column_tile(g, slot0, par, t, before_half=None):
                for half in range(2):
                    if before_half:
                        before_half(half)
                    by_halves = isinstance(g, int) and g == 0 and t == 0 and half == 0
                    if by_halves:
                        pe.wait_ge(half_lo, 1)
                    elif t == 0:
                        pe.wait_ge(lo_done, g + (half + 1))
                    for unit in range(4):
                        if by_halves and unit == 2:
                            pe.wait_ge(lo_done, 1)
                        i = product(acc[:, t, par], xT_hi, xT_lo, 4 * half + unit, t, (slot0 + half) % RING, unit,
                                    half == 0 and unit == 0, half == 1 and unit == 3)
                    if t == 1 and half == 0:
                        i.then_inc(group_used, 1)
                i.then_inc(acc_full[t], 1)

            def wait_operand(fills):
                pe.wait_ge(bank_free, fills)

            def out_tile(st, n, t, hi, lo, chunks, target, done, between=None):
                g = FIRST_GROUP[st] + n
                if t == 0:
                    pe.wait_ge(lo_done, g + 1)
                for kk in range(2):
                    if kk and between:
                        between()
                    k = 2 * n + kk
                    for half in range(2):
                        i = product(target(t, half), hi, lo, k, t, g % RING, 2 * kk + half, k == 0, k == chunks - 1)
                if n == chunks // 2 - 1:
                    i.then_inc(*done(t))
                elif t == 1:
                    i.then_inc(group_used, 1)

            def acc_target(t, half):
                return acc[:, t, half]

            def norm_transposes(n):
                def run(t):
                    for h in range(2):
                        pe.wait_ge(xn_ready, 4 * n + 2 * t + h + 1)
                        if FIRST_FILL[f"t{n}"]:
                            pe.wait_ge(bank_free, FIRST_FILL[f"t{n}"])
                        for c in range(4):
                            i = m.transpose(aux[:, 2 * t + h, c * P:(c + 1) * P],
                                            tmp[:, t, (4 * h + c) * P:(4 * h + c + 1) * P], ident[:])
                        i.then_inc(bank_full, 1)
                return run

            def out_stage(st, hi, lo, chunks, wait_chunk=lambda n: None, after_first=lambda: None, norm=None,
                          last=3):
                groups = chunks // 2
                blocks = [(0, 1)] + [(n,) for n in range(2, groups - last)] + [tuple(range(groups - last, groups))]
                for block in blocks:
                    for t in range(T):
                        if block[0] == 0:
                            wait_acc_free(pe, t, FIRST_ACC[st])
                        for n in block:
                            if t == 0:
                                wait_chunk(n)
                            end = norm if t == 1 and n == groups - 1 else None
                            out_tile(st, n, t, hi, lo, chunks, acc_target, lambda t: (acc_full[t], 1),
                                     (lambda: norm_transposes(norm)(0)) if end else None)
                    if block[0] == 0:
                        after_first()

            def first_columns(n, st):
                run = norm_transposes(n)
                g0 = FIRST_GROUP[st]

                def operand(t):
                    return lambda half: wait_operand(FIRST_FILL[f"t{n}"] + 2 * t + half + 1)

                if n == 0:
                    run(0)
                wait_acc_free(pe, 0, FIRST_ACC[st])

                def first_half(half):
                    if half and n == 0:
                        run(1)
                    operand(0)(half)

                column_tile(g0, g0 % RING, 0, 0, first_half)
                if n == 0:
                    column_tile(g0, g0 % RING, 0, 1, operand(1))
                    for t in range(T):
                        column_tile(g0 + 2, (g0 + 2) % RING, 1, t)
                    return
                column_tile(g0 + 2, (g0 + 2) % RING, 1, 0, lambda half: run(1) if half else None)
                wait_acc_free(pe, 1, FIRST_ACC[st])
                column_tile(g0, g0 % RING, 0, 1, operand(1))
                column_tile(g0 + 2, (g0 + 2) % RING, 1, 1)

            def swiglu(which, n):
                st = f"{which}_in"
                g0, c0, f0 = FIRST_GROUP[st], FIRST_ACC[st], FIRST_FILL[st]
                prods0 = ACC_ORDER[:c0].count("V")
                n_act = ACC_ORDER[:c0].count("A")
                n_dve = c0 - n_act

                def hidden_transposes(j, par):
                    for t in range(T):
                        pe.wait_ge(acc_free_dve[t], prods0 + 1 + j)
                    pe.wait_ge(bank_free, f0 if isinstance(j, int) and j < 2 else f0 - 1 + j)
                    for c in range(2):
                        for t in range(T):
                            i = m.transpose(aux[:, par, c * S + t * P:c * S + (t + 1) * P],
                                            prod[:, par, t, c * P:(c + 1) * P], ident[:])
                    i.then_inc(bank_full, 1)

                def column(j, par):
                    for t in range(T):
                        pe.wait_ge(acc_free_dve[t], n_dve - 1 + j)
                        column_tile(g0 + 2 * j, (g0 + 2 * par) % RING, par, t)
                        if t == 0:
                            hidden_transposes(j - 1, 1 - par)

                first_columns(n, st)
                hidden_transposes(0, 0)
                with pe.Fori(1, 5) as i:
                    for b in range(2):
                        column(i * 2 + b, b)
                column(10, 0)

                def wait_chunk(g):
                    pe.wait_ge(bank_free, f0 + g + 1)

                out_stage(f"{which}_out", hT_hi, hT_lo, FF // P, wait_chunk, lambda: hidden_transposes(10, 0),
                          n + 1, 4)

            pe.wait_ge(ident_landed, 16)
            swiglu("f1", 0)

            g0, c0 = FIRST_GROUP["mix_in"], FIRST_ACC["mix_in"]

            def transposes(bank, source, n_free):
                pe.wait_ge(bank_free, n_free)
                for c in range(4):
                    i = m.transpose(aux[:, bank, c * P:(c + 1) * P], source[:, c * P:(c + 1) * P], ident[:])
                i.then_inc(bank_full, 1)

            def scores(s):
                t, h = s // NH, s % NH
                if s:
                    pe.wait_ge(s_reduced, s)
                else:
                    pe.wait_ge(bank_free, FIRST_FILL["nk"] + 2)
                m.matmul(aux[:, 1, 0:S], nqT[h % 2][:, h // 2, t * P:(t + 1) * P], nkT[:, h // 2, :],
                         start=True, stop=True).then_inc(s_full, 1)

            def prob_transposes(s):
                pe.wait_ge(p_ready, s + 1)
                if s:
                    pe.wait_ge(pT_copied, s)
                for k in range(T):
                    i = m.transpose(aux[:, 2, k * P:(k + 1) * P], prob[:, s % 2, k * P:(k + 1) * P], ident[:])
                i.then_inc(pT_full, 1)

            def attend(s):
                pe.wait_ge(pT_copied, s + 1)
                if s:
                    pe.wait_ge(o_taken, s)
                h = s % NH
                for k in range(T):
                    i = m.matmul(aux[:, 3, 0:ND], probT[:, s % 2, k, :], nv[:, k, h * ND:(h + 1) * ND],
                                 start=k == 0, stop=k == T - 1)
                i.then_inc(o_full, 1)

            def extras(slot):
                if slot == 3:
                    for t in range(T):
                        pe.wait_ge(acc_free_act[t], 1)
                        transposes(t, stage[:, t], FIRST_FILL["nq"])
                if slot == 4:
                    for t in range(T):
                        pe.wait_ge(acc_free_act[t], 2)
                        transposes(t, stage[:, t], FIRST_FILL["nk"])
                if 8 <= slot < 12:
                    t = slot % 2
                    n = slot - 8
                    pe.wait_ge(rot_done, n + 1)
                    transposes(0, stage[:, t], FIRST_FILL["rq"] + n)
                if 12 <= slot < 16:
                    h = slot - 12
                    pe.wait_ge(bank_free, FIRST_FILL["rs"] + h)
                    for k in range(T):
                        i = m.matmul(aux[:, 0, k * S:(k + 1) * S], rkT[:, h, k * P:(k + 1) * P], rqT[:, h, :],
                                     start=True, stop=True)
                    i.then_inc(bank_full, 1)
                if 18 <= slot < 22:
                    h = slot - 18
                    pe.wait_ge(bank_free, FIRST_FILL["rp"] + h)
                    if h == 0:
                        for t in range(T):
                            pe.wait_ge(acc_free_act[t], ACC_ORDER[:c0 + 7].count("A"))
                    for t in range(T):
                        for k in range(T):
                            i = m.matmul(aux[:, 0, t * RV:(t + 1) * RV], decay[:, h, k, t * P:(t + 1) * P],
                                         rv[:, k, h * RV:(h + 1) * RV], start=k == 0, stop=k == T - 1)
                    i.then_inc(bank_full, 1)
                s = slot - 6
                if 0 <= s < 16:
                    scores(s)
                if 0 <= s - 1 < 16:
                    prob_transposes(s - 1)
                if 0 <= s - 2 < 16:
                    attend(s - 2)
                if slot == 24:
                    pe.wait_ge(o_taken, 16)
                    for t in range(T):
                        transposes(1 + t, y_na[:, t], FIRST_FILL["yna"])
                if slot in (24, 25):
                    t = slot - 24
                    pe.wait_ge(y_ret_ready, t + 1)
                    for h in range(2):
                        transposes(0 if h == 0 else 3, y_ret[:, t, h * 512:(h + 1) * 512],
                                   FIRST_FILL["yret"] + 2 * t if t else FIRST_FILL["yna"])

            first_columns(1, "mix_in")
            extras(3)
            for c in range(2, 13):
                for t in range(T):
                    wait_acc_free(pe, t, c0 + c - 1)
                    column_tile(g0 + 2 * c, (g0 + 2 * c) % RING, c % 2, t)
                    extras(2 * c + t)

            for t in range(T):
                wait_acc_free(pe, t, FIRST_ACC["na_out"])
                if t == 0:
                    pe.wait_ge(bank_free, FIRST_FILL["yna"] + 2)
                for n in range(2):
                    out_tile("na_out", n, t, ynaT_hi, ynaT_lo, NH // 2, acc_target, lambda t: (acc_full[t], 1))

            def aux_target(t, half):
                return aux[:, 2 * t + half]

            def merged_transposes(t):
                for h in range(2):
                    pe.wait_ge(merged_ready, 2 * t + h + 1)
                    bank = 2 * t + h
                    for c in range(4):
                        i = m.transpose(aux[:, bank, c * P:(c + 1) * P],
                                        m_ret[:, t, (4 * h + c) * P:(4 * h + c + 1) * P], ident[:])
                    i.then_inc(bank_full, 1)

            pe.wait_ge(bank_free, FIRST_FILL["yret"] + 4)
            for t in range(T):
                for n in range(4):
                    out_tile("ret_out", n, t, yretT_hi, yretT_lo, KD, aux_target, lambda t: (ret_acc_full, 1))
                    if t == 1 and n == 1:
                        merged_transposes(0)
            for t in range(T):
                wait_acc_free(pe, t, FIRST_ACC["mix_out"])
                for n in range(4):
                    pe.wait_ge(bank_free, FIRST_FILL["merged"] + 2 * t + n // 2 + 1)
                    out_tile("mix_out", n, t, xT_hi, xT_lo, KD, acc_target, lambda t: (acc_full[t], 1),
                             (lambda: norm_transposes(2)(0)) if t == 1 and n == 3 else None)
                    if t == 0 and n == 1:
                        merged_transposes(1)

            swiglu("f2", 2)

            g0, c0, f0 = FIRST_GROUP["a_in"], FIRST_ACC["a_in"], FIRST_FILL["a_in"]

            def pair_transposes(c, banks):
                for k in range(2):
                    f = 2 * c + k
                    pe.wait_ge(bank_free, f0 + max(0, f - 1) if f < 8 else f0 + 6 if f < 10 else f0 + f - 3)
                    for j in range(2):
                        for t in range(T):
                            col = (2 * k + j) * P
                            i = m.transpose(aux[:, banks[k], j * S + t * P:j * S + (t + 1) * P],
                                            a_stage[:, t, col:col + P], ident[:])
                    i.then_inc(bank_full, 1)

            def lru_gates(ch):
                pe.wait_ge(bank_free, f0 + ch // 2 + 1)
                if ch >= 2:
                    pe.wait_ge(g_taken, ch - 1)
                if ch == 0:
                    pe.wait_ge(gate_w_in_s, 16)
                for k in range(2):
                    i = m.matmul(aux[:, 2 + ch % 2, k * S:(k + 1) * S], gate_w[:, ch, k], u[:, ch], start=True, stop=True)
                i.then_inc(g_full, 1)

            def staged_transposes(c):
                for t in range(T):
                    wait_acc_free(pe, t, c0 + c + 1)
                if c == 4:
                    pe.wait_ge(g_taken, CH)
                pair_transposes(c, (2, 3) if c == 4 else (0, 1))

            first_columns(3, "a_in")
            staged_transposes(0)
            for c in range(2, 6):
                for t in range(T):
                    wait_acc_free(pe, t, c0 + c - 1)

                    def before_half(half):
                        if (t, half) == {2: (1, 1), 5: (1, 1)}.get(c, (0, 1)):
                            staged_transposes(c - 1)
                        first = {(2, 1, 0): 0, (2, 1, 1): 2, (3, 1, 0): 4, (3, 1, 1): 6, (4, 0, 0): 8,
                                 (4, 0, 1): 10}.get((c, t, half))
                        if first is not None:
                            lru_gates(first)
                            lru_gates(first + 1)

                    column_tile(g0 + 2 * c, (g0 + 2 * c) % RING, c % 2, t, before_half)
            out_stage("a_out", yT_hi, yT_lo, CH, lambda n: pe.wait_ge(bank_free, f0 + 6 + n + 1),
                      lambda: staged_transposes(5), 4)

            g0, c0, f0 = FIRST_GROUP["b_in"], FIRST_ACC["b_in"], FIRST_FILL["b_in"]
            n_dve = ACC_ORDER[:c0].count("V")

            def b_transposes(j, par):
                for t in range(T):
                    pe.wait_ge(acc_free_dve[t], n_dve + 1 + j)
                if isinstance(j, int) and j < 2:
                    pe.wait_ge(bank_free, f0)
                else:
                    pe.wait_ge(b_y_ready, j - 1)
                for k in range(2):
                    for t in range(T):
                        i = m.transpose(aux[:, par, k * S + t * P:k * S + (t + 1) * P],
                                        b_prod[:, par, t, k * P:(k + 1) * P], ident[:])
                i.then_inc(bank_full, 1)

            def b_column(j, par):
                for t in range(T):
                    pe.wait_ge(acc_free_dve[t], n_dve - 1 + j)
                    column_tile(g0 + 2 * j, (g0 + 2 * par) % RING, par, t)
                    if t == 0:
                        b_transposes(j - 1, 1 - par)

            first_columns(4, "b_in")
            b_transposes(0, 0)
            with pe.Fori(1, 6) as i:
                for b in range(2):
                    b_column(i * 2 + b, b)
            out_stage("b_out", yT_hi, yT_lo, CH, lambda n: pe.wait_ge(bank_free, f0 + 2 * n + 2),
                      lambda: b_transposes(11, 1))


def _stream(inputs):
    def columns(w, order):
        w = w.reshape(KD, P, -1)[:, :, order]
        w = w.reshape(2, 4, P, order.shape[0], UNIT).transpose(3, 0, 2, 1, 4)
        return w.reshape(-1, P, GROUP)

    def rows(w):
        return w.reshape(-1, 2, P, DM).transpose(0, 2, 1, 3).reshape(-1, P, GROUP)

    def blocks(parts, width, at):
        each = at[1] // width
        return np.array([[p * at[1] + b * width + i for p in parts for i in range(width)] for b in range(each)])

    ff = blocks((0, 1), 256, (0, FF))
    mix_starts = {"rq": 0, "rk": 512, "rv": 1024, "rg": 2048, "nq": 3072, "nk": 3584, "nv": 4096,
                  "gr": 4608, "gn": 5632}
    mix = np.array([np.arange(mix_starts[n] + 512 * c, mix_starts[n] + 512 * (c + 1))
                    for n, c in (("nq", 0), ("nk", 0), ("nv", 0), ("rq", 0), ("rk", 0), ("rv", 0), ("rv", 1),
                                 ("rg", 0), ("rg", 1), ("gr", 0), ("gr", 1), ("gn", 0), ("gn", 1))])
    a_cols = np.array([np.arange(W2 + 512 * c, W2 + 512 * (c + 1)) for c in range(3)]
                      + [np.arange(512 * c, 512 * (c + 1)) for c in range(3)])
    b_cols = blocks((0, 1, 3, 2), P, (0, W2))
    a = {k: np.asarray(v) for k, v in inputs.items()}
    return np.concatenate([
        columns(a["ffn1_w_in"][0], ff), rows(a["ffn1_w_out"][0]), columns(a["w_mix_in"][0], mix),
        rows(a["w_na_out"][0]), rows(a["w_ret_out"][0]), rows(a["w_mix_out"][0]),
        columns(a["ffn2_w_in"][0], ff), rows(a["ffn2_w_out"][0]), columns(a["a_w_in_2"][0], a_cols),
        rows(a["a_w_out_2"][0]), columns(a["b_w_in_2"][0], b_cols), rows(a["b_w_out_2"][0])])


def _bias_windows(rel):
    rows = rel[:, REL_R // 2 - (GR - 1):REL_R // 2 + GR]
    padded = np.pad(rows, ((0, 0), (0, 0), (GW - 1 - REL_C // 2, GW - 1 - REL_C // 2)))
    return np.stack([padded[:, :, GW - 1 - c:2 * GW - 1 - c] for c in range(GW)])


def _by_chunk(v):
    v = np.asarray(v)
    return np.moveaxis(v.reshape(v.shape[:-1] + (CH, P)), (-1, -2), (0, 1))


def kernel(**inputs):
    import concourse.bacc as bacc
    from concourse.bass_utils import run_bass_kernel_spmd

    f = np.float32
    inv = (f(1.0) / (f(10000.0) ** np.linspace(0.0, 1.0, 64, dtype=f))).astype(f)
    angle = np.arange(S, dtype=f)[:, None] * inv[None, :]
    rot = np.stack([np.cos(angle), np.sin(angle), -np.sin(angle)], axis=1).astype(f)
    rot = rot.reshape(T, P, 3, 64).transpose(1, 0, 2, 3)
    col = np.arange(P) % GW
    start = np.clip(col - WIN // 2, 0, GW - WIN)[:, None]
    key = np.arange(GW)[None, :]
    colmask = np.where((key >= start) & (key < start + WIN), f(0), f(-BIG)).astype(f)
    diff = (np.arange(S)[None, :] - np.arange(S)[:, None]).astype(f)
    dist = np.stack([np.maximum(diff, 0), np.maximum(-diff, 0)]).reshape(2, T, P, S).transpose(2, 0, 1, 3)

    a = {k: np.asarray(v) for k, v in inputs.items()}
    arrays = {
        "weights": _stream(inputs),
        "x_in": a["x"][0],
        "gains": np.concatenate([a["ffn1_pre_norm"], a["ffn1_post_norm"], a["mix_pre_norm"], a["mix_post_norm"],
                                 a["ffn2_pre_norm"], a["ffn2_post_norm"], a["norm_g_2"], a["final_g_2"][None]]),
        "ident_in": np.eye(P, dtype=f),
        "rot_in": rot,
        "colmask_in": colmask,
        "dist_in": dist,
        "decay_in": np.concatenate([a["ret_decay_fwd"], a["ret_decay_bwd"]], axis=1),
        "lam_in": _by_chunk(a["a_lambda_2"][0]),
        "bias_in": _bias_windows(a["na_rel_bias"][0]),
        "gate_w_in": a["a_gate_w_2"][0].reshape(CH, P, 2, P).transpose(1, 0, 2, 3),
        "gate_b_in": a["a_gate_b_2"][0].reshape(CH, 2, P).transpose(2, 0, 1),
        "conv_a_in": _by_chunk(a["a_conv_w_2"][0]),
        "conv_ab_in": _by_chunk(a["a_conv_b_2"][0]),
        "conv_b_in": _by_chunk(a["b_conv_w_2"][0]),
    }
    nc = bacc.Bacc("TRN2", target_bir_lowering=False, num_devices=1)
    args = {}
    for name, value in arrays.items():
        arrays[name] = np.ascontiguousarray(value)
        args[name] = nc.dram_tensor(name, arrays[name].shape, F32, kind="ExternalInput").ap()
    args["out"] = nc.dram_tensor("out", (S, DM), F32, kind="ExternalOutput").ap()
    build(nc, **args)
    result = run_bass_kernel_spmd(nc, [arrays], core_ids=[0])
    return np.asarray(result.results[0]["out"]).reshape(1, S, DM)
```
